# Optimizing a Trainium2 kernel written in Bass

```python
import jax, jax.numpy as jnp
from jax import lax
import numpy as np

D_MODEL = 1024
BATCH = 1
SEQ = 512
DEPTH = 2

GRID_W = 64
CTX_LEN = 256
N_MIXERS = 3
RETENTION, FOURIER, NEIGHBOURHOOD = 0, 1, 2
N_MOD = 6
EPS = 1e-6
NEG_INF = -1e30

RET_HEADS = 4
RET_DK = D_MODEL // RET_HEADS
RET_DV = 2 * RET_DK
RET_CHUNK = 128
RET_BASE_SHIFT = 5
ROPE_BASE = 10000.0

FN_GROUPS = 4

NA_HEADS = 16
NA_HD = D_MODEL // NA_HEADS
NA_KH = 8
NA_KW = 16

N_EXPERTS = 16
N_GROUPS = 4
EXPERTS_PER_GROUP = N_EXPERTS // N_GROUPS
TOP_K = 2
D_EXPERT = D_MODEL
MOE_BLOCK = 128

kernel_name = 'hybrid_retention_fnet_natten_moe_dit'

def _rmsnorm(x, g):
    xf = x.astype(jnp.float32)
    y = xf * lax.rsqrt(jnp.mean(xf * xf, axis=-1, keepdims=True) + EPS)
    return (y * g.astype(jnp.float32)).astype(x.dtype)

def _modulate(h, shift, scale):
    return h * (1.0 + scale) + shift

def _axial_rope(x):
    L, dh = x.shape[1], x.shape[-1]
    half = dh // 2
    nf = half // 2
    t = jnp.arange(L)
    row = (t // GRID_W).astype(jnp.float32)
    col = (t % GRID_W).astype(jnp.float32)
    inv = ROPE_BASE ** (-jnp.arange(nf, dtype=jnp.float32) / nf)

    def rot(seg, pos):
        ang = pos[:, None] * inv[None, :]
        cos = jnp.cos(ang)[None, :, None, :]
        sin = jnp.sin(ang)[None, :, None, :]
        a, b = seg[..., :nf], seg[..., nf:]
        return jnp.concatenate([a * cos - b * sin, a * sin + b * cos], axis=-1)

    xf = x.astype(jnp.float32)
    return jnp.concatenate([rot(xf[..., :half], row), rot(xf[..., half:], col)], axis=-1).astype(x.dtype)

def _to_bhld(a):
    return jnp.transpose(a, (0, 2, 1, 3)).astype(jnp.float32)

def _retention_scan(q, k, v, log_g, s0):
    B, H, L, _ = q.shape
    dv = v.shape[-1]
    C = RET_CHUNK
    n = L // C
    pos = jnp.arange(C, dtype=jnp.float32)
    diff = pos[:, None] - pos[None, :]
    dmat = jnp.where(diff >= 0, jnp.exp(jnp.maximum(diff, 0.0)[None] * log_g[:, None, None]), 0.0)
    q_dec = jnp.exp((pos + 1.0)[None, :] * log_g[:, None])
    k_dec = jnp.exp((C - 1.0 - pos)[None, :] * log_g[:, None])
    c_dec = jnp.exp(C * log_g)

    def chunks(a):
        return jnp.moveaxis(a.reshape(B, H, n, C, a.shape[-1]), 2, 0)

    def step(s, inp):
        qi, ki, vi = inp
        att = jnp.einsum('bhik,bhjk->bhij', qi, ki) * dmat
        o = (jnp.einsum('bhij,bhjv->bhiv', att, vi)
             + jnp.einsum('bhik,bhkv->bhiv', qi * q_dec[None, :, :, None], s))
        s = s * c_dec[None, :, None, None] + jnp.einsum('bhjk,bhjv->bhkv', ki * k_dec[None, :, :, None], vi)
        return s, o

    s_fin, o = lax.scan(step, s0, (chunks(q), chunks(k), chunks(v)))
    return jnp.moveaxis(o, 0, 2).reshape(B, H, L, dv), s_fin

def _retention_bidir(q, k, v, log_g, s0_f, s0_b):
    o_f, s_f = _retention_scan(q, k, v, log_g[0], s0_f)
    o_b, s_b = _retention_scan(q[:, :, ::-1], k[:, :, ::-1], v[:, :, ::-1], log_g[1], s0_b)
    return o_f + o_b[:, :, ::-1], s_f, s_b

def _retention_final_states(k, v, log_g):
    L = k.shape[2]
    t = jnp.arange(L, dtype=jnp.float32)
    w_f = jnp.exp((L - 1.0 - t)[None, :] * log_g[0][:, None])
    w_b = jnp.exp(t[None, :] * log_g[1][:, None])
    s_f = jnp.einsum('bhtk,ht,bhtv->bhkv', k, w_f, v)
    s_b = jnp.einsum('bhtk,ht,bhtv->bhkv', k, w_b, v)
    return s_f, s_b

def _retention_out(o, g, gn_w, w_out):
    B, H, L, dv = o.shape
    o = jnp.transpose(o, (0, 2, 1, 3))
    mu = jnp.mean(o, axis=-1, keepdims=True)
    var = jnp.mean(jnp.square(o - mu), axis=-1, keepdims=True)
    o = ((o - mu) * lax.rsqrt(var + EPS)).reshape(B, L, H * dv) * gn_w.astype(jnp.float32)
    return (o.astype(g.dtype) * jax.nn.silu(g)) @ w_out

def _retention_mixer(hx, hc, w_in, decay_logit, gn_w, w_out, need_ctx):
    D = D_MODEL
    B, T, _ = hx.shape
    Lc = hc.shape[1]
    log_g = jax.nn.log_sigmoid(decay_logit.astype(jnp.float32))
    k_scale = RET_DK ** -0.5
    qx, kx, vx, gx = jnp.split(hx @ w_in, [D, 2 * D, 4 * D], axis=-1)
    qx = _to_bhld(_axial_rope(qx.reshape(B, T, RET_HEADS, RET_DK)))
    kx = _to_bhld(_axial_rope(kx.reshape(B, T, RET_HEADS, RET_DK))) * k_scale
    vx = _to_bhld(vx.reshape(B, T, RET_HEADS, RET_DV))
    if need_ctx:
        qc, kc, vc, gc = jnp.split(hc @ w_in, [D, 2 * D, 4 * D], axis=-1)
        qc = _to_bhld(qc.reshape(B, Lc, RET_HEADS, RET_DK))
        kc = _to_bhld(kc.reshape(B, Lc, RET_HEADS, RET_DK)) * k_scale
        vc = _to_bhld(vc.reshape(B, Lc, RET_HEADS, RET_DV))
        zeros = jnp.zeros((B, RET_HEADS, RET_DK, RET_DV), jnp.float32)
        oc, s_f, s_b = _retention_bidir(qc, kc, vc, log_g, zeros, zeros)
        yc = _retention_out(oc, gc, gn_w, w_out)
    else:
        kc, vc = jnp.split(hc @ w_in[:, D:4 * D], [D], axis=-1)
        kc = _to_bhld(kc.reshape(B, Lc, RET_HEADS, RET_DK)) * k_scale
        vc = _to_bhld(vc.reshape(B, Lc, RET_HEADS, RET_DV))
        s_f, s_b = _retention_final_states(kc, vc, log_g)
        yc = None
    ox, _, _ = _retention_bidir(qx, kx, vx, log_g, s_f, s_b)
    return _retention_out(ox, gx, gn_w, w_out), yc

def _fourier_mix(h, w_out):
    B, L, D = h.shape
    hg = h.astype(jnp.float32).reshape(B, L, FN_GROUPS, D // FN_GROUPS)
    f = jnp.fft.fft2(hg, axes=(1, 3), norm='ortho').real
    return f.reshape(B, L, D).astype(h.dtype) @ w_out

def _na_mixer(hx, hc, w_qkv, rpb, w_out, need_ctx):
    B, T, D = hx.shape
    Lc = hc.shape[1]
    rows = T // GRID_W
    KH = min(NA_KH, rows)
    KW = NA_KW
    QB = KW
    NCB = GRID_W // QB
    BW = 2 * KW
    NK = KH * BW
    scale = NA_HD ** -0.5

    def heads(a):
        return a.reshape(a.shape[0], a.shape[1], NA_HEADS, NA_HD)

    qx, kx, vx = [heads(a) for a in jnp.split(hx @ w_qkv, 3, axis=-1)]
    if need_ctx:
        qc, kc, vc = [heads(a) for a in jnp.split(hc @ w_qkv, 3, axis=-1)]
    else:
        kc, vc = [heads(a) for a in jnp.split(hc @ w_qkv[:, D:], 2, axis=-1)]

    cb = np.clip(np.arange(NCB) * QB - KW // 2, 0, GRID_W - BW)
    qcol = np.arange(NCB)[:, None] * QB + np.arange(QB)[None, :]
    cstart = np.clip(qcol - KW // 2, 0, GRID_W - KW)
    kcol = np.tile(cb[:, None] + np.arange(BW)[None, :], (1, KH))
    krow = np.repeat(np.arange(KH), BW)
    valid = (kcol[:, None, :] >= cstart[:, :, None]) & (kcol[:, None, :] < cstart[:, :, None] + KW)
    dc_idx = np.clip(kcol[:, None, :] - qcol[:, :, None], -(KW - 1), KW - 1) + (KW - 1)

    def row_block(r):
        rs = jnp.clip(r - KH // 2, 0, rows - KH)
        idx = ((rs + krow)[None, :] * GRID_W + kcol).reshape(-1)
        kb = jnp.take(kx, idx, axis=1).reshape(B, NCB, NK, NA_HEADS, NA_HD)
        vb = jnp.take(vx, idx, axis=1).reshape(B, NCB, NK, NA_HEADS, NA_HD)
        qb = lax.dynamic_slice_in_dim(qx, r * GRID_W, GRID_W, axis=1).reshape(B, NCB, QB, NA_HEADS, NA_HD)
        dr_idx = rs + krow - r + (NA_KH - 1)
        bias = rpb[:, dr_idx[None, None, :], dc_idx].astype(jnp.float32)
        s_win = jnp.einsum('bjqhd,bjkhd->bhjqk', qb, kb).astype(jnp.float32) * scale + bias
        s_win = jnp.where(valid, s_win, NEG_INF)
        s_ctx = jnp.einsum('bjqhd,bchd->bhjqc', qb, kc).astype(jnp.float32) * scale
        p = jax.nn.softmax(jnp.concatenate([s_win, s_ctx], axis=-1), axis=-1).astype(vx.dtype)
        o = (jnp.einsum('bhjqk,bjkhd->bjqhd', p[..., :NK], vb)
             + jnp.einsum('bhjqc,bchd->bjqhd', p[..., NK:], vc))
        return o.reshape(B, GRID_W, D)

    o = lax.map(row_block, jnp.arange(rows))
    yx = jnp.moveaxis(o, 0, 1).reshape(B, T, D) @ w_out
    if need_ctx:
        s = jnp.einsum('bqhd,bkhd->bhqk', qc, kc).astype(jnp.float32) * scale
        p = jax.nn.softmax(s, axis=-1).astype(vc.dtype)
        yc = jnp.einsum('bhqk,bkhd->bqhd', p, vc).reshape(B, Lc, D) @ w_out
    else:
        yc = None
    return yx, yc

def _moe(tokens, router_w, router_bias, w_gate, w_up, w_down):
    N, D = tokens.shape
    rows = jnp.arange(N)
    scores = jax.nn.sigmoid((tokens @ router_w).astype(jnp.float32))
    sel = scores + router_bias.astype(jnp.float32)
    grp = sel.reshape(N, N_GROUPS, EXPERTS_PER_GROUP)
    grp_score = jnp.sum(lax.top_k(grp, 2)[0], axis=-1)
    g_idx = jnp.argmax(grp_score, axis=-1)
    _, local = lax.top_k(grp[rows, g_idx], TOP_K)
    experts = g_idx[:, None] * EXPERTS_PER_GROUP + local
    w = scores[rows[:, None], experts]
    w = w / jnp.sum(w, axis=-1, keepdims=True)

    S = N * TOP_K
    flat_e = experts.reshape(-1)
    flat_tok = jnp.repeat(rows, TOP_K)
    flat_w = w.reshape(-1)
    order = jnp.argsort(flat_e, stable=True)
    se, stok, sw = flat_e[order], flat_tok[order], flat_w[order]
    counts = jnp.bincount(flat_e, length=N_EXPERTS)
    starts = jnp.cumsum(counts) - counts
    padded = (counts + MOE_BLOCK - 1) // MOE_BLOCK * MOE_BLOCK
    pend = jnp.cumsum(padded)
    pstart = pend - padded
    dest = pstart[se] + jnp.arange(S) - starts[se]
    n_blocks = (S + N_EXPERTS * (MOE_BLOCK - 1) + MOE_BLOCK - 1) // MOE_BLOCK
    P = n_blocks * MOE_BLOCK
    row_tok = jnp.full((P,), N, jnp.int32).at[dest].set(stok.astype(jnp.int32))
    row_w = jnp.zeros((P,), jnp.float32).at[dest].set(sw)
    block_e = jnp.minimum(jnp.searchsorted(pend, jnp.arange(n_blocks) * MOE_BLOCK, side='right'), N_EXPERTS - 1)
    xpad = jnp.concatenate([tokens, jnp.zeros((1, D), tokens.dtype)], axis=0)
    xb = xpad[row_tok].reshape(n_blocks, MOE_BLOCK, D)

    def expert_block(args):
        xblk, e = args
        h = jax.nn.silu(xblk @ w_gate[e]) * (xblk @ w_up[e])
        return h @ w_down[e]

    yb = lax.map(expert_block, (xb, block_e)).reshape(P, D)
    y = yb * row_w[:, None].astype(yb.dtype)
    return jax.ops.segment_sum(y, row_tok, num_segments=N + 1)[:N]

def setup_inputs(seed: int = 0) -> dict:
    key = jax.random.key(seed)
    ks = jax.random.split(key, 22)
    f32 = jnp.float32
    D = D_MODEL
    n_ret = len(range(RETENTION, DEPTH, N_MIXERS))
    n_fn = len(range(FOURIER, DEPTH, N_MIXERS))
    n_na = len(range(NEIGHBOURHOOD, DEPTH, N_MIXERS))

    def nrm(k, shape, s):
        return jax.random.normal(k, shape, f32) * s

    base_logit = jnp.log(2.0 ** (RET_BASE_SHIFT + jnp.arange(RET_HEADS, dtype=f32)) - 1.0)
    return {
        'x': nrm(ks[0], (BATCH, SEQ, D), 1.0),
        'c': nrm(ks[1], (BATCH, D), 1.0),
        'ctx': nrm(ks[2], (BATCH, CTX_LEN, D), 1.0),
        'c_ctx': nrm(ks[3], (D,), 1.0),
        'w_mod': nrm(ks[4], (DEPTH, D, N_MOD * D), 0.5 * D ** -0.5),
        'b_mod': nrm(ks[5], (DEPTH, N_MOD * D), 0.02),
        'norm_mix': 1.0 + nrm(ks[6], (DEPTH, D), 0.02),
        'norm_ffn': 1.0 + nrm(ks[7], (DEPTH, D), 0.02),
        'norm_final': 1.0 + nrm(ks[8], (D,), 0.02),
        'ret_w_in': nrm(ks[9], (n_ret, D, 6 * D), D ** -0.5),
        'ret_decay': base_logit + nrm(ks[10], (n_ret, 2, RET_HEADS), 0.1),
        'ret_gn': 1.0 + nrm(ks[11], (n_ret, RET_HEADS * RET_DV), 0.02),
        'ret_w_out': nrm(ks[12], (n_ret, RET_HEADS * RET_DV, D), (RET_HEADS * RET_DV) ** -0.5),
        'fn_w_out': nrm(ks[13], (n_fn, D, D), D ** -0.5),
        'na_w_qkv': nrm(ks[14], (n_na, D, 3 * D), D ** -0.5),
        'na_rpb': nrm(ks[15], (n_na, NA_HEADS, 2 * NA_KH - 1, 2 * NA_KW - 1), 0.1),
        'na_w_out': nrm(ks[16], (n_na, D, D), D ** -0.5),
        'router_w': nrm(ks[17], (D, N_EXPERTS), D ** -0.5),
        'router_bias': nrm(ks[18], (N_EXPERTS,), 0.01),
        'moe_w_gate': nrm(ks[19], (DEPTH, N_EXPERTS, D, D_EXPERT), D ** -0.5),
        'moe_w_up': nrm(ks[20], (DEPTH, N_EXPERTS, D, D_EXPERT), D ** -0.5),
        'moe_w_down': nrm(ks[21], (DEPTH, N_EXPERTS, D_EXPERT, D), D_EXPERT ** -0.5),
    }

def reference(x, c, ctx, c_ctx, w_mod, b_mod, norm_mix, norm_ffn, norm_final,
              ret_w_in, ret_decay, ret_gn, ret_w_out, fn_w_out,
              na_w_qkv, na_rpb, na_w_out,
              router_w, router_bias, moe_w_gate, moe_w_up, moe_w_down):
    B, T, D = x.shape
    Lc = ctx.shape[1]
    c_act = jax.nn.silu(c)
    cc_act = jax.nn.silu(c_ctx)
    for i in range(DEPTH):
        kind, j = i % N_MIXERS, i // N_MIXERS
        need_ctx = i < DEPTH - 1
        mx = jnp.split(c_act @ w_mod[i] + b_mod[i], N_MOD, axis=-1)
        mc = jnp.split(cc_act @ w_mod[i] + b_mod[i], N_MOD, axis=-1)
        hx = _modulate(_rmsnorm(x, norm_mix[i]), mx[0][:, None], mx[1][:, None])
        if kind == FOURIER:
            yx = _fourier_mix(hx, fn_w_out[j])
            if need_ctx:
                hc = _modulate(_rmsnorm(ctx, norm_mix[i]), mc[0], mc[1])
                yc = _fourier_mix(hc, fn_w_out[j])
        else:
            hc = _modulate(_rmsnorm(ctx, norm_mix[i]), mc[0], mc[1])
            if kind == RETENTION:
                yx, yc = _retention_mixer(hx, hc, ret_w_in[j], ret_decay[j], ret_gn[j], ret_w_out[j], need_ctx)
            else:
                yx, yc = _na_mixer(hx, hc, na_w_qkv[j], na_rpb[j], na_w_out[j], need_ctx)
        x = x + mx[2][:, None] * yx
        fx = _modulate(_rmsnorm(x, norm_ffn[i]), mx[3][:, None], mx[4][:, None]).reshape(B * T, D)
        if need_ctx:
            ctx = ctx + mc[2] * yc
            fc = _modulate(_rmsnorm(ctx, norm_ffn[i]), mc[3], mc[4]).reshape(B * Lc, D)
            f = _moe(jnp.concatenate([fx, fc], axis=0), router_w, router_bias,
                     moe_w_gate[i], moe_w_up[i], moe_w_down[i])
            x = x + mx[5][:, None] * f[:B * T].reshape(B, T, D)
            ctx = ctx + mc[5] * f[B * T:].reshape(B, Lc, D)
        else:
            f = _moe(fx, router_w, router_bias, moe_w_gate[i], moe_w_up[i], moe_w_down[i])
            x = x + mx[5][:, None] * f.reshape(B, T, D)
    return _rmsnorm(x, norm_final)


_drawn_inputs = setup_inputs


def setup_inputs(seed=0):
    import zlib

    import numpy as np

    out = dict(_drawn_inputs(seed))
    spreads = {}
    factors = {'norm_final': 27.858, 'ret_gn': 8.29, 'norm_ffn': 2.903}
    for name, (base, spread) in spreads.items():
        noise = np.random.default_rng([zlib.crc32(name.encode()), seed]).standard_normal(out[name].shape)
        drawn = base * np.exp(spread * noise) if base else spread * noise
        out[name] = __import__('jax').numpy.asarray(drawn.astype(out[name].dtype))
    for name, factor in factors.items():
        out[name] = (out[name] * factor).astype(out[name].dtype)
    return out
```

```python
import concourse.bass as bass
from concourse import mybir
from contextlib import ExitStack

F32, F32R = mybir.dt.float32, mybir.dt.float32r
I32, U32 = mybir.dt.int32, mybir.dt.uint32
ALU = mybir.AluOpType
ACT = mybir.ActivationFunctionType
AX = mybir.AxisListType

P = 128
D = 1024
KT = D // P
SEQ, CTX = 512, 256
NX, NC = SEQ // P, CTX // P
NTOK = NX + NC
NMOD = 6
EPS = 1e-6
HEADS, DK, DV = 4, 256, 512
NE, NG, EPG = 16, 4, 4
MAX_OVER = (2 * SEQ) // (P + 1)
NBLK = NE + MAX_OVER
XR = SEQ + 3 * P
XO = SEQ - P
CR = SEQ + P
STRIPS = XR + CR
H = 512
FG = 256
BIG = 1e30


class Count:

    def __init__(self, sem, base=0):
        self.sem, self.n, self.base = sem, 0, base

    def inc(self, ins):
        ins.then_inc(self.sem, 1)
        self.n += 1
        return self.n

    def after(self, eng):
        eng.wait_ge(self.sem, self.base + self.n)


def alloc(nc, ctx, tag):
    def sb(name, shape, dt=F32):
        return ctx.enter_context(nc.sbuf_tensor(f"{tag}_{name}", shape, dt))

    sems = []

    def clear():
        nc.clear_and_free_semaphores(sems)
        nc.all_engine_barrier()

    ctx.callback(clear)

    def sem(name):
        sems.append(nc.alloc_semaphore(f"{tag}_{name}"))
        return sems[-1]

    def banks(name, n):
        return [ctx.enter_context(nc.psum_tensor(f"{tag}_{name}{i}", [P, H], F32)) for i in range(n)]

    return sb, sem, banks


def f(ap):
    return ap.bitcast(F32)


def phase_modulation(nc, a, scr, ident, minus_half):
    RING, SL = 8, 4
    NCH = 2 * SL
    STEPS = NMOD * D // (SL * H)
    with ExitStack() as ctx:
        sb, sem, banks = alloc(nc, ctx, "modulation")
        crow = sb("crow", [2 * KT, P])
        csilu = sb("csilu", [2 * KT, P])
        cT = sb("cT", [P, 2 * KT])
        wm = sb("wm", [P, RING, 4, H])
        brow = sb("brow", [2, 2, NMOD * D])
        dist = sb("dist", [P, 2 * XR + 2 * CR])
        zero = sb("zero", [P, D])
        dl = sb("dl", [P, 2 * HEADS])
        t = sb("t", [P, 8, 2 * HEADS])
        ex = sb("ex", [P, 2, 2 * XR + 2 * CR])
        strip = sb("strip", [P, 2, STRIPS])
        pm = banks("pm", 2)
        pT = banks("pT", 1)[0]
        s_c, s_id, s_b, s_dist, s_dl = (sem(n) for n in ("c_in", "id_in", "b_in", "dist_in", "dl_in"))
        w_in = [sem(f"w_in{i}") for i in range(RING)]
        s_silu, s_cT, s_cTs = sem("c_silu"), sem("c_transposed"), sem("cT_ready")
        chunk_used, row_ready = sem("chunk_used"), sem("row_ready")
        mod_out = sem("mod_out")
        dv, lg, e_ready, strip_ready = sem("dve_steps"), sem("log_decay"), sem("exps_ready"), sem("strip_ready")
        s_exp, zeroed, zero_out = sem("exp_abs"), sem("zeroed"), sem("zero_out")
        strip_out = [sem("strip_out0"), sem("strip_out1")]
        w_view = a["w_mod"].rearrange("l (a k p) n -> l a p k n", p=P, k=4)
        ys_rows = scr["ys"].rearrange("(b p) d -> b p d", p=P)
        xs_rows = scr["xs"].rearrange("(b p) d -> b p d", p=P)
        with nc.Block() as block:

            @block.sync
            def _(sp):
                sp.dma_start(crow[0:KT, :], a["c"].rearrange("o (k p) -> (o k) p", p=P)).then_inc(s_c, 16)
                sp.dma_start(crow[KT:2 * KT, :], a["c_ctx"].rearrange("(k p) -> k p", p=P)).then_inc(s_c, 16)
                sp.dma_start(ident[:], a["identity"]).then_inc(s_id, 16)
                for lay in range(2):
                    for st in range(2):
                        sp.dma_start(brow[st:st + 1, lay, :], a["b_mod"][lay:lay + 1, :]).then_inc(s_b, 16)
                for lay in range(2):
                    with sp.Fori(0, STEPS) as it:
                        g = it + lay * STEPS
                        for c in range(NCH):
                            sp.wait_ge(chunk_used, g * NCH + c + 1)
                            sp.dma_start(wm[:, c],
                                         w_view[lay, c % 2, :, :, bass.ds(it * (SL * H) + (c // 2) * H, H)]
                                         ).then_inc(w_in[c], 16)

            @block.tensor
            def _(pe):
                pe.nop().then_inc(chunk_used, RING)
                pe.wait_ge(s_id, 16)
                pe.wait_ge(s_silu, 1)
                pe.transpose(pT[:, 0:2 * KT], csilu[:], ident[0:2 * KT, 0:2 * KT]).then_inc(s_cT, 1)
                pe.wait_ge(s_cTs, 1)
                for lay in range(2):
                    with pe.Fori(0, STEPS) as it:
                        g = it + lay * STEPS
                        for c in range(NCH):
                            sl = c // 2
                            if c % 2 == 0:
                                pe.wait_ge(row_ready, g * SL + sl + 1)
                            pe.wait_ge(w_in[c], g * 16 + 16)
                            for k in range(4):
                                kk = (c % 2) * 4 + k
                                mm = pe.matmul(pm[sl % 2][0:2, :], cT[:, kk:kk + KT + 1:KT], wm[:, c, k, :],
                                               start=kk == 0, stop=kk == KT - 1)
                            mm.then_inc(chunk_used, 1)

            @block.scalar
            def _(act):
                act.wait_ge(s_c, 32)
                act.activation(csilu[:], crow[:], ACT.Silu).then_inc(s_silu, 1)
                act.wait_ge(s_cT, 1)
                act.activation(cT[:], pT[:, 0:2 * KT], ACT.Copy).then_inc(s_cTs, 1)
                act.wait_ge(dv, 2)
                act.activation(t[:, 1, :], t[:, 0, :], ACT.Exp, scale=-1.0).then_inc(s_exp, 1)
                act.wait_ge(lg, 1)
                act.wait_ge(s_dist, 16)
                for h in range(HEADS):
                    if h >= 2:
                        act.wait_ge(strip_ready, h - 1)
                    fwd, bwd = t[:, 7, h:h + 1], t[:, 7, HEADS + h:HEADS + h + 1]
                    o = ex[:, h % 2, :]
                    act.activation(o[:, 0:XR], dist[:, 0:XR], ACT.Exp, scale=fwd)
                    act.activation(o[:, XR:2 * XR], dist[:, XR:2 * XR], ACT.Exp, scale=bwd)
                    act.activation(o[:, 2 * XR:2 * XR + CR], dist[:, 2 * XR:2 * XR + CR], ACT.Exp, scale=fwd)
                    act.activation(o[:, 2 * XR + CR:], dist[:, 2 * XR + CR:], ACT.Exp, scale=bwd).then_inc(e_ready, 1)
                for lay in range(2):
                    act.wait_ge(row_ready, 2 + (lay + 1) * STEPS * SL)
                    act.dma_start(scr["mod"][lay], brow[:, lay, :]).then_inc(mod_out, 16)
                act.wait_ge(mod_out, 32)

            @block.gpsimd
            def _(pool):
                pool.dma_start(dist[:], a["distances"]).then_inc(s_dist, 16)
                pool.dma_start(dl[:], a["ret_decay"].rearrange("o a h -> o (a h)").to_broadcast([P, 2 * HEADS])
                               ).then_inc(s_dl, 16)
                pool.memset(minus_half[:], -0.5)
                pool.memset(zero[:], 0.0).then_inc(zeroed, 1)
                pool.wait_ge(zeroed, 1)
                for b in range(NBLK + 1):
                    pool.dma_start(xs_rows[b], zero[:]).then_inc(zero_out, 16)
                for b in range(NE + 1, NBLK + 1):
                    pool.dma_start(ys_rows[b], zero[:]).then_inc(zero_out, 16)
                for h in range(HEADS):
                    pool.wait_ge(strip_ready, h + 1)
                    pool.dma_start(scr["strips"][h], strip[:, h % 2, :]).then_inc(strip_out[h % 2], 16)
                pool.wait_ge(zero_out, 16 * (NBLK + 1 + MAX_OVER))
                for s in strip_out:
                    pool.wait_ge(s, 16 * HEADS // 2)

            @block.vector
            def _(dve):
                own = Count(dv)

                def step(ins):
                    own.inc(ins)
                    own.after(dve)

                dve.wait_ge(s_dl, 16)
                step(dve.tensor_scalar(t[:, 2, :], dl[:], -1.0, None, ALU.mult))
                step(dve.tensor_tensor(t[:, 0, :], dl[:], t[:, 2, :], ALU.max))
                dve.wait_ge(s_exp, 1)
                step(dve.tensor_scalar(t[:, 2, :], t[:, 1, :], 2.0, None, ALU.add))
                step(dve.reciprocal(t[:, 3, :], t[:, 2, :]))
                step(dve.tensor_tensor(t[:, 3, :], t[:, 1, :], t[:, 3, :], ALU.mult))
                step(dve.tensor_tensor(t[:, 4, :], t[:, 3, :], t[:, 3, :], ALU.mult))
                step(dve.memset(t[:, 5, :], 2.0 / 17))
                for n in (15, 13, 11, 9, 7, 5, 3, 1):
                    step(dve.tensor_tensor(t[:, 6, :], t[:, 5, :], t[:, 4, :], ALU.mult))
                    step(dve.tensor_scalar(t[:, 5, :], t[:, 6, :], 2.0 / n, None, ALU.add))
                step(dve.tensor_tensor(t[:, 6, :], t[:, 5, :], t[:, 3, :], ALU.mult))
                step(dve.tensor_scalar(t[:, 2, :], dl[:], 0.0, None, ALU.min))
                dve.tensor_tensor(t[:, 7, :], t[:, 2, :], t[:, 6, :], ALU.subtract).then_inc(lg, 1)
                for h in range(HEADS):
                    dve.wait_ge(e_ready, h + 1)
                    if h >= 2:
                        dve.wait_ge(strip_out[h % 2], 16 * (h // 2))
                    o = ex[:, h % 2, :]
                    step(dve.scalar_tensor_tensor(o[:, 0:XR], dist[:, XR:2 * XR], 0.0, o[:, 0:XR],
                                                  ALU.is_le, ALU.mult))
                    step(dve.scalar_tensor_tensor(o[:, XR:2 * XR], dist[:, 0:XR], 0.0, o[:, XR:2 * XR],
                                                  ALU.is_le, ALU.mult))
                    step(dve.tensor_tensor(strip[:, h % 2, 0:XR], o[:, 0:XR], o[:, XR:2 * XR], ALU.add))
                    dve.tensor_tensor(strip[:, h % 2, XR:], o[:, 2 * XR:2 * XR + CR], o[:, 2 * XR + CR:],
                                      ALU.add).then_inc(strip_ready, 1)
                dve.wait_ge(s_b, 64)
                dve.nop().then_inc(row_ready, 2)
                for lay in range(2):
                    with dve.Fori(0, STEPS) as it:
                        g = it + lay * STEPS
                        for sl in range(SL):
                            dve.wait_ge(chunk_used, RING + (g * SL + sl + 1) * 2)
                            dve.tensor_tensor(brow[:, lay, bass.ds(it * (SL * H) + sl * H, H)], pm[sl % 2][0:2, :],
                                              brow[:, lay, bass.ds(it * (SL * H) + sl * H, H)],
                                              ALU.add).then_inc(row_ready, 1)


def phase_norm_transposed(nc, a, scr, ident, minus_half, hTh, hTl):
    with ExitStack() as ctx:
        sb, sem, banks = alloc(nc, ctx, "norm_transposed")
        xt = sb("xt", [P, NTOK, D])
        md = sb("md", [P, 4, D])
        nm = sb("nm", [P, D])
        junk = sb("junk", [P, D])
        ss, rs = sb("ss", [P, NTOK]), sb("rs", [P, NTOK])
        pT = banks("pT", 4)
        x_in = [sem(f"x_in{t}") for t in range(NTOK)]
        md_in, sq, ms, rs_ready = sem("md_in"), sem("squares"), sem("mean_square"), sem("rs_ready")
        dv, h_ready, tr, hi, lo = sem("dve_steps"), sem("h_ready"), sem("transposed"), sem("hi_ready"), sem("lo_ready")
        with nc.Block() as block:

            @block.sync
            def _(sp):
                for t in range(NTOK):
                    src = a["x"][0, t * P:(t + 1) * P, :] if t < NX else a["ctx"][0, (t - NX) * P:(t - NX + 1) * P, :]
                    sp.dma_start(xt[:, t, :], src).then_inc(x_in[t], 16)
                for s in range(2):
                    for v in range(2):
                        sp.dma_start(md[:, 2 * s + v, :],
                                     scr["mod"][0, s:s + 1, v * D:(v + 1) * D].to_broadcast([P, D])).then_inc(md_in, 16)
                sp.dma_start(nm[:], a["norm_mix"][0:1, :].to_broadcast([P, D])).then_inc(md_in, 16)

            @block.scalar
            def _(act):
                for t in range(NTOK):
                    act.wait_ge(x_in[t], 16)
                    if t:
                        act.wait_ge(sq, t)
                    act.activation(junk[:], xt[:, t, :], ACT.Square, accum_out=ss[:, t:t + 1]).then_inc(sq, 1)
                for t in range(NTOK):
                    for half in range(2):
                        n = 2 * t + half
                        act.wait_ge(tr, n + 1)
                        act.activation(hTh[:, 4 * half:4 * half + 4, t * P:(t + 1) * P],
                                       pT[n % 4][:, :].rearrange("p (k c) -> p k c", k=4), ACT.Copy).then_inc(hi, 1)

            @block.gpsimd
            def _(pool):
                pool.wait_ge(ms, 1)
                pool.tensor_tensor(rs[:], ss[:], minus_half[:, 0:NTOK], ALU.pow).then_inc(rs_ready, 1)

            @block.tensor
            def _(pe):
                for t in range(NTOK):
                    pe.wait_ge(h_ready, t + 1)
                    for half in range(2):
                        n = 2 * t + half
                        if n >= 4:
                            pe.wait_ge(lo, n - 3)
                        for k in range(4):
                            ins = pe.transpose(pT[n % 4][:, k * P:(k + 1) * P],
                                               xt[:, t, (4 * half + k) * P:(4 * half + k + 1) * P], ident[:])
                        ins.then_inc(tr, 1)

            @block.vector
            def _(dve):
                own = Count(dv)
                dve.wait_ge(sq, NTOK)
                dve.tensor_scalar(ss[:], ss[:], 1.0 / D, EPS, ALU.mult, ALU.add).then_inc(ms, 1)
                dve.wait_ge(md_in, 16 * 5)
                for s in range(2):
                    own.inc(dve.scalar_tensor_tensor(md[:, 2 * s + 1, :], md[:, 2 * s + 1, :], 1.0, nm[:],
                                                     ALU.add, ALU.mult))
                own.after(dve)
                dve.wait_ge(rs_ready, 1)

                def modulate(t):
                    s = t // NX
                    own.inc(dve.scalar_tensor_tensor(xt[:, t, :], xt[:, t, :], rs[:, t:t + 1], md[:, 2 * s + 1, :],
                                                     ALU.mult, ALU.mult))
                    own.after(dve)
                    dve.tensor_tensor(xt[:, t, :], xt[:, t, :], md[:, 2 * s, :], ALU.add).then_inc(h_ready, 1)

                modulate(0)
                for t in range(NTOK):
                    if t + 1 < NTOK:
                        modulate(t + 1)
                    for half in range(2):
                        n = 2 * t + half
                        dve.wait_ge(hi, n + 1)
                        dst = slice(4 * half, 4 * half + 4)
                        dve.tensor_tensor(hTl[:, dst, t * P:(t + 1) * P],
                                          pT[n % 4][:, :].rearrange("p (k c) -> p k c", k=4),
                                          f(hTh[:, dst, t * P:(t + 1) * P]), ALU.subtract).then_inc(lo, 1)


def three(pe, out, lhs, rhs, start, stop):
    pe.matmul(out, lhs[0], rhs[0], start=start, stop=False)
    pe.matmul(out, lhs[0], rhs[1], start=False, stop=False)
    return pe.matmul(out, lhs[1], rhs[0], start=False, stop=stop)


def phase_heads(nc, a, scr, ident, minus_half, hTh, hTl):
    RING, CPS = 4, 4
    NCH = 3 * CPS
    NSL = 2 * NTOK + NX
    with ExitStack() as ctx:
        sb, sem, banks = alloc(nc, ctx, "heads")
        raw = sb("raw", [P, RING, 2, H])
        wh, wl = sb("wh", [P, RING, 2, H], F32R), sb("wl", [P, RING, 2, H], F32R)
        rope = sb("rope", [P, NX, 2, 2, DK // 4])
        rt = sb("rt", [P, 2, 4, 2, 2, DK // 4])
        qk = sb("qk", [P, NTOK, 2, 2, 2, DK // 4])
        qkh, qkl = sb("qkh", [P, 4, NTOK * P], F32R), sb("qkl", [P, 4, NTOK * P], F32R)
        vh, vl = sb("vh", [P, NTOK, DV], F32R), sb("vl", [P, NTOK, DV], F32R)
        gs = sb("gs", [P, NX, DV])
        gn = sb("gn", [P, DV])
        strip = sb("strip", [P, STRIPS])
        af = sb("af", [P, 2, SEQ])
        ah, al = sb("ah", [P, 2, SEQ], F32R), sb("al", [P, 2, SEQ], F32R)
        og = sb("og", [P, NX, DV])
        pad = sb("pad", [1, 1])
        bst, mv = sb("bst", [P, NX, 6]), sb("mv", [P, NX, 4])
        pj, pS = banks("pj", NTOK), banks("pS", 2)
        raw_in = [sem(f"raw_in{i}") for i in range(RING)]
        rope_in, strip_in, gn_in = sem("rope_in"), sem("strip_in"), sem("gn_in")
        hi, lo, chunk_used, proj = sem("w_hi"), sem("w_lo"), sem("chunk_used"), sem("projected")
        rope_read, kc_read, rotated = sem("rope_read"), sem("ctx_key_read"), sem("rotated")
        v_hi, v_lo, g_read, g_ready = sem("v_hi"), sem("v_lo"), sem("gate_read"), sem("gate_ready")
        qkt, qkt_hi, qkt_lo = sem("qk_transposed"), sem("qkT_hi"), sem("qkT_lo")
        s_done, a_f, a_hi, a_lo = sem("scores_done"), sem("att_f32"), sem("att_hi"), sem("att_lo")
        av, o_done, ms, rstd, o_read = sem("av_done"), sem("o_done"), sem("o_var"), sem("o_rstd"), sem("o_read")
        gated, dv = sem("gated"), sem("dve_steps")
        g_out = [sem(f"gated_out{i}") for i in range(NX)]
        w2 = a["ret_w_in"].rearrange("o (k p) (s n) -> p (o k) s n", p=P, n=D)
        w1 = a["ret_w_in"].rearrange("o (k p) n -> p (o k) n", p=P)
        with nc.Block() as block:

            @block.sync
            def _(sp):
                sp.dma_start(rope[:], a["rope"].rearrange("p t (a b c) -> p t a b c", a=2, b=2)).then_inc(rope_in, 16)
                with sp.Fori(0, HEADS) as h:
                    for c in range(NCH):
                        s, cc = c // CPS, c % CPS
                        sp.wait_ge(lo, h * NCH + c + 1)
                        if s == 0:
                            for part in range(2):
                                last = sp.dma_start(raw[:, c % RING, :, part * DK:(part + 1) * DK],
                                                    w1[:, 2 * cc:2 * cc + 2, bass.ds(h * DK + part * D, DK)])
                                last.then_inc(raw_in[c % RING], 16)
                        else:
                            sp.dma_start(raw[:, c % RING], w1[:, 2 * cc:2 * cc + 2, bass.ds(h * DV + 2 * s * D, DV)]
                                         ).then_inc(raw_in[c % RING], 16)
                        if c == 7:
                            sp.wait_ge(g_ready, h * NX + 1)
                            sp.wait_ge(a_lo, h * NTOK + 1)
                            sp.dma_start(strip[:], scr["strips"][bass.ds(h, 1)].rearrange("o p w -> (o p) w")
                                         ).then_inc(strip_in, 16)
                            sp.dma_start(gn[:], a["ret_gn"][0:1, bass.ds(h * DV, DV)].to_broadcast([P, DV])
                                         ).then_inc(gn_in, 16)

            @block.tensor
            def _(pe):
                pe.nop().then_inc(chunk_used, RING - 1)
                pe.nop().then_inc(proj, 1)
                with pe.Fori(0, HEADS) as h:
                    for c in range(NCH):
                        s, cc = c // CPS, c % CPS
                        pe.wait_ge(lo, h * NCH + RING + c + 1)
                        blocks = range(NX if s == 2 else NTOK)
                        for t in blocks:
                            if cc == 0:
                                if s == 0 and t < NX:
                                    pe.wait_ge(o_read, h * NX + t + 1)
                                elif s == 1 and t < NX:
                                    pe.wait_ge(rope_read, h * NX + t + 1)
                                elif s == 1:
                                    pe.wait_ge(kc_read, h * NC + t - NX + 1)
                                elif s == 2:
                                    pe.wait_ge(v_lo, h * NTOK + t + 1)
                            c0 = DK if s == 0 and t >= NX else 0
                            for k in range(2):
                                kk = 2 * cc + k
                                last = three(pe, pj[t][:, c0:H],
                                             (hTh[:, kk, t * P:(t + 1) * P], hTl[:, kk, t * P:(t + 1) * P]),
                                             (wh[:, c % RING, k, c0:H], wl[:, c % RING, k, c0:H]),
                                             kk == 0, kk == KT - 1)
                            if cc == CPS - 1:
                                last.then_inc(proj, 1)
                        if cc < CPS - 1:
                            last.then_inc(chunk_used, 1)
                    for t in range(NTOK):
                        if t < NX:
                            pe.wait_ge(rotated, h * NX + t + 1)
                        else:
                            pe.wait_ge(kc_read, h * NC + t - NX + 1)
                        if t >= 2:
                            pe.wait_ge(qkt_lo, h * NTOK + t - 1)
                        for i in range(0 if t < NX else 2, 4):
                            last = pe.transpose(pS[t % 2][:, i * P:(i + 1) * P],
                                                qk[:, t, i // 2, i % 2].rearrange("p b c -> p (b c)"), ident[:])
                        last.then_inc(qkt, 1)
                    pe.wait_ge(qkt_lo, h * NTOK + NTOK)
                    pe.wait_ge(v_lo, h * NTOK + NTOK)

                    def scores(j):
                        for kk in range(2):
                            last = three(pe, pS[j % 2][:, :],
                                         tuple(m[:, 2 + kk, j * P:(j + 1) * P] for m in (qkh, qkl)),
                                         tuple(m[:, kk, 0:SEQ] for m in (qkh, qkl)), kk == 0, kk == 1)
                        last.then_inc(s_done, 1)

                    def weighted(j):
                        pe.wait_ge(a_lo, h * NTOK + j + 2)
                        for i in range(NX):
                            if j == 0:
                                pe.wait_ge(g_read, h * NX + i + 1)
                            last = three(pe, pj[i][:, :], tuple(m[:, j % 2, i * P:(i + 1) * P] for m in (ah, al)),
                                         (vh[:, j], vl[:, j]), j == 0, j == NTOK - 1)
                            if j == NTOK - 1:
                                last.then_inc(o_done, 1)
                        if j < NTOK - 1:
                            last.then_inc(av, 1)

                    scores(0)
                    for j in range(1, NTOK):
                        scores(j)
                        weighted(j - 1)
                    weighted(NTOK - 1)

            @block.scalar
            def _(act):
                for s in g_out:
                    act.nop().then_inc(s, 1)
                with act.Fori(0, HEADS) as h:

                    def split(c):
                        s, cc = c // CPS, c % CPS
                        n_in = 4
                        done = {0: 2, 1: 3, 2: 4}[s]
                        act.wait_ge(raw_in[c % RING], h * (16 * n_in) + 16 * done)
                        if cc < CPS - 1:
                            act.wait_ge(chunk_used, h * (NCH - 3) + s * (CPS - 1) + cc + 1)
                        else:
                            act.wait_ge(proj, h * NSL + (0, NTOK, 2 * NTOK)[s] + 1)
                        act.activation(wh[:, c % RING], raw[:, c % RING], ACT.Copy).then_inc(hi, 1)

                    for c in range(7):
                        split(c)
                    for t in range(NX, NTOK):
                        act.wait_ge(proj, h * NSL + t + 2)
                        act.activation(qk[:, t, 1].rearrange("p a b c -> p (a b c)"), pj[t][:, DK:H], ACT.Copy
                                       ).then_inc(kc_read, 1)
                    for c in range(7, 11):
                        split(c)
                    for t in range(NTOK):
                        act.wait_ge(proj, h * NSL + NTOK + t + 2)
                        act.activation(vh[:, t], pj[t][:, :], ACT.Copy).then_inc(v_hi, 1)
                    split(11)
                    for t in range(NX):
                        act.wait_ge(proj, h * NSL + 2 * NTOK + t + 2)
                        act.activation(gs[:, t], pj[t][:, :], ACT.Silu).then_inc(g_read, 1)
                    for t in range(NTOK):
                        act.wait_ge(qkt, h * NTOK + t + 1)
                        i = 0 if t < NX else 2
                        act.activation(qkh[:, i:4, t * P:(t + 1) * P],
                                       pS[t % 2][:, i * P:].rearrange("p (i c) -> p i c", c=P), ACT.Copy
                                       ).then_inc(qkt_hi, 1)
                    for j in range(NTOK):
                        act.wait_ge(a_f, h * NTOK + j + 1)
                        if j >= 2:
                            act.wait_ge(av, h * (NTOK - 1) + j - 1)
                        act.activation(ah[:, j % 2], af[:, j % 2], ACT.Copy).then_inc(a_hi, 1)
                    for i in range(NX):
                        act.wait_ge(gated, h * NX + i + 1)
                        act.dma_start(scr["gated"][i * P:(i + 1) * P, bass.ds(h * DV, DV)], og[:, i]
                                      ).then_inc(g_out[i], 16)
                for s in g_out:
                    act.wait_ge(s, 16 * HEADS + 1)

            @block.gpsimd
            def _(pool):
                pool.nop().then_inc(g_ready, 1)
                with pool.Fori(0, HEADS) as h:
                    for t in range(NX):
                        pool.wait_ge(rope_read, h * NX + t + 1)
                        m = rt[:, t % 2]
                        pool.tensor_tensor(qk[:, t, :, :, 0], m[:, 0], m[:, 1], ALU.subtract)
                        pool.tensor_tensor(qk[:, t, :, :, 1], m[:, 2], m[:, 3], ALU.add).then_inc(rotated, 1)
                    pool.wait_ge(gn_in, h * 16 + 16)
                    for t in range(NX):
                        pool.wait_ge(g_read, h * NX + t + 1)
                        pool.tensor_tensor(gs[:, t], gs[:, t], gn[:], ALU.mult).then_inc(g_ready, 1)
                    for i in range(NX):
                        pool.wait_ge(ms, h * NX + i + 1)
                        pool.tensor_tensor(mv[:, i, 3:4], mv[:, i, 2:3], minus_half[:, 0:1], ALU.pow
                                           ).then_inc(rstd, 1)

            @block.vector
            def _(dve):
                dve.nop().then_inc(lo, RING)
                dve.nop().then_inc(o_read, NX)
                dve.nop().then_inc(a_lo, 1)
                dve.wait_ge(rope_in, 16)
                with dve.Fori(0, HEADS) as h:

                    def split(c):
                        dve.wait_ge(hi, h * NCH + c + 1)
                        dve.tensor_tensor(wl[:, c % RING], raw[:, c % RING], f(wh[:, c % RING]), ALU.subtract
                                          ).then_inc(lo, 1)

                    for c in range(7):
                        split(c)
                    for t in range(NX):
                        dve.wait_ge(proj, h * NSL + t + 2)
                        if t >= 2:
                            dve.wait_ge(rotated, h * NX + t - 1)
                        m = rt[:, t % 2]
                        src = pj[t][:, :].rearrange("p (q s b c) -> p q s b c", q=2, s=2, b=2)
                        cos = rope[:, t, 0:1].to_broadcast([P, 2, 2, DK // 4])
                        sin = rope[:, t, 1:2].to_broadcast([P, 2, 2, DK // 4])
                        dve.tensor_tensor(m[:, 0], src[:, :, :, 0], cos, ALU.mult)
                        dve.tensor_tensor(m[:, 1], src[:, :, :, 1], sin, ALU.mult)
                        dve.tensor_tensor(m[:, 2], src[:, :, :, 0], sin, ALU.mult)
                        dve.tensor_tensor(m[:, 3], src[:, :, :, 1], cos, ALU.mult).then_inc(rope_read, 1)
                    for c in range(7, 11):
                        split(c)
                    for t in range(NTOK):
                        dve.wait_ge(v_hi, h * NTOK + t + 1)
                        dve.tensor_tensor(vl[:, t], pj[t][:, :], f(vh[:, t]), ALU.subtract).then_inc(v_lo, 1)
                    split(11)
                    for t in range(NTOK):
                        dve.wait_ge(qkt_hi, h * NTOK + t + 1)
                        i = 0 if t < NX else 2
                        dve.tensor_tensor(qkl[:, i:4, t * P:(t + 1) * P],
                                          pS[t % 2][:, i * P:].rearrange("p (i c) -> p i c", c=P),
                                          f(qkh[:, i:4, t * P:(t + 1) * P]), ALU.subtract).then_inc(qkt_lo, 1)
                    dve.wait_ge(strip_in, h * 16 + 16)
                    for j in range(NTOK):
                        at = XO - j * P if j < NX else XR + P - (j - NX) * P
                        dve.wait_ge(s_done, h * NTOK + j + 1)
                        dve.scalar_tensor_tensor(af[:, j % 2], pS[j % 2][:, :], DK ** -0.5, strip[:, at:at + SEQ],
                                                 ALU.mult, ALU.mult).then_inc(a_f, 1)
                        dve.wait_ge(a_hi, h * NTOK + j + 1)
                        dve.tensor_tensor(al[:, j % 2], af[:, j % 2], f(ah[:, j % 2]), ALU.subtract
                                          ).then_inc(a_lo, 1)
                    n = 0
                    PER = 2 * NX

                    def step(ins):
                        nonlocal n
                        n += 1
                        ins.then_inc(dv, 1)
                        dve.wait_ge(dv, h * PER + n)

                    dve.wait_ge(g_ready, h * NX + NX + 1)
                    for i in range(NX):
                        dve.wait_ge(o_done, h * NX + i + 1)
                        step(dve.bn_stats(bst[:, i], pj[i][:, :]))
                        dve.memset(pad[:], 0.0)
                        step(dve.bn_aggr(mv[:, i, 0:2], bst[:, i]))
                        dve.tensor_scalar(mv[:, i, 2:3], mv[:, i, 1:2], EPS, None, ALU.add).then_inc(ms, 1)
                        dve.wait_ge(rstd, h * NX + i + 1)
                        dve.wait_ge(g_out[i], h * 16 + 1)
                        dve.tensor_scalar(og[:, i], pj[i][:, :], mv[:, i, 0:1], mv[:, i, 3:4],
                                          ALU.subtract, ALU.mult).then_inc(o_read, 1)
                        dve.wait_ge(o_read, h * NX + NX + i + 1)
                        dve.tensor_tensor(og[:, i], og[:, i], gs[:, i], ALU.mult).then_inc(gated, 1)


def project_residual(nc, a, scr, tag, layer, kt, w_view, gT, x_src, res, ident, gated=None):
    RING = 4
    with ExitStack() as ctx:
        sb, sem, banks = alloc(nc, ctx, tag)
        raw = sb("raw", [P, RING, D])
        wh, wl = sb("wh", [P, RING, D], F32R), sb("wl", [P, RING, D], F32R)
        gate = sb("gate", [P, D])
        xin = sb("xin", [P, NX, D]) if x_src is not None else None
        rows = sb("rows", [P, NX, kt * P]) if gated is not None else None
        acc = banks("acc", 2 * NX)
        raw_in = [sem(f"raw_in{i}") for i in range(RING)]
        rows_in = [sem(f"rows_in{t}") for t in range(NX)]
        gate_in, x_in = sem("gate_in"), sem("x_in")
        tr, g_hi, g_lo = sem("transposed"), sem("g_hi"), sem("g_lo")
        hi, lo, used, done, dv = sem("w_hi"), sem("w_lo"), sem("chunk_used"), sem("acc_done"), sem("dve_steps")
        groups = NX * kt // 4 if gated is not None else 0
        with nc.Block() as block:

            @block.sync
            def _(sp):
                if gated is not None:
                    for t in range(NX):
                        sp.dma_start(rows[:, t], gated[t * P:(t + 1) * P, :]).then_inc(rows_in[t], 16)
                for k in range(kt):
                    if k >= RING:
                        sp.wait_ge(lo, k - RING + 1)
                    sp.dma_start(raw[:, k % RING], w_view[:, k, :]).then_inc(raw_in[k % RING], 16)
                    if k == 3:
                        sp.dma_start(gate[:], scr["mod"][layer, 0:1, 2 * D:3 * D].to_broadcast([P, D])
                                     ).then_inc(gate_in, 16)
                        if xin is not None:
                            sp.dma_start(xin[:], x_src.rearrange("(t p) d -> p t d", p=P)).then_inc(x_in, 16)

            @block.tensor
            def _(pe):
                for n in range(groups):
                    t, q = n // (kt // 4), n % (kt // 4)
                    if q == 0:
                        pe.wait_ge(rows_in[t], 16)
                    if n >= 2 * NX:
                        pe.wait_ge(g_lo, n - 2 * NX + 1)
                    for k in range(4):
                        last = pe.transpose(acc[n % (2 * NX)][:, k * P:(k + 1) * P],
                                            rows[:, t, (4 * q + k) * P:(4 * q + k + 1) * P], ident[:])
                    last.then_inc(tr, 1)
                if groups:
                    pe.wait_ge(g_lo, groups)
                for k in range(kt):
                    pe.wait_ge(lo, k + 1)
                    for t in range(NX):
                        for half in range(2):
                            cols = slice(half * H, (half + 1) * H)
                            last = three(pe, acc[2 * t + half][:, :], tuple(m[:, k, t * P:(t + 1) * P] for m in gT),
                                         (wh[:, k % RING, cols], wl[:, k % RING, cols]), k == 0, k == kt - 1)
                            if k == kt - 1:
                                last.then_inc(done, 1)
                    if k < kt - 1:
                        last.then_inc(used, 1)

            @block.scalar
            def _(act):
                for n in range(groups):
                    t, q = n // (kt // 4), n % (kt // 4)
                    act.wait_ge(tr, n + 1)
                    act.activation(gT[0][:, 4 * q:4 * q + 4, t * P:(t + 1) * P],
                                   acc[n % (2 * NX)][:, :].rearrange("p (k c) -> p k c", k=4), ACT.Copy
                                   ).then_inc(g_hi, 1)
                for k in range(kt):
                    act.wait_ge(raw_in[k % RING], 16 * (k // RING + 1))
                    if k >= RING:
                        act.wait_ge(used, k - RING + 1)
                    act.activation(wh[:, k % RING], raw[:, k % RING], ACT.Copy).then_inc(hi, 1)

            @block.vector
            def _(dve):
                own = Count(dv)
                for n in range(groups):
                    t, q = n // (kt // 4), n % (kt // 4)
                    dve.wait_ge(g_hi, n + 1)
                    at = (slice(None), slice(4 * q, 4 * q + 4), slice(t * P, (t + 1) * P))
                    dve.tensor_tensor(gT[1][at], acc[n % (2 * NX)][:, :].rearrange("p (k c) -> p k c", k=4),
                                      f(gT[0][at]), ALU.subtract).then_inc(g_lo, 1)
                for k in range(kt):
                    dve.wait_ge(hi, k + 1)
                    dve.tensor_tensor(wl[:, k % RING], raw[:, k % RING], f(wh[:, k % RING]), ALU.subtract
                                      ).then_inc(lo, 1)
                dve.wait_ge(gate_in, 16)
                if xin is not None:
                    dve.wait_ge(x_in, 16)
                for t in range(NX):
                    for half in range(2):
                        cols = slice(half * H, (half + 1) * H)
                        dve.wait_ge(done, 2 * t + half + 1)
                        y = raw[:, half, 0:H]
                        own.inc(dve.tensor_tensor(y, acc[2 * t + half][:, :], gate[:, cols], ALU.mult))
                        own.after(dve)
                        x_old = xin[:, t, cols] if xin is not None else res[:, t, cols]
                        own.inc(dve.tensor_tensor(res[:, t, cols], x_old, y, ALU.add))


def phase_route(nc, a, scr, ident, minus_half, layer, res, dest, wk, table):
    with ExitStack() as ctx:
        sb, sem, banks = alloc(nc, ctx, f"route{layer}")
        tok = sb("tok", [P, NX, D])
        fT = sb("fT", [P, 2, KT, P])
        md, nm, junk = sb("md", [P, 2, D]), sb("nm", [P, D]), sb("junk", [P, D])
        rw = sb("rw", [P, KT, NE])
        bias, order = sb("bias", [P, NE]), sb("order", [P, NE + NG + MAX_OVER + 1])
        below = sb("below", [P, 2, P])
        ss, rs = sb("ss", [P, NX]), sb("rs", [P, NX])
        sc, sel, oh0, oh1, tmp, both = (sb(n, [P, NX, NE]) for n in ("sc", "sel", "oh0", "oh1", "tmp", "both"))
        rank = sb("rank", [P, NX, NE])
        pair = sb("pair", [P, NX * NG, 6])
        gsum, gone, gkey = (sb(n, [P, NX, NG]) for n in ("gsum", "gone", "gkey"))
        mx, wf, df = sb("mx", [P, NX, 1]), sb("wf", [P, NX, 2]), sb("df", [P, NX, 2])
        cnt = sb("cnt", [P, 8, NE])
        cmp_ = sb("cmp", [P, MAX_OVER, NE])
        tf = sb("tf", [P, NBLK + 1])
        pT, pL = banks("pT", 4), banks("pL", 3)
        in_tok, in_c, sq, ms, rs_ok = sem("mod_in"), sem("consts_in"), sem("squares"), sem("ms"), sem("rs_ready")
        tok_ok, tr, fT_ok, logit, score = sem("tok_ready"), sem("transposed"), sem("fT_ready"), sem("logits"), sem("scores")
        chosen, ranked, placed, dv = sem("chosen"), sem("ranked"), sem("placed"), sem("dve_steps")
        sent = sem("rows_sent")
        with nc.Block() as block:

            @block.sync
            def _(sp):
                for v in range(2):
                    sp.dma_start(md[:, v], scr["mod"][layer, 0:1, (3 + v) * D:(4 + v) * D].to_broadcast([P, D])
                                 ).then_inc(in_tok, 16)
                sp.dma_start(nm[:], a["norm_ffn"][layer:layer + 1, :].to_broadcast([P, D])).then_inc(in_tok, 16)
                sp.dma_start(rw[:], a["router_w"].rearrange("(k p) e -> p k e", p=P)).then_inc(in_c, 16)
                sp.dma_start(bias[:], a["router_bias"].rearrange("(o e) -> o e", o=1).to_broadcast([P, NE])
                             ).then_inc(in_c, 16)
                sp.dma_start(order[:], a["order"].to_broadcast([P, NE + NG + MAX_OVER + 1])).then_inc(in_c, 16)
                sp.dma_start(below[:], a["below"].rearrange("s p c -> p s c")).then_inc(in_c, 16)

            @block.scalar
            def _(act):
                for t in range(NX):
                    if t:
                        act.wait_ge(sq, t)
                    act.activation(junk[:], res[:, t], ACT.Square, accum_out=ss[:, t:t + 1]).then_inc(sq, 1)
                for t in range(NX):
                    for half in range(2):
                        n = 2 * t + half
                        act.wait_ge(tr, n + 1)
                        if t >= 2:
                            act.wait_ge(logit, t - 1)
                        act.activation(fT[:, t % 2, 4 * half:4 * half + 4].rearrange("p k c -> p (k c)"),
                                       pT[n % 4][:, :], ACT.Copy).then_inc(fT_ok, 1)
                act.wait_ge(logit, NX)
                act.activation(sc[:].rearrange("p t e -> p (t e)"), pL[0][:, 0:NX * NE], ACT.Sigmoid).then_inc(score, 1)

            @block.gpsimd
            def _(pool):
                pool.wait_ge(ms, 1)
                pool.tensor_tensor(rs[:], ss[:], minus_half[:, 0:NX], ALU.pow).then_inc(rs_ok, 1)
                pool.wait_ge(placed, 1)
                for t in range(NX):
                    for s in range(2):
                        pool.indirect_dma_start(
                            out=scr["xs"], out_offset=bass.IndirectOffsetOnAxis(ap=dest[:, 0, s, t:t + 1].bitcast(U32), axis=0),
                            in_=tok[:, t], in_offset=None, bounds_check=(NBLK + 1) * P - 1, oob_is_err=False
                        ).then_inc(sent, 16)
                pool.wait_ge(sent, 16 * 2 * NX)

            @block.tensor
            def _(pe):
                pe.wait_ge(in_c, 64)

                def logits(t):
                    pe.wait_ge(fT_ok, 2 * t + 2)
                    for k in range(KT):
                        last = pe.matmul(pL[0][:, t * NE:(t + 1) * NE], fT[:, t % 2, k], rw[:, k],
                                         start=k == 0, stop=k == KT - 1)
                    last.then_inc(logit, 1)

                for t in range(NX):
                    pe.wait_ge(tok_ok, t + 1)
                    for half in range(2):
                        n = 2 * t + half
                        if n >= 4:
                            pe.wait_ge(fT_ok, n - 3)
                        for k in range(4):
                            last = pe.transpose(pT[n % 4][:, k * P:(k + 1) * P],
                                                tok[:, t, (4 * half + k) * P:(4 * half + k + 1) * P], ident[:])
                        last.then_inc(tr, 1)
                    if t:
                        logits(t - 1)
                logits(NX - 1)
                pe.wait_ge(chosen, 1)
                for t in range(NX):
                    for u in range(t + 1):
                        last = pe.matmul(pL[1][:, t * NE:(t + 1) * NE], below[:, 0 if u == t else 1], both[:, u],
                                         start=u == 0, stop=u == t)
                for u in range(NX):
                    last = pe.matmul(pL[2][:, 0:NE], below[:, 1], both[:, u], start=u == 0, stop=u == NX - 1)
                last.then_inc(ranked, 1)

            @block.vector
            def _(dve):
                own = Count(dv)

                def step(ins):
                    own.inc(ins)
                    own.after(dve)

                dve.wait_ge(sq, NX)
                dve.tensor_scalar(ss[:], ss[:], 1.0 / D, EPS, ALU.mult, ALU.add).then_inc(ms, 1)
                dve.wait_ge(in_tok, 48)
                step(dve.scalar_tensor_tensor(md[:, 1], md[:, 1], 1.0, nm[:], ALU.add, ALU.mult))
                dve.wait_ge(rs_ok, 1)
                for t in range(NX):
                    step(dve.scalar_tensor_tensor(tok[:, t], res[:, t], rs[:, t:t + 1], md[:, 1], ALU.mult, ALU.mult))
                    dve.tensor_tensor(tok[:, t], tok[:, t], md[:, 0], ALU.add).then_inc(tok_ok, 1)
                dve.wait_ge(in_c, 64)
                dve.wait_ge(score, 1)
                flat = [P, NX * NG, EPG]
                step(dve.tensor_tensor(sel[:], sc[:], bias[:].rearrange("p (o e) -> p o e", o=1).to_broadcast([P, NX, NE]),
                                       ALU.add))
                s4 = sel[:].rearrange("p t (g e) -> p (t g) e", e=EPG)
                pairs = [(i, j) for i in range(EPG) for j in range(i + 1, EPG)]
                for n, (i, j) in enumerate(pairs):
                    own.inc(dve.tensor_tensor(pair[:, :, n:n + 1], s4[:, :, i:i + 1], s4[:, :, j:j + 1], ALU.add))
                own.after(dve)
                step(dve.tensor_reduce(gsum[:].rearrange("p t g -> p (t g)"), pair[:], AX.X, ALU.max))

                def first_largest(out, v, key, n, first):
                    step(dve.tensor_reduce(mx[:].rearrange("p t o -> p (t o)"), v, AX.X, ALU.max))
                    step(dve.tensor_tensor(key, v, mx[:].to_broadcast([P, NX, n]), ALU.is_ge))
                    step(dve.tensor_tensor(key, key, first.rearrange("p (o e) -> p o e", o=1).to_broadcast([P, NX, n]),
                                           ALU.mult))
                    step(dve.tensor_reduce(mx[:].rearrange("p t o -> p (t o)"), key, AX.X, ALU.max))
                    step(dve.tensor_tensor(out, key, mx[:].to_broadcast([P, NX, n]), ALU.is_equal))

                first_largest(gone[:], gsum[:], gkey[:], NG, order[:, NE:NE + NG])
                step(dve.tensor_scalar(gkey[:], gone[:], BIG, -BIG, ALU.mult, ALU.add))
                step(dve.tensor_tensor(s4, s4, gkey[:].rearrange("p t (g o) -> p (t g) o", o=1).to_broadcast(flat), ALU.add))
                for s, oh in enumerate((oh0, oh1)):
                    first_largest(oh[:], sel[:], tmp[:], NE, order[:, 0:NE])
                    if s == 0:
                        step(dve.scalar_tensor_tensor(sel[:], oh[:], -2 * BIG, sel[:], ALU.mult, ALU.add))
                    step(dve.tensor_tensor(tmp[:], oh[:], sc[:], ALU.mult))
                    step(dve.tensor_reduce(wf[:, :, s], tmp[:], AX.X, ALU.add))
                dve.tensor_tensor(both[:], oh0[:], oh1[:], ALU.add).then_inc(chosen, 1)
                step(dve.tensor_tensor(mx[:], wf[:, :, 0:1], wf[:, :, 1:2], ALU.add))
                step(dve.reciprocal(mx[:], mx[:]))
                step(dve.tensor_tensor(wk[:], wf[:], mx[:].to_broadcast([P, NX, 2]), ALU.mult))
                dve.wait_ge(ranked, 1)
                step(dve.tensor_copy(rank[:].rearrange("p t e -> p (t e)"), pL[1][:, 0:NX * NE]))
                total, more, end, other = (cnt[:, i] for i in range(4))
                step(dve.tensor_copy(total, pL[2][:, 0:NE]))
                step(dve.tensor_scalar(more, total, float(P), None, ALU.is_gt))
                for m in range(2, SEQ // P):
                    step(dve.scalar_tensor_tensor(more, total, float(m * P), more, ALU.is_gt, ALU.add))
                step(dve.tensor_copy(end, more))
                src, dst = end, other
                for d in (1, 2, 4, 8):
                    own.inc(dve.tensor_copy(dst[:, 0:d], src[:, 0:d]))
                    step(dve.tensor_tensor(dst[:, d:], src[:, d:], src[:, 0:NE - d], ALU.add))
                    src, dst = dst, src
                end = src
                base, over = cnt[:, 4], cnt[:, 5]
                step(dve.tensor_scalar(base, order[:, 0:NE], -float(P), float(NE * P), ALU.mult, ALU.add))
                step(dve.tensor_tensor(over, end, more, ALU.subtract))
                step(dve.tensor_scalar(over, over, float(P), float(NE * P - P), ALU.mult, ALU.add))
                step(dve.tensor_tensor(over, over, base, ALU.subtract))
                wide = lambda v: v.rearrange("p (o e) -> p o e", o=1).to_broadcast([P, NX, NE])
                step(dve.tensor_scalar(tmp[:], rank[:], float(P), None, ALU.is_ge))
                step(dve.tensor_tensor(tmp[:], tmp[:], wide(over), ALU.mult))
                step(dve.tensor_tensor(tmp[:], tmp[:], wide(base), ALU.add))
                step(dve.tensor_tensor(rank[:], rank[:], tmp[:], ALU.add))
                for s, oh in enumerate((oh0, oh1)):
                    step(dve.tensor_tensor(tmp[:], oh[:], rank[:], ALU.mult))
                    step(dve.tensor_reduce(df[:, :, s], tmp[:], AX.X, ALU.add))
                step(dve.tensor_copy(dest[:, 0], df[:].rearrange("p t s -> p s t")))
                step(dve.tensor_scalar(df[:], df[:], float(P), None, ALU.add))
                step(dve.tensor_copy(dest[:, 1], df[:].rearrange("p t s -> p s t")))
                step(dve.tensor_scalar(tf[:, 0:NE], order[:, 0:NE], -1.0, float(NE), ALU.mult, ALU.add))
                step(dve.tensor_tensor(cmp_[:], end.rearrange("p (o e) -> p o e", o=1).to_broadcast([P, MAX_OVER, NE]),
                                       order[:, NE + NG:NE + NG + MAX_OVER].rearrange("p (b o) -> p b o", o=1
                                                                                      ).to_broadcast([P, MAX_OVER, NE]),
                                       ALU.is_le))
                step(dve.tensor_reduce(tf[:, NE:NBLK], cmp_[:], AX.X, ALU.add))
                step(dve.tensor_scalar(tf[:, NE:NBLK], tf[:, NE:NBLK], float(NE - 1), None, ALU.min))
                step(dve.tensor_scalar(tf[:, NBLK:NBLK + 1], end[:, NE - 1:NE], float(NE), None, ALU.add))
                step(dve.tensor_copy(table[:], tf[:]))
                dve.nop().then_inc(placed, 1)


def phase_experts(nc, a, scr, ident, layer, table):
    RAW, RING = 12, 8
    NCH = 3 * KT
    with ExitStack() as ctx:
        sb, sem, banks = alloc(nc, ctx, f"moe{layer}")
        raw = sb("raw", [P, RAW, D])
        wh, wl = sb("wh", [P, RING, D], F32R), sb("wl", [P, RING, D], F32R)
        xb, sg, hs, yb = sb("xb", [P, D]), sb("sg", [P, D]), sb("hs", [P, D]), sb("yb", [P, D])
        xh, xl = sb("xh", [P, KT, P], F32R), sb("xl", [P, KT, P], F32R)
        hh, hl = sb("hh", [P, KT, P], F32R), sb("hl", [P, KT, P], F32R)
        pg, pu, pd, pT = banks("pg", 2), banks("pu", 2), banks("pd", 2), banks("pT", 2)
        raw_in = [sem(f"raw_in{i}") for i in range(RAW)]
        x_in, x_t, x_hi, x_lo = sem("x_in"), sem("x_transposed"), sem("x_hi"), sem("x_lo")
        hi, lo, used = sem("w_hi"), sem("w_lo"), sem("chunk_used")
        sg_ok, h_ok, h_t, h_hi, h_lo = sem("silu_ready"), sem("h_ready"), sem("h_transposed"), sem("h_hi"), sem("h_lo")
        y_read, y_out, d_set = sem("y_read"), sem("y_out"), sem("y_first")
        weights = [a[n][layer].rearrange("e (k p) n -> e p k n", p=P) for n in ("moe_w_gate", "moe_w_up", "moe_w_down")]
        xs = scr["xs"].rearrange("(b p) d -> b p d", p=P)
        ys = scr["ys"].rearrange("(b p) d -> b p d", p=P)

        def turns(eng, body, bound):
            with eng.Fori(0, NBLK) as b:
                with eng.If(b < bound):
                    body(b)
                with eng.Else():
                    eng.nop()
            eng.nop()

        with nc.Block() as block:

            @block.sync
            def _(sp):
                bound = sp.value_load(table[0:1, NBLK:NBLK + 1], min_val=NE, max_val=NBLK)
                sp.dma_start(xb[:], xs[0]).then_inc(x_in, 16)

                def body(b):
                    e = sp.value_load(table[0:1, bass.ds(b, 1)], min_val=0, max_val=NE - 1)
                    for c in range(NCH):
                        sp.wait_ge(lo, b * NCH + c + 1)
                        sp.dma_start(raw[:, c % RAW],
                                     weights[c // KT][bass.ds(e, 1), :, c % KT, :].rearrange("o p n -> (o p) n")
                                     ).then_inc(raw_in[c % RAW], 16)
                        if c == 4:
                            sp.wait_ge(x_t, b * 2 + 2)
                            sp.dma_start(xb[:], xs[bass.ds(b + 1, 1)].rearrange("o p d -> (o p) d")).then_inc(x_in, 16)

                turns(sp, body, bound)

            @block.tensor
            def _(pe):
                pe.nop().then_inc(used, RING)
                bound = pe.value_load(table[0:1, NBLK:NBLK + 1], min_val=NE, max_val=NBLK)

                def transpose_x():
                    for half in range(2):
                        for k in range(4):
                            last = pe.transpose(pT[half][:, k * P:(k + 1) * P],
                                                xb[:, (4 * half + k) * P:(4 * half + k + 1) * P], ident[:])
                        last.then_inc(x_t, 1)

                pe.wait_ge(x_in, 16)
                for half in range(2):
                    pe.matmul(pd[half][:, :], ident[:], xb[:, half * H:(half + 1) * H], start=True, stop=True
                              ).then_inc(d_set, 1)
                transpose_x()

                def body(b):
                    pe.wait_ge(x_lo, b * 2 + 2)
                    for c in range(NCH):
                        k = c % KT
                        pe.wait_ge(lo, b * NCH + RAW + c + 1)
                        if c < 2 * KT:
                            out, lhs = (pg, pu)[c // KT], (xh[:, k], xl[:, k])
                        else:
                            out, lhs = pd, (hh[:, k], hl[:, k])
                            if k == 0:
                                pe.wait_ge(y_read, b * 2 + 2)
                            if k % 4 == 0:
                                pe.wait_ge(h_lo, b * 2 + k // 4 + 1)
                        for half in range(2):
                            cols = slice(half * H, (half + 1) * H)
                            last = three(pe, out[half][:, :], lhs, (wh[:, c % RING, cols], wl[:, c % RING, cols]),
                                         k == 0, k == KT - 1)
                        last.then_inc(used, 1)
                        if c == 2 * KT - 1:
                            for half in range(2):
                                pe.wait_ge(h_ok, b * 2 + half + 1)
                                for kk in range(4):
                                    last = pe.transpose(pT[half][:, kk * P:(kk + 1) * P],
                                                        hs[:, (4 * half + kk) * P:(4 * half + kk + 1) * P], ident[:])
                                last.then_inc(h_t, 1)
                        if c == 2 * KT + 4:
                            pe.wait_ge(x_in, b * 16 + 32)
                            transpose_x()

                turns(pe, body, bound)

            @block.scalar
            def _(act):
                bound = act.value_load(table[0:1, NBLK:NBLK + 1], min_val=NE, max_val=NBLK)

                def x_parts(n0):
                    for half in range(2):
                        act.wait_ge(x_t, n0 + half)
                        act.activation(xh[:, 4 * half:4 * half + 4].rearrange("p k c -> p (k c)"), pT[half][:, :],
                                       ACT.Copy).then_inc(x_hi, 1)

                x_parts(1)

                act.wait_ge(d_set, 2)

                def store(b):
                    act.wait_ge(used, b * NCH + RING)
                    act.wait_ge(y_out, b * 16 + 1)
                    for half in range(2):
                        act.activation(yb[:, half * H:(half + 1) * H], pd[half][:, :], ACT.Copy).then_inc(y_read, 1)
                    act.wait_ge(y_read, b * 2 + 2)
                    act.dma_start(ys[bass.ds(b, 1)].rearrange("o p d -> (o p) d"), yb[:]).then_inc(y_out, 16)

                act.nop().then_inc(y_out, 1)

                def body(b):
                    for c in range(NCH):
                        act.wait_ge(raw_in[c % RAW], b * (16 * NCH // RAW) + 16 * (c // RAW + 1))
                        act.wait_ge(used, b * NCH + c + 1)
                        act.activation(wh[:, c % RING], raw[:, c % RAW], ACT.Copy).then_inc(hi, 1)
                        if c == 3:
                            store(b)
                        if c == 12:
                            act.wait_ge(used, b * NCH + RING + KT)
                            for half in range(2):
                                act.activation(sg[:, half * H:(half + 1) * H], pg[half][:, :], ACT.Silu).then_inc(sg_ok, 1)
                        if c == 19:
                            for half in range(2):
                                act.wait_ge(h_t, b * 2 + half + 1)
                                act.activation(hh[:, 4 * half:4 * half + 4].rearrange("p k c -> p (k c)"), pT[half][:, :],
                                               ACT.Copy).then_inc(h_hi, 1)
                    x_parts(b * 2 + 3)

                turns(act, body, bound)
                store(bound)
                act.wait_ge(y_out, bound * 16 + 17)
                act.activation(yb[0:1, 0:1], sg[0:1, 0:1], ACT.Copy)

            @block.vector
            def _(dve):
                dve.nop().then_inc(lo, RAW)
                bound = dve.value_load(table[0:1, NBLK:NBLK + 1], min_val=NE, max_val=NBLK)

                def x_parts(n0):
                    for half in range(2):
                        dve.wait_ge(x_hi, n0 + half)
                        at = xh[:, 4 * half:4 * half + 4].rearrange("p k c -> p (k c)")
                        dve.tensor_tensor(xl[:, 4 * half:4 * half + 4].rearrange("p k c -> p (k c)"), pT[half][:, :],
                                          f(at), ALU.subtract).then_inc(x_lo, 1)

                x_parts(1)

                def body(b):
                    for c in range(NCH):
                        dve.wait_ge(hi, b * NCH + c + 1)
                        dve.tensor_tensor(wl[:, c % RING], raw[:, c % RAW], f(wh[:, c % RING]), ALU.subtract
                                          ).then_inc(lo, 1)
                        if c == 19:
                            dve.wait_ge(used, b * NCH + RING + 2 * KT)
                            for half in range(2):
                                cols = slice(half * H, (half + 1) * H)
                                dve.wait_ge(sg_ok, b * 2 + half + 1)
                                dve.tensor_tensor(hs[:, cols], pu[half][:, :], sg[:, cols], ALU.mult).then_inc(h_ok, 1)
                            for half in range(2):
                                dve.wait_ge(h_hi, b * 2 + half + 1)
                                at = hh[:, 4 * half:4 * half + 4].rearrange("p k c -> p (k c)")
                                dve.tensor_tensor(hl[:, 4 * half:4 * half + 4].rearrange("p k c -> p (k c)"),
                                                  pT[half][:, :], f(at), ALU.subtract).then_inc(h_lo, 1)
                    x_parts(b * 2 + 3)

                turns(dve, body, bound)


def phase_combine(nc, a, scr, layer, res, dest, wk, minus_half, then):
    with ExitStack() as ctx:
        sb, sem, banks = alloc(nc, ctx, f"combine{layer}")
        yg = sb("yg", [P, 2, NX, D])
        gate, nm, junk = sb("gate", [P, D]), sb("nm", [P, D]), sb("junk", [P, 2, D])
        md = sb("md", [P, 2, D])
        ss, rs = sb("ss", [P, NX]), sb("rs", [P, NX])
        got = [[sem(f"y{s}_{t}") for t in range(NX)] for s in range(2)]
        c_in, sq, ms, rs_ok, dv, res_ok = (sem(n) for n in ("consts_in", "squares", "ms", "rs_ready", "dve_steps", "res_ready"))
        h_f32, h_hi, outs, normed = sem("h_f32"), sem("h_hi"), sem("outs"), sem("normed")
        norm_row, mod_layer, hh, hl = then
        with nc.Block() as block:

            @block.gpsimd
            def _(pool):
                for t in range(NX):
                    for s in range(2):
                        pool.indirect_dma_start(
                            out=yg[:, s, t], out_offset=None, in_=scr["ys"],
                            in_offset=bass.IndirectOffsetOnAxis(ap=dest[:, 1, s, t:t + 1].bitcast(U32), axis=0),
                            bounds_check=(NBLK + 1) * P - 1, oob_is_err=False).then_inc(got[s][t], 16)
                for t in range(NX):
                    pool.wait_ge(ms, t + 1)
                    pool.tensor_tensor(rs[:, t:t + 1], ss[:, t:t + 1], minus_half[:, 0:1], ALU.pow).then_inc(rs_ok, 1)

            @block.sync
            def _(sp):
                sp.dma_start(gate[:], scr["mod"][layer, 0:1, 5 * D:6 * D].to_broadcast([P, D])).then_inc(c_in, 16)
                sp.dma_start(nm[:], norm_row.to_broadcast([P, D])).then_inc(c_in, 16)
                if mod_layer is not None:
                    for v in range(2):
                        sp.dma_start(md[:, v], scr["mod"][mod_layer, 0:1, v * D:(v + 1) * D].to_broadcast([P, D])
                                     ).then_inc(c_in, 16)
                else:
                    for t in range(NX):
                        sp.wait_ge(normed, t + 1)
                        sp.dma_start(a["out"][0, t * P:(t + 1) * P, :], yg[:, 0, t]).then_inc(outs, 16)
                    sp.wait_ge(outs, 16 * NX)

            @block.scalar
            def _(act):
                for t in range(NX):
                    act.wait_ge(res_ok, t + 1)
                    if t >= 2:
                        act.wait_ge(sq, t - 1)
                    act.activation(junk[:, t % 2], res[:, t], ACT.Square, accum_out=ss[:, t:t + 1]).then_inc(sq, 1)
                if mod_layer is not None:
                    for t in range(NX):
                        act.wait_ge(h_f32, t + 1)
                        act.activation(hh[:, t], yg[:, 0, t], ACT.Copy).then_inc(h_hi, 1)

            @block.vector
            def _(dve):
                own = Count(dv)

                def step(ins):
                    own.inc(ins)
                    own.after(dve)

                dve.wait_ge(c_in, 16 * (4 if mod_layer is not None else 2))
                if mod_layer is not None:
                    step(dve.scalar_tensor_tensor(md[:, 1], md[:, 1], 1.0, nm[:], ALU.add, ALU.mult))
                for t in range(NX):
                    for s in range(2):
                        dve.wait_ge(got[s][t], 16)
                    step(dve.tensor_scalar(yg[:, 0, t], yg[:, 0, t], wk[:, t, 0:1], None, ALU.mult))
                    step(dve.scalar_tensor_tensor(yg[:, 0, t], yg[:, 1, t], wk[:, t, 1:2], yg[:, 0, t],
                                                  ALU.mult, ALU.add))
                    step(dve.tensor_tensor(yg[:, 0, t], yg[:, 0, t], gate[:], ALU.mult))
                    dve.tensor_tensor(res[:, t], res[:, t], yg[:, 0, t], ALU.add).then_inc(res_ok, 1)
                for t in range(NX):
                    dve.wait_ge(sq, t + 1)
                    dve.tensor_scalar(ss[:, t:t + 1], ss[:, t:t + 1], 1.0 / D, EPS, ALU.mult, ALU.add).then_inc(ms, 1)
                    dve.wait_ge(rs_ok, t + 1)
                    scale = md[:, 1] if mod_layer is not None else nm[:]
                    ins = dve.scalar_tensor_tensor(yg[:, 0, t], res[:, t], rs[:, t:t + 1], scale, ALU.mult, ALU.mult)
                    if mod_layer is None:
                        ins.then_inc(normed, 1)
                    else:
                        step(ins)
                        dve.tensor_tensor(yg[:, 0, t], yg[:, 0, t], md[:, 0], ALU.add).then_inc(h_f32, 1)
                        dve.wait_ge(h_hi, t + 1)
                        dve.tensor_tensor(hl[:, t], yg[:, 0, t], f(hh[:, t]), ALU.subtract)


def phase_fourier(nc, a, hh, hl, fh, fl):
    with ExitStack() as ctx:
        sb, sem, banks = alloc(nc, ctx, "fourier")
        raw = sb("raw", [P, 2, NX, SEQ])
        ch, cl = sb("ch", [P, 2, NX, SEQ], F32R), sb("cl", [P, 2, NX, SEQ], F32R)
        gr = sb("gr", [P, 2, 2, FG])
        gh, gl = sb("gh", [P, 2, 2, FG], F32R), sb("gl", [P, 2, 2, FG], F32R)
        uh, ul = sb("uh", [P, 2, 2, SEQ], F32R), sb("ul", [P, 2, 2, SEQ], F32R)
        pU, pF = banks("pU", 4), banks("pF", 4)
        c_in = [sem("cos_in"), sem("sin_in"), sem("chan_in")]
        hi, lo, u_done, u_hi, u_lo = sem("table_hi"), sem("table_lo"), sem("u_done"), sem("u_hi"), sem("u_lo")
        f_done, f_hi, f_lo = sem("f_done"), sem("f_hi"), sem("f_lo")
        tables = [(raw[:, 0], ch[:, 0], cl[:, 0]), (raw[:, 1], ch[:, 1], cl[:, 1]), (gr[:], gh[:], gl[:])]
        NGR = D // FG
        with nc.Block() as block:

            @block.sync
            def _(sp):
                for s in range(2):
                    sp.dma_start(raw[:, s], a["dft_seq"][s].rearrange("(t p) n -> p t n", p=P)).then_inc(c_in[s], 16)
                sp.dma_start(gr[:], a["dft_chan"].rearrange("s (k p) n -> p s k n", p=P)).then_inc(c_in[2], 16)

            @block.tensor
            def _(pe):
                def sequence(g):
                    for d in range(2):
                        col = (g * 2 + d) * P
                        for s in range(2):
                            n = g * 4 + d * 2 + s
                            pe.wait_ge(lo, s + 1)
                            if g:
                                pe.wait_ge(u_lo, n - 3)
                            for t in range(NX):
                                last = three(pe, pU[d * 2 + s][:, :], (hh[:, t, col:col + P], hl[:, t, col:col + P]),
                                             (ch[:, s, t], cl[:, s, t]), t == 0, t == NX - 1)
                            last.then_inc(u_done, 1)

                def channels(g):
                    pe.wait_ge(lo, 3)
                    pe.wait_ge(u_lo, g * 4 + 4)
                    for e in range(2):
                        n = g * 2 + e
                        if n >= 4:
                            pe.wait_ge(f_lo, n - 3)
                        for d in range(2):
                            for s in range(2):
                                last = three(pe, pF[n % 4][:, :],
                                             tuple(m[:, s, d, e * P:(e + 1) * P] for m in (gh, gl)),
                                             (uh[:, d, s], ul[:, d, s]), d + s == 0, d + s == 2)
                        last.then_inc(f_done, 1)

                for g in range(NGR):
                    sequence(g)
                    channels(g)

            @block.scalar
            def _(act):
                for i, (r, h_, l_) in enumerate(tables):
                    act.wait_ge(c_in[i], 16)
                    act.activation(h_, r, ACT.Copy).then_inc(hi, 1)
                for g in range(NGR):
                    for n in range(4):
                        act.wait_ge(u_done, g * 4 + n + 1)
                        if g:
                            act.wait_ge(f_done, g * 2)
                        act.activation(uh[:, n // 2, n % 2], pU[n][:, :], ACT.Copy).then_inc(u_hi, 1)
                    for n in range(g * 2, g * 2 + 2):
                        act.wait_ge(f_done, n + 1)
                        act.activation(fh[:, n], pF[n % 4][:, :], ACT.Copy).then_inc(f_hi, 1)

            @block.vector
            def _(dve):
                for i, (r, h_, l_) in enumerate(tables):
                    dve.wait_ge(hi, i + 1)
                    dve.tensor_tensor(l_, r, f(h_), ALU.subtract).then_inc(lo, 1)
                for g in range(NGR):
                    for n in range(4):
                        dve.wait_ge(u_hi, g * 4 + n + 1)
                        dve.tensor_tensor(ul[:, n // 2, n % 2], pU[n][:, :], f(uh[:, n // 2, n % 2]), ALU.subtract
                                          ).then_inc(u_lo, 1)
                    for n in range(g * 2, g * 2 + 2):
                        dve.wait_ge(f_hi, n + 1)
                        dve.tensor_tensor(fl[:, n], pF[n % 4][:, :], f(fh[:, n]), ALU.subtract).then_inc(f_lo, 1)


def build(nc, a):
    def dram(name, shape):
        return nc.dram_tensor(name, shape, F32, kind="Internal").ap()

    scr = {"mod": dram("mod_scr", (2, 2, NMOD * D)), "strips": dram("strips_scr", (HEADS, P, STRIPS)),
           "gated": dram("gated_scr", (SEQ, HEADS * DV)),
           "xs": dram("xs_scr", ((NBLK + 1) * P, D)), "ys": dram("ys_scr", ((NBLK + 1) * P, D))}
    with ExitStack() as ctx:
        def keep(name, shape, dt=F32):
            return ctx.enter_context(nc.sbuf_tensor(name, shape, dt))

        ident, minus_half = keep("ident", [P, P]), keep("minus_half", [P, 8])
        phase_modulation(nc, a, scr, ident, minus_half)
        with nc.sbuf_tensor("hTh", [P, KT, NTOK * P], F32R) as hTh, nc.sbuf_tensor("hTl", [P, KT, NTOK * P], F32R) as hTl:
            phase_norm_transposed(nc, a, scr, ident, minus_half, hTh, hTl)
            phase_heads(nc, a, scr, ident, minus_half, hTh, hTl)
        res = keep("res", [P, NX, D])
        dest, wk = keep("dest", [P, 2, 2, NX], I32), keep("wk", [P, NX, 2])
        table = keep("table", [P, NBLK + 1], I32)
        KO = HEADS * DV // P
        with nc.sbuf_tensor("gTh", [P, KO, SEQ], F32R) as gTh, nc.sbuf_tensor("gTl", [P, KO, SEQ], F32R) as gTl:
            project_residual(nc, a, scr, "out0", 0, KO, a["ret_w_out"][0].rearrange("(k p) n -> p k n", p=P),
                             (gTh, gTl), a["x"][0], res, ident, scr["gated"])
        phase_route(nc, a, scr, ident, minus_half, 0, res, dest, wk, table)
        phase_experts(nc, a, scr, ident, 0, table)
        with nc.sbuf_tensor("fh", [P, KT, SEQ], F32R) as fh, nc.sbuf_tensor("fl", [P, KT, SEQ], F32R) as fl:
            with nc.sbuf_tensor("h2h", [P, NX, D], F32R) as h2h, nc.sbuf_tensor("h2l", [P, NX, D], F32R) as h2l:
                phase_combine(nc, a, scr, 0, res, dest, wk, minus_half, (a["norm_mix"][1:2, :], 1, h2h, h2l))
                phase_fourier(nc, a, h2h, h2l, fh, fl)
            project_residual(nc, a, scr, "out1", 1, KT, a["fn_w_out"][0].rearrange("(k p) n -> p k n", p=P),
                             (fh, fl), None, res, ident)
        phase_route(nc, a, scr, ident, minus_half, 1, res, dest, wk, table)
        phase_experts(nc, a, scr, ident, 1, table)
        phase_combine(nc, a, scr, 1, res, dest, wk, minus_half,
                      (a["norm_final"].rearrange("(o d) -> o d", o=1), None, None, None))


_INS = ["x", "c", "ctx", "c_ctx", "w_mod", "b_mod", "norm_mix", "norm_ffn", "norm_final", "ret_w_in", "ret_decay",
        "ret_gn", "ret_w_out", "fn_w_out", "router_w", "router_bias", "moe_w_gate", "moe_w_up", "moe_w_down"]


def shape_constants():
    import numpy as np
    p = np.arange(P, dtype=np.float64)[:, None]
    delta = np.arange(XR)[None, :] - XO - p
    w = np.arange(CR)[None, :]
    ahead, behind = w - P + CTX - p, SEQ - (w - P) + p
    distances = np.concatenate([np.maximum(delta, 0), np.maximum(-delta, 0), ahead, behind], 1)
    nf = DK // 4
    inv = (np.float32(10000.0) ** (-np.arange(nf, dtype=np.float32) / np.float32(nf))).astype(np.float32)
    t = np.arange(SEQ)
    ang = np.stack([(t // 64).astype(np.float32)[:, None] * inv, (t % 64).astype(np.float32)[:, None] * inv], 1)
    rope = np.stack([np.cos(ang), np.sin(ang)], 1)
    rope = rope.reshape(NX, P, 2 * 2 * nf).transpose(1, 0, 2)
    a = 2 * np.pi * (np.outer(np.arange(SEQ), np.arange(SEQ)) % SEQ) / SEQ
    g = 2 * np.pi * (np.outer(np.arange(FG), np.arange(FG)) % FG) / FG
    return {
        "identity": np.eye(P), "distances": distances, "rope": rope,
        "dft_seq": np.stack([np.cos(a), np.sin(a)]) / np.sqrt(SEQ),
        "dft_chan": np.stack([np.cos(g), -np.sin(g)]) / np.sqrt(FG),
        "below": np.stack([np.tril(np.ones((P, P)), -1).T, np.ones((P, P))]),
        "order": np.concatenate([NE - np.arange(NE), NG - np.arange(NG), np.arange(MAX_OVER + 1)])[None],
    }


def kernel(**inputs):
    import numpy as _np
    import concourse.bacc as _bacc
    from concourse import mybir as _mybir
    from concourse.bass_utils import run_bass_kernel_spmd as _run

    nc = _bacc.Bacc("TRN2", target_bir_lowering=False, num_devices=1)
    arrays, args = {}, {}
    given = {name: _np.ascontiguousarray(inputs[name]) for name in _INS}
    given.update({k: _np.ascontiguousarray(v, dtype=_np.float32) for k, v in shape_constants().items()})
    for name, arr in given.items():
        arrays[f"in_{name}_dram"] = arr
        args[name] = nc.dram_tensor(f"in_{name}_dram", arr.shape, _mybir.dt.from_np(arr.dtype),
                                    kind="ExternalInput").ap()
    args["out"] = nc.dram_tensor("out_0_dram", (1, SEQ, D), _mybir.dt.float32, kind="ExternalOutput").ap()
    build(nc, args)
    r = _run(nc, [arrays], core_ids=[0])
    return r.results[0]["out_0_dram"]
```

```python
import concourse.bass as bass
from concourse import mybir
from contextlib import ExitStack

F32, F32R = mybir.dt.float32, mybir.dt.float32r
I32, U32 = mybir.dt.int32, mybir.dt.uint32
ALU = mybir.AluOpType
ACT = mybir.ActivationFunctionType
AX = mybir.AxisListType

P = 128
D = 1024
KT = D // P
SEQ, CTX = 512, 256
NX, NC = SEQ // P, CTX // P
NTOK = NX + NC
NMOD = 6
EPS = 1e-6
HEADS, DK, DV = 4, 256, 512
NE, NG, EPG = 16, 4, 4
MAX_OVER = (2 * SEQ) // (P + 1)
NBLK = NE + MAX_OVER
XR = SEQ + 3 * P
XO = SEQ - P
CR = SEQ + P
STRIPS = XR + CR
H = 512
FG = 256
BIG = 1e30


class Count:

    def __init__(self, sem, base=0):
        self.sem, self.n, self.base = sem, 0, base

    def inc(self, ins):
        ins.then_inc(self.sem, 1)
        self.n += 1
        return self.n

    def after(self, eng):
        eng.wait_ge(self.sem, self.base + self.n)


def alloc(nc, ctx, tag):
    def sb(name, shape, dt=F32):
        return ctx.enter_context(nc.sbuf_tensor(f"{tag}_{name}", shape, dt))

    sems = []

    def clear():
        nc.clear_and_free_semaphores(sems)
        nc.all_engine_barrier()

    ctx.callback(clear)

    def sem(name):
        sems.append(nc.alloc_semaphore(f"{tag}_{name}"))
        return sems[-1]

    def banks(name, n):
        return [ctx.enter_context(nc.psum_tensor(f"{tag}_{name}{i}", [P, H], F32)) for i in range(n)]

    return sb, sem, banks


def f(ap):
    return ap.bitcast(F32)


def phase_first(nc, a, scr, ident, minus_half, cT, hTh, hTl):
    SL = 2 * D // H
    NCH = 2 * SL
    EW = 2 * XR + 2 * CR
    with ExitStack() as ctx:
        sb, sem, banks = alloc(nc, ctx, "first")
        crow, csilu = sb("crow", [2 * KT, P]), sb("csilu", [2 * KT, P])
        wm = sb("wm", [P, 4, 4, H])
        brow = sb("brow", [2, 2 * D])
        dist, dl = sb("dist", [P, EW]), sb("dl", [P, 2 * HEADS])
        t = sb("t", [P, 8, 2 * HEADS])
        ex, strip = sb("ex", [P, EW]), sb("strip", [P, STRIPS])
        xt = sb("xt", [P, NTOK, D])
        md, nm, junk = sb("md", [P, 4, D]), sb("nm", [P, D]), sb("junk", [P, D])
        ss, rs = sb("ss", [P, NTOK]), sb("rs", [P, NTOK])
        pm, pc, pT = banks("pm", 2), banks("pc", 1)[0], banks("pT", 4)
        s_c, s_id, s_b, s_dist, s_dl = (sem(n) for n in ("c_in", "id_in", "b_in", "dist_in", "dl_in"))
        w_in = [sem(f"w_in{i}") for i in range(NCH)]
        s_silu, s_cT, s_cTs, half_ok = sem("c_silu"), sem("c_transposed"), sem("cT_ready"), sem("minus_half")
        chunk_used, row_ready, mod_out = sem("chunk_used"), sem("row_ready"), sem("mod_out")
        dv, lg, e_ready, strip_ready = sem("dve_steps"), sem("log_decay"), sem("exps_ready"), sem("strip_ready")
        s_exp, strip_out = sem("exp_abs"), sem("strip_out")
        x_in = [sem(f"x_in{i}") for i in range(NTOK)]
        md_in, nm_in, sq, ms, rs_ready = sem("md_in"), sem("nm_in"), sem("squares"), sem("mean_square"), sem("rs_ready")
        h_ready, tr, hi, lo = sem("h_ready"), sem("transposed"), sem("hi_ready"), sem("lo_ready")
        w_view = a["w_mod"][0].rearrange("(b k p) n -> b p k n", p=P, k=4)
        with nc.Block() as block:

            @block.sync
            def _(sp):
                sp.dma_start(crow[0:KT, :], a["c"].rearrange("o (k p) -> (o k) p", p=P)).then_inc(s_c, 16)
                sp.dma_start(crow[KT:2 * KT, :], a["c_ctx"].rearrange("(k p) -> k p", p=P)).then_inc(s_c, 16)
                sp.dma_start(ident[:], a["identity"]).then_inc(s_id, 16)
                for c in range(NCH):
                    if c >= 4:
                        sp.wait_ge(chunk_used, c - 3)
                    sp.dma_start(wm[:, c % 4], w_view[c % 2, :, :, (c // 2) * H:(c // 2 + 1) * H]).then_inc(w_in[c], 16)
                sp.wait_ge(row_ready, SL)
                sp.dma_start(scr["mod"][0, :, 0:2 * D], brow[:]).then_inc(mod_out, 16)
                sp.wait_ge(mod_out, 16)
                for s in range(2):
                    for v in (1, 0):
                        sp.dma_start(md[:, 2 * s + v, :],
                                     scr["mod"][0, s:s + 1, v * D:(v + 1) * D].to_broadcast([P, D])).then_inc(md_in, 16)

            @block.tensor
            def _(pe):
                pe.wait_ge(s_id, 16)
                pe.wait_ge(s_silu, 1)
                pe.transpose(pc[:, 0:2 * KT], csilu[:], ident[0:2 * KT, 0:2 * KT]).then_inc(s_cT, 1)
                pe.wait_ge(s_cTs, 1)
                for c in range(NCH):
                    sl = c // 2
                    if c % 2 == 0 and sl >= 2:
                        pe.wait_ge(row_ready, sl - 1)
                    pe.wait_ge(w_in[c], 16)
                    for k in range(4):
                        kk = (c % 2) * 4 + k
                        mm = pe.matmul(pm[sl % 2][0:2, :], cT[:, kk:kk + KT + 1:KT], wm[:, c % 4, k, :],
                                       start=kk == 0, stop=kk == KT - 1)
                    mm.then_inc(chunk_used, 1)
                for tb in range(NTOK):
                    pe.wait_ge(h_ready, tb + 1)
                    for half in range(2):
                        n = 2 * tb + half
                        if n >= 4:
                            pe.wait_ge(lo, n - 3)
                        for k in range(4):
                            ins = pe.transpose(pT[n % 4][:, k * P:(k + 1) * P],
                                               xt[:, tb, (4 * half + k) * P:(4 * half + k + 1) * P], ident[:])
                        ins.then_inc(tr, 1)

            @block.scalar
            def _(act):
                act.dma_start(brow[0:1, :], a["b_mod"][0:1, 0:2 * D]).then_inc(s_b, 16)
                act.dma_start(brow[1:2, :], a["b_mod"][0:1, 0:2 * D]).then_inc(s_b, 16)
                for tb in range(NTOK):
                    src = (a["x"][0, tb * P:(tb + 1) * P, :] if tb < NX
                           else a["ctx"][0, (tb - NX) * P:(tb - NX + 1) * P, :])
                    act.dma_start(xt[:, tb, :], src).then_inc(x_in[tb], 16)
                act.dma_start(nm[:], a["norm_mix"][0:1, :].to_broadcast([P, D])).then_inc(nm_in, 16)
                act.dma_start(dist[:], a["distances"]).then_inc(s_dist, 16)
                act.wait_ge(s_c, 32)
                act.activation(csilu[:], crow[:], ACT.Silu).then_inc(s_silu, 1)
                act.wait_ge(s_cT, 1)
                act.activation(cT[:], pc[:, 0:2 * KT], ACT.Copy).then_inc(s_cTs, 1)
                for tb in range(NTOK):
                    act.wait_ge(x_in[tb], 16)
                    if tb:
                        act.wait_ge(sq, tb)
                    act.activation(junk[:], xt[:, tb, :], ACT.Square, accum_out=ss[:, tb:tb + 1]).then_inc(sq, 1)
                act.wait_ge(dv, 2)
                act.activation(t[:, 1, :], t[:, 0, :], ACT.Exp, scale=-1.0).then_inc(s_exp, 1)
                act.wait_ge(lg, 1)
                act.wait_ge(s_dist, 16)

                def exps(h):
                    if h:
                        act.wait_ge(strip_ready, h)
                    fwd, bwd = t[:, 7, h:h + 1], t[:, 7, HEADS + h:HEADS + h + 1]
                    act.activation(ex[:, 0:XR], dist[:, 0:XR], ACT.Exp, scale=fwd)
                    act.activation(ex[:, XR:2 * XR], dist[:, XR:2 * XR], ACT.Exp, scale=bwd)
                    act.activation(ex[:, 2 * XR:2 * XR + CR], dist[:, 2 * XR:2 * XR + CR], ACT.Exp, scale=fwd)
                    act.activation(ex[:, 2 * XR + CR:], dist[:, 2 * XR + CR:], ACT.Exp, scale=bwd).then_inc(e_ready, 1)

                for h in range(HEADS):
                    exps(h)
                for tb in range(NTOK):
                    for half in range(2):
                        n = 2 * tb + half
                        act.wait_ge(tr, n + 1)
                        act.activation(hTh[:, 4 * half:4 * half + 4, tb * P:(tb + 1) * P],
                                       pT[n % 4][:, :].rearrange("p (k c) -> p k c", k=4), ACT.Copy).then_inc(hi, 1)

            @block.gpsimd
            def _(pool):
                pool.dma_start(dl[:], a["ret_decay"].rearrange("o a h -> o (a h)").to_broadcast([P, 2 * HEADS])
                               ).then_inc(s_dl, 16)
                pool.memset(minus_half[:], -0.5).then_inc(half_ok, 1)
                pool.wait_ge(half_ok, 1)
                pool.wait_ge(ms, 1)
                pool.tensor_tensor(rs[:], ss[:], minus_half[:, 0:NTOK], ALU.pow).then_inc(rs_ready, 1)
                for h in range(HEADS):
                    pool.wait_ge(strip_ready, h + 1)
                    pool.dma_start(scr["strips"][h], strip[:]).then_inc(strip_out, 16)
                    pool.wait_ge(strip_out, 16 * h + 16)

            @block.vector
            def _(dve):
                own = Count(dv)

                def step(ins):
                    own.inc(ins)
                    own.after(dve)

                dve.wait_ge(s_dl, 16)
                step(dve.tensor_scalar(t[:, 2, :], dl[:], -1.0, None, ALU.mult))
                step(dve.tensor_tensor(t[:, 0, :], dl[:], t[:, 2, :], ALU.max))
                dve.wait_ge(s_exp, 1)
                step(dve.tensor_scalar(t[:, 2, :], t[:, 1, :], 2.0, None, ALU.add))
                step(dve.reciprocal(t[:, 3, :], t[:, 2, :]))
                step(dve.tensor_tensor(t[:, 3, :], t[:, 1, :], t[:, 3, :], ALU.mult))
                step(dve.tensor_tensor(t[:, 4, :], t[:, 3, :], t[:, 3, :], ALU.mult))
                step(dve.memset(t[:, 5, :], 2.0 / 17))
                for n in (15, 13, 11, 9, 7, 5, 3, 1):
                    step(dve.tensor_tensor(t[:, 6, :], t[:, 5, :], t[:, 4, :], ALU.mult))
                    step(dve.tensor_scalar(t[:, 5, :], t[:, 6, :], 2.0 / n, None, ALU.add))
                step(dve.tensor_tensor(t[:, 6, :], t[:, 5, :], t[:, 3, :], ALU.mult))
                step(dve.tensor_scalar(t[:, 2, :], dl[:], 0.0, None, ALU.min))
                dve.tensor_tensor(t[:, 7, :], t[:, 2, :], t[:, 6, :], ALU.subtract).then_inc(lg, 1)
                dve.wait_ge(sq, NTOK)
                dve.tensor_scalar(ss[:], ss[:], 1.0 / D, EPS, ALU.mult, ALU.add).then_inc(ms, 1)
                dve.wait_ge(s_b, 32)

                def row(sl):
                    dve.wait_ge(chunk_used, (sl + 1) * 2)
                    dve.tensor_tensor(brow[:, sl * H:(sl + 1) * H], pm[sl % 2][0:2, :], brow[:, sl * H:(sl + 1) * H],
                                      ALU.add).then_inc(row_ready, 1)

                def strips(h):
                    dve.wait_ge(e_ready, h + 1)
                    if h:
                        dve.wait_ge(strip_out, 16 * h)
                    step(dve.scalar_tensor_tensor(ex[:, 0:XR], dist[:, XR:2 * XR], 0.0, ex[:, 0:XR],
                                                  ALU.is_le, ALU.mult))
                    step(dve.scalar_tensor_tensor(ex[:, XR:2 * XR], dist[:, 0:XR], 0.0, ex[:, XR:2 * XR],
                                                  ALU.is_le, ALU.mult))
                    step(dve.tensor_tensor(strip[:, 0:XR], ex[:, 0:XR], ex[:, XR:2 * XR], ALU.add))
                    dve.tensor_tensor(strip[:, XR:], ex[:, 2 * XR:2 * XR + CR], ex[:, 2 * XR + CR:],
                                      ALU.add).then_inc(strip_ready, 1)

                for sl in range(SL):
                    row(sl)
                    strips(sl)
                dve.wait_ge(md_in, 16 * 4)
                dve.wait_ge(nm_in, 16)
                for s in range(2):
                    own.inc(dve.scalar_tensor_tensor(md[:, 2 * s + 1, :], md[:, 2 * s + 1, :], 1.0, nm[:],
                                                     ALU.add, ALU.mult))
                own.after(dve)
                dve.wait_ge(rs_ready, 1)

                def modulate(tb):
                    s = tb // NX
                    own.inc(dve.scalar_tensor_tensor(xt[:, tb, :], xt[:, tb, :], rs[:, tb:tb + 1], md[:, 2 * s + 1, :],
                                                     ALU.mult, ALU.mult))
                    own.after(dve)
                    dve.tensor_tensor(xt[:, tb, :], xt[:, tb, :], md[:, 2 * s, :], ALU.add).then_inc(h_ready, 1)

                modulate(0)
                for tb in range(NTOK):
                    if tb + 1 < NTOK:
                        modulate(tb + 1)
                    for half in range(2):
                        n = 2 * tb + half
                        dve.wait_ge(hi, n + 1)
                        dst = slice(4 * half, 4 * half + 4)
                        dve.tensor_tensor(hTl[:, dst, tb * P:(tb + 1) * P],
                                          pT[n % 4][:, :].rearrange("p (k c) -> p k c", k=4),
                                          f(hTh[:, dst, tb * P:(tb + 1) * P]), ALU.subtract).then_inc(lo, 1)


def three(pe, out, lhs, rhs, start, stop):
    pe.matmul(out, lhs[0], rhs[0], start=start, stop=False)
    pe.matmul(out, lhs[0], rhs[1], start=False, stop=False)
    return pe.matmul(out, lhs[1], rhs[0], start=False, stop=stop)


def phase_heads(nc, a, scr, ident, minus_half, cT, hTh, hTl):
    CPS = 4
    NCH = 3 * CPS
    NSL = 2 * NTOK + NX
    MH = 5
    ITEMS = []
    for c in range(CPS, NCH + CPS):
        ITEMS.append(("w", c, 0))
        if c < CPS + MH:
            ITEMS += [("m", c - CPS, q) for q in range(4)]
    NIT = len(ITEMS)
    RING = 4
    assert NIT % RING == 0 and CPS == RING
    at_item = {it: r for r, it in enumerate(ITEMS)}
    arrivals, seen = {}, [2] * RING
    for r, it in enumerate(ITEMS):
        seen[r % RING] += 2 if it[0] == "w" and it[1] >= NCH else 1
        arrivals[it] = seen[r % RING]
    per_turn = [n - 2 for n in seen]
    with ExitStack() as ctx:
        sb, sem, banks = alloc(nc, ctx, "heads")
        raw = sb("raw", [P, RING, 2, H])
        wh, wl = sb("wh", [P, RING, 2, H], F32R), sb("wl", [P, RING, 2, H], F32R)
        rope = sb("rope", [P, NX, 2, 2, DK // 4])
        rt = sb("rt", [P, 2, 4, 2, 2, DK // 4])
        qk = sb("qk", [P, NX, 2, 2, 2, DK // 4])
        kc = sb("kc", [P, NC, DK])
        qh, ql = sb("qh", [P, 2, SEQ], F32R), sb("ql", [P, 2, SEQ], F32R)
        kh, kl = sb("kh", [P, 2, NTOK * P], F32R), sb("kl", [P, 2, NTOK * P], F32R)
        vh, vl = sb("vh", [P, NTOK, DV], F32R), sb("vl", [P, NTOK, DV], F32R)
        gs, gn = sb("gs", [P, NX, DV]), sb("gn", [P, DV])
        strip = sb("strip", [P, STRIPS])
        af = sb("af", [P, 2, SEQ])
        ah, al = sb("ah", [P, 2, SEQ], F32R), sb("al", [P, 2, SEQ], F32R)
        og = sb("og", [P, NX, DV])
        bst, mv, pad = sb("bst", [P, NX, 6]), sb("mv", [P, NX, 4]), sb("pad", [1, 1])
        macc, mbias, mout = sb("macc", [P, 2, H]), sb("mbias", [P, H]), sb("mout", [1, H])
        ones, zero = sb("ones", [P, 1]), sb("zero", [P, D // 8])
        pj, pS = banks("pj", NTOK), banks("pS", 2)
        raw_in = [sem(f"raw_in{i}") for i in range(RING)]
        rope_in, strip_in, gn_in, set_ok = sem("rope_in"), sem("strip_in"), sem("gn_in"), sem("constants_set")
        hi, consumed, chunk_used, proj = sem("w_hi"), sem("raw_consumed"), sem("chunk_used"), sem("projected")
        rope_read, kc_read, rotated = sem("rope_read"), sem("ctx_key_read"), sem("rotated")
        v_hi, v_lo, g_read, g_ready = sem("v_hi"), sem("v_lo"), sem("gate_read"), sem("gate_ready")
        qkt, qkt_hi, qkt_lo = sem("qk_transposed"), sem("qkT_hi"), sem("qkT_lo")
        s_done, a_f, a_hi, a_lo = sem("scores_done"), sem("att_f32"), sem("att_hi"), sem("att_lo")
        av, o_done, o_read, ms, rstd = sem("av_done"), sem("o_done"), sem("o_read"), sem("o_var"), sem("o_rstd")
        normed, gated, dv, zero_out = sem("o_normed"), sem("gated"), sem("dve_steps"), sem("zero_out")
        bias_in, m_first, m_sum, m_row, m_out = (sem(n) for n in ("mod_bias_in", "mod_first", "mod_summed", "mod_row", "mod_out"))
        row_free, pool_pad = sem("mod_row_free"), sb("pool_pad", [1, 1])
        m_acc, m_step = sem("mod_accumulated"), sem("mod_steps")
        g_out = [sem(f"gated_out{i}") for i in range(NX)]
        w1 = a["ret_w_in"].rearrange("o (k p) n -> p (o k) n", p=P)
        wm = [a["w_mod"][lay].rearrange("(k p) n -> p k n", p=P) for lay in range(2)]
        xs_rows, ys_rows = (scr[n].rearrange("(b p) (q d) -> b p q d", p=P, q=8) for n in ("xs", "ys"))

        b_mod = a["b_mod"].rearrange("(o l) n -> o (l n)", o=1)

        def mod_at(h, v):
            return (0, h * (2 * H) + (2 * D + v * H)) if v < 2 else (1, h * (3 * H) + (v - 2) * H)

        with nc.Block() as block:

            @block.sync
            def _(sp):
                def load_w(h, c, slot):
                    s, cc = c % NCH // CPS, c % CPS
                    if s == 0:
                        for part in range(2):
                            sp.dma_start(raw[:, slot, :, part * DK:(part + 1) * DK],
                                         w1[:, 2 * cc:2 * cc + 2, bass.ds(h * DK + (c // NCH) * DK + part * D, DK)]
                                         ).then_inc(raw_in[slot], 16)
                    else:
                        sp.dma_start(raw[:, slot], w1[:, 2 * cc:2 * cc + 2, bass.ds(h * DV + 2 * s * D, DV)]
                                     ).then_inc(raw_in[slot], 16)

                for c in range(CPS):
                    load_w(0, c, c)
                sp.dma_start(rope[:], a["rope"].rearrange("p t (a b c) -> p t a b c", a=2, b=2)).then_inc(rope_in, 16)
                sp.wait_ge(set_ok, 1)
                sp.dma_start(mbias[0:1, :], a["b_mod"][0:1, 2 * D:2 * D + H]).then_inc(bias_in, 16)
                with sp.Fori(0, HEADS) as h:
                    for r, it in enumerate(ITEMS):
                        sp.wait_ge(consumed, h * NIT + r + 1)
                        if it[0] == "w":
                            load_w(h, it[1], r % RING)
                        else:
                            lay, col = mod_at(h, it[1])
                            sp.dma_start(raw[:, r % RING], wm[lay][:, 2 * it[2]:2 * it[2] + 2, bass.ds(col, H)]
                                         ).then_inc(raw_in[r % RING], 16)
                            if it[2] == 2:
                                lay, col = mod_at(h, it[1] + 1) if it[1] + 1 < MH else mod_at(h + 1, 0)
                                sp.wait_ge(m_first, h * MH + it[1] + 1)
                                sp.dma_start(mbias[0:1, :], b_mod[:, bass.ds(lay * NMOD * D + col, H)]
                                             ).then_inc(bias_in, 16)
                        if it == ("w", 9, 0):
                            sp.wait_ge(g_ready, h * NX + 1)
                            sp.wait_ge(a_lo, h * NTOK + 1)
                            sp.dma_start(strip[:], scr["strips"][bass.ds(h, 1)].rearrange("o p w -> (o p) w")
                                         ).then_inc(strip_in, 16)
                            sp.dma_start(gn[:], a["ret_gn"][0:1, bass.ds(h * DV, DV)].to_broadcast([P, DV])
                                         ).then_inc(gn_in, 16)
                sp.wait_ge(bias_in, 16 * (HEADS * MH + 1))

            @block.tensor
            def _(pe):
                with pe.Fori(0, HEADS) as h:

                    def transpose_qk(t):
                        if t < NX:
                            pe.wait_ge(rotated, h * NX + t + 1)
                        else:
                            pe.wait_ge(kc_read, h * NC + t - NX + 1)
                        if t >= 2:
                            pe.wait_ge(qkt_lo, h * NTOK + t - 1)
                        for i in range(0 if t < NX else 2, 4):
                            src = (qk[:, t, i // 2, i % 2].rearrange("p b c -> p (b c)") if t < NX
                                   else kc[:, t - NX, (i - 2) * P:(i - 1) * P])
                            last = pe.transpose(pS[t % 2][:, i * P:(i + 1) * P], src, ident[:])
                        last.then_inc(qkt, 1)

                    def sum_mod(v):
                        if v >= 2:
                            pe.wait_ge(m_row, h * MH + v - 1)
                        pe.wait_ge(m_acc, h * MH + v + 1)
                        pe.matmul(pS[v % 2][0:1, :], ones[:], macc[:, v % 2], start=True, stop=True).then_inc(m_sum, 1)

                    for c in range(NCH):
                        s, cc = c // CPS, c % CPS
                        if c < CPS:
                            pe.wait_ge(consumed, h * NIT + c + 1)
                        else:
                            pe.wait_ge(consumed, h * NIT + RING + at_item["w", c, 0] + 1)
                        for t in range(NX if s == 2 else NTOK):
                            if cc == 0:
                                if s == 0 and t < NX:
                                    pe.wait_ge(o_read, h * NX + t + 1)
                                elif s == 1 and t < NX:
                                    pe.wait_ge(rope_read, h * NX + t + 1)
                                elif s == 1:
                                    pe.wait_ge(kc_read, h * NC + t - NX + 1)
                                elif s == 2:
                                    pe.wait_ge(v_lo, h * NTOK + t + 1)
                            c0 = DK if s == 0 and t >= NX else 0
                            for k in range(2):
                                kk = 2 * cc + k
                                last = three(pe, pj[t][:, c0:H],
                                             (hTh[:, kk, t * P:(t + 1) * P], hTl[:, kk, t * P:(t + 1) * P]),
                                             (wh[:, cc, k, c0:H], wl[:, cc, k, c0:H]),
                                             kk == 0, kk == KT - 1)
                            if cc == CPS - 1:
                                last.then_inc(proj, 1)
                        if cc < CPS - 1:
                            last.then_inc(chunk_used, 1)
                        if c in (2, 3, 4, 6, 7):
                            sum_mod({2: 0, 3: 1, 4: 2, 6: 3, 7: 4}[c])
                        if c == 8:
                            pe.wait_ge(m_row, h * MH + MH)
                        if 8 <= c < 11:
                            transpose_qk(2 * (c - 8))
                            transpose_qk(2 * (c - 8) + 1)
                    pe.wait_ge(qkt_lo, h * NTOK + NTOK)
                    pe.wait_ge(v_lo, h * NTOK + NTOK)

                    def scores(j):
                        for kk in range(2):
                            last = three(pe, pS[j % 2][:, :],
                                         tuple(m[:, kk, j * P:(j + 1) * P] for m in (kh, kl)),
                                         tuple(m[:, kk] for m in (qh, ql)), kk == 0, kk == 1)
                        last.then_inc(s_done, 1)

                    def weighted(j):
                        pe.wait_ge(a_lo, h * NTOK + j + 2)
                        for i in range(NX):
                            if j == 0:
                                pe.wait_ge(g_read, h * NX + i + 1)
                            last = three(pe, pj[i][:, :], tuple(m[:, j % 2, i * P:(i + 1) * P] for m in (ah, al)),
                                         (vh[:, j], vl[:, j]), j == 0, j == NTOK - 1)
                            if j == NTOK - 1:
                                last.then_inc(o_done, 1)
                        if j < NTOK - 1:
                            last.then_inc(av, 1)

                    scores(0)
                    for j in range(1, NTOK):
                        scores(j)
                        weighted(j - 1)
                    weighted(NTOK - 1)

            def split_hi(act, h, c):
                s, cc = c // CPS, c % CPS
                if c < CPS:
                    act.wait_ge(raw_in[cc], 32)
                else:
                    it = ("w", c, 0)
                    slot = at_item[it] % RING
                    act.wait_ge(raw_in[slot], h * (16 * per_turn[slot]) + 16 * arrivals[it])
                    if cc < CPS - 1:
                        act.wait_ge(chunk_used, h * (NCH - 3) + (s - 1) * (CPS - 1) + cc + 1)
                    else:
                        act.wait_ge(proj, h * NSL + (NTOK, 2 * NTOK, NSL)[s - 1])
                slot = cc if c < CPS else at_item["w", c, 0] % RING
                act.activation(wh[:, cc], raw[:, slot], ACT.Copy).then_inc(hi, 1)

            @block.scalar
            def _(act):
                for s in g_out:
                    act.nop().then_inc(s, 1)
                for c in range(CPS):
                    split_hi(act, 0, c)
                with act.Fori(0, HEADS) as h:

                    def qkT_hi(t):
                        act.wait_ge(qkt, h * NTOK + t + 1)
                        cols = slice(t * P, (t + 1) * P)
                        if t < NX:
                            act.activation(qh[:, :, cols], pS[t % 2][:, 0:2 * P].rearrange("p (i c) -> p i c", c=P),
                                           ACT.Copy)
                        act.activation(kh[:, :, cols], pS[t % 2][:, 2 * P:].rearrange("p (i c) -> p i c", c=P),
                                       ACT.Copy).then_inc(qkt_hi, 1)

                    def att_hi(j):
                        act.wait_ge(a_f, h * NTOK + j + 1)
                        if j >= 2:
                            act.wait_ge(av, h * (NTOK - 1) + j - 1)
                        act.activation(ah[:, j % 2], af[:, j % 2], ACT.Copy).then_inc(a_hi, 1)

                    for c in (4, 5, 6):
                        split_hi(act, h, c)
                    for t in range(NX, NTOK):
                        act.wait_ge(proj, h * NSL + t + 1)
                        act.activation(kc[:, t - NX], pj[t][:, DK:H], ACT.Copy).then_inc(kc_read, 1)
                    for c in (7, 8, 9, 10):
                        split_hi(act, h, c)
                    for t in range(NTOK):
                        act.wait_ge(proj, h * NSL + NTOK + t + 1)
                        act.activation(vh[:, t], pj[t][:, :], ACT.Copy).then_inc(v_hi, 1)
                    for n, c in enumerate((11, 12, 13)):
                        split_hi(act, h, c)
                        qkT_hi(2 * n)
                        qkT_hi(2 * n + 1)
                    split_hi(act, h, 14)
                    for t in range(NX):
                        act.wait_ge(proj, h * NSL + 2 * NTOK + t + 1)
                        act.activation(gs[:, t], pj[t][:, :], ACT.Silu).then_inc(g_read, 1)
                    att_hi(0)
                    split_hi(act, h, 15)
                    for j in range(1, NTOK):
                        att_hi(j)
                    for i in range(NX):
                        act.wait_ge(g_out[i], h * 16 + 1)
                        act.wait_ge(o_done, h * NX + i + 1)
                        act.activation(og[:, i], pj[i][:, :], ACT.Copy).then_inc(o_read, 1)
                    for i in range(NX):
                        act.wait_ge(gated, h * NX + i + 1)
                        act.dma_start(scr["gated"][i * P:(i + 1) * P, bass.ds(h * DV, DV)], og[:, i]
                                      ).then_inc(g_out[i], 16)
                for s in g_out:
                    act.wait_ge(s, 16 * HEADS + 1)

            @block.gpsimd
            def _(pool):
                pool.memset(ones[:], 1.0)
                pool.memset(zero[:], 0.0)
                pool.memset(mbias[:], 0.0).then_inc(set_ok, 1)
                pool.nop().then_inc(g_ready, 1)
                pool.nop().then_inc(row_free, 1)
                pool.wait_ge(set_ok, 1)
                src = zero[:].rearrange("p (q d) -> p q d", q=1).to_broadcast([P, 8, D // 8])
                for b in range(NBLK + 1):
                    pool.dma_start(xs_rows[b], src).then_inc(zero_out, 16)
                for b in range(NE + 1, NBLK + 1):
                    pool.dma_start(ys_rows[b], src).then_inc(zero_out, 16)
                with pool.Fori(0, HEADS) as h:

                    def store_mod(v):
                        pool.wait_ge(m_row, h * MH + v + 1)
                        lay, col = mod_at(h, v)
                        pool.dma_start(scr["mod"][lay, 0:1, bass.ds(col, H)], mout[:]).then_inc(m_out, 16)
                        pool.wait_ge(m_out, h * (16 * MH) + 16 * v + 16)
                        pool.tensor_tensor(pool_pad[:], ones[0:1, :], ones[0:1, :], ALU.mult).then_inc(row_free, 1)

                    store_mod(0)
                    for t in range(NX):
                        pool.wait_ge(rope_read, h * NX + t + 1)
                        m = rt[:, t % 2]
                        pool.tensor_tensor(qk[:, t, :, :, 0], m[:, 0], m[:, 1], ALU.subtract)
                        pool.tensor_tensor(qk[:, t, :, :, 1], m[:, 2], m[:, 3], ALU.add).then_inc(rotated, 1)
                    for v in range(1, MH):
                        store_mod(v)
                    pool.wait_ge(gn_in, h * 16 + 16)
                    for t in range(NX):
                        pool.wait_ge(g_read, h * NX + t + 1)
                        pool.tensor_tensor(gs[:, t], gs[:, t], gn[:], ALU.mult).then_inc(g_ready, 1)
                    for i in range(NX):
                        pool.wait_ge(ms, h * NX + i + 1)
                        pool.tensor_tensor(mv[:, i, 3:4], mv[:, i, 2:3], minus_half[:, 0:1], ALU.pow
                                           ).then_inc(rstd, 1)
                pool.wait_ge(zero_out, 16 * (NBLK + 1 + MAX_OVER))
                pool.wait_ge(m_out, 16 * HEADS * MH)

            @block.vector
            def _(dve):
                def split_lo(h, c):
                    dve.wait_ge(hi, h * NCH + c + 1)
                    slot = c if c < CPS else at_item["w", c, 0] % RING
                    dve.tensor_tensor(wl[:, c % CPS], raw[:, slot], f(wh[:, c % CPS]), ALU.subtract
                                      ).then_inc(consumed, 1)

                dve.nop().then_inc(o_read, NX)
                dve.nop().then_inc(a_lo, 1)
                for c in range(CPS):
                    split_lo(0, c)
                dve.wait_ge(rope_in, 16)
                with dve.Fori(0, HEADS) as h:

                    def weigh_mod(v):
                        dve.wait_ge(bias_in, h * (16 * MH) + 16 * v + 16)
                        steps = 0
                        for k in range(KT):
                            it = ("m", v, k // 2)
                            slot = at_item[it] % RING
                            if k % 2 == 0:
                                dve.wait_ge(raw_in[slot], h * (16 * per_turn[slot]) + 16 * arrivals[it])
                            if k == 0:
                                if v >= 2:
                                    dve.wait_ge(m_sum, h * MH + v - 1)
                            elif k == 1:
                                dve.wait_ge(m_first, h * MH + v + 1)
                            elif k % 2:
                                dve.wait_ge(m_step, h * (3 * MH) + v * 3 + k // 2)
                            else:
                                dve.wait_ge(consumed, h * NIT + RING + at_item[it])
                            ins = dve.scalar_tensor_tensor(macc[:, v % 2], raw[:, slot, k % 2], cT[:, k:k + 1],
                                                           mbias[:] if k == 0 else macc[:, v % 2], ALU.mult, ALU.add)
                            if k == 0:
                                ins.then_inc(m_first, 1)
                            elif k % 2 == 0:
                                ins.then_inc(m_step, 1)
                            elif k < KT - 1:
                                ins.then_inc(consumed, 1)
                            else:
                                ins.then_inc(m_acc, 1)
                        dve.wait_ge(m_acc, h * MH + v + 1)
                        dve.memset(pad[:], 0.0).then_inc(consumed, 1)

                    def row_mod(v):
                        dve.wait_ge(m_sum, h * MH + v + 1)
                        dve.wait_ge(row_free, h * MH + v + 1)
                        dve.tensor_copy(mout[:], pS[v % 2][0:1, :]).then_inc(m_row, 1)

                    def rotate(t):
                        dve.wait_ge(proj, h * NSL + t + 1)
                        if t >= 2:
                            dve.wait_ge(rotated, h * NX + t - 1)
                        m = rt[:, t % 2]
                        src = pj[t][:, :].rearrange("p (q s b c) -> p q s b c", q=2, s=2, b=2)
                        cos = rope[:, t, 0:1].to_broadcast([P, 2, 2, DK // 4])
                        sin = rope[:, t, 1:2].to_broadcast([P, 2, 2, DK // 4])
                        dve.tensor_tensor(m[:, 0], src[:, :, :, 0], cos, ALU.mult)
                        dve.tensor_tensor(m[:, 1], src[:, :, :, 1], sin, ALU.mult)
                        dve.tensor_tensor(m[:, 2], src[:, :, :, 0], sin, ALU.mult)
                        dve.tensor_tensor(m[:, 3], src[:, :, :, 1], cos, ALU.mult).then_inc(rope_read, 1)

                    def qkT_lo(t):
                        dve.wait_ge(qkt_hi, h * NTOK + t + 1)
                        cols = slice(t * P, (t + 1) * P)
                        if t < NX:
                            dve.tensor_tensor(ql[:, :, cols], pS[t % 2][:, 0:2 * P].rearrange("p (i c) -> p i c", c=P),
                                              f(qh[:, :, cols]), ALU.subtract)
                        dve.tensor_tensor(kl[:, :, cols], pS[t % 2][:, 2 * P:].rearrange("p (i c) -> p i c", c=P),
                                          f(kh[:, :, cols]), ALU.subtract).then_inc(qkt_lo, 1)

                    def att(j):
                        at = XO - j * P if j < NX else XR + P - (j - NX) * P
                        dve.wait_ge(s_done, h * NTOK + j + 1)
                        dve.scalar_tensor_tensor(af[:, j % 2], pS[j % 2][:, :], DK ** -0.5, strip[:, at:at + SEQ],
                                                 ALU.mult, ALU.mult).then_inc(a_f, 1)
                        dve.wait_ge(a_hi, h * NTOK + j + 1)
                        dve.tensor_tensor(al[:, j % 2], af[:, j % 2], f(ah[:, j % 2]), ALU.subtract
                                          ).then_inc(a_lo, 1)

                    split_lo(h, 4)
                    weigh_mod(0)
                    split_lo(h, 5)
                    weigh_mod(1)
                    row_mod(0)
                    split_lo(h, 6)
                    weigh_mod(2)
                    for t in range(NX):
                        rotate(t)
                    row_mod(1)
                    split_lo(h, 7)
                    weigh_mod(3)
                    row_mod(2)
                    split_lo(h, 8)
                    weigh_mod(4)
                    split_lo(h, 9)
                    split_lo(h, 10)
                    row_mod(3)
                    row_mod(4)
                    for t in range(NTOK):
                        dve.wait_ge(v_hi, h * NTOK + t + 1)
                        dve.tensor_tensor(vl[:, t], pj[t][:, :], f(vh[:, t]), ALU.subtract).then_inc(v_lo, 1)
                    for n, c in enumerate((11, 12, 13)):
                        split_lo(h, c)
                        qkT_lo(2 * n)
                        qkT_lo(2 * n + 1)
                    split_lo(h, 14)
                    dve.wait_ge(strip_in, h * 16 + 16)
                    att(0)
                    split_lo(h, 15)
                    for j in range(1, NTOK):
                        att(j)
                    for i in range(NX):
                        dve.wait_ge(o_read, h * NX + NX + i + 1)
                        dve.bn_stats(bst[:, i], og[:, i]).then_inc(dv, 1)
                    dve.wait_ge(dv, h * (2 * NX) + NX)
                    dve.memset(pad[:], 0.0)
                    for i in range(NX):
                        dve.bn_aggr(mv[:, i, 0:2], bst[:, i]).then_inc(dv, 1)
                    for i in range(NX):
                        dve.wait_ge(dv, h * (2 * NX) + NX + i + 1)
                        dve.tensor_scalar(mv[:, i, 2:3], mv[:, i, 1:2], EPS, None, ALU.add).then_inc(ms, 1)
                    dve.wait_ge(g_ready, h * NX + NX + 1)
                    for i in range(NX):
                        dve.wait_ge(rstd, h * NX + i + 1)
                        dve.tensor_scalar(og[:, i], og[:, i], mv[:, i, 0:1], mv[:, i, 3:4],
                                          ALU.subtract, ALU.mult).then_inc(normed, 1)
                    for i in range(NX):
                        dve.wait_ge(normed, h * NX + i + 1)
                        dve.tensor_tensor(og[:, i], og[:, i], gs[:, i], ALU.mult).then_inc(gated, 1)


def project_residual(nc, a, scr, tag, layer, kt, w_view, gT, x_src, res, ident, gated=None):
    RING = 4
    with ExitStack() as ctx:
        sb, sem, banks = alloc(nc, ctx, tag)
        raw = sb("raw", [P, RING, D])
        wh, wl = sb("wh", [P, RING, D], F32R), sb("wl", [P, RING, D], F32R)
        gate = sb("gate", [P, D])
        xin = sb("xin", [P, NX, D]) if x_src is not None else None
        rows = sb("rows", [P, NX, kt * P]) if gated is not None else None
        acc = banks("acc", 2 * NX)
        raw_in = [sem(f"raw_in{i}") for i in range(RING)]
        rows_in = [sem(f"rows_in{t}") for t in range(NX)]
        gate_in, x_in = sem("gate_in"), sem("x_in")
        tr, g_hi, g_lo = sem("transposed"), sem("g_hi"), sem("g_lo")
        hi, lo, used, done, dv = sem("w_hi"), sem("w_lo"), sem("chunk_used"), sem("acc_done"), sem("dve_steps")
        groups = NX * kt // 4 if gated is not None else 0
        with nc.Block() as block:

            @block.sync
            def _(sp):
                if gated is not None:
                    for t in range(NX):
                        sp.dma_start(rows[:, t], gated[t * P:(t + 1) * P, :]).then_inc(rows_in[t], 16)
                for k in range(kt):
                    if k >= RING:
                        sp.wait_ge(lo, k - RING + 1)
                    sp.dma_start(raw[:, k % RING], w_view[:, k, :]).then_inc(raw_in[k % RING], 16)
                    if k == 3:
                        sp.dma_start(gate[:], scr["mod"][layer, 0:1, 2 * D:3 * D].to_broadcast([P, D])
                                     ).then_inc(gate_in, 16)
                        if xin is not None:
                            sp.dma_start(xin[:], x_src.rearrange("(t p) d -> p t d", p=P)).then_inc(x_in, 16)

            @block.tensor
            def _(pe):
                for n in range(groups):
                    t, q = n // (kt // 4), n % (kt // 4)
                    if q == 0:
                        pe.wait_ge(rows_in[t], 16)
                    if n >= 2 * NX:
                        pe.wait_ge(g_lo, n - 2 * NX + 1)
                    for k in range(4):
                        last = pe.transpose(acc[n % (2 * NX)][:, k * P:(k + 1) * P],
                                            rows[:, t, (4 * q + k) * P:(4 * q + k + 1) * P], ident[:])
                    last.then_inc(tr, 1)
                if groups:
                    pe.wait_ge(g_lo, groups)
                for k in range(kt):
                    pe.wait_ge(lo, k + 1)
                    for t in range(NX):
                        for half in range(2):
                            cols = slice(half * H, (half + 1) * H)
                            last = three(pe, acc[2 * t + half][:, :], tuple(m[:, k, t * P:(t + 1) * P] for m in gT),
                                         (wh[:, k % RING, cols], wl[:, k % RING, cols]), k == 0, k == kt - 1)
                            if k == kt - 1:
                                last.then_inc(done, 1)
                    if k < kt - 1:
                        last.then_inc(used, 1)

            @block.scalar
            def _(act):
                for n in range(groups):
                    t, q = n // (kt // 4), n % (kt // 4)
                    act.wait_ge(tr, n + 1)
                    act.activation(gT[0][:, 4 * q:4 * q + 4, t * P:(t + 1) * P],
                                   acc[n % (2 * NX)][:, :].rearrange("p (k c) -> p k c", k=4), ACT.Copy
                                   ).then_inc(g_hi, 1)
                for k in range(kt):
                    act.wait_ge(raw_in[k % RING], 16 * (k // RING + 1))
                    if k >= RING:
                        act.wait_ge(used, k - RING + 1)
                    act.activation(wh[:, k % RING], raw[:, k % RING], ACT.Copy).then_inc(hi, 1)

            @block.vector
            def _(dve):
                own = Count(dv)
                for n in range(groups):
                    t, q = n // (kt // 4), n % (kt // 4)
                    dve.wait_ge(g_hi, n + 1)
                    at = (slice(None), slice(4 * q, 4 * q + 4), slice(t * P, (t + 1) * P))
                    dve.tensor_tensor(gT[1][at], acc[n % (2 * NX)][:, :].rearrange("p (k c) -> p k c", k=4),
                                      f(gT[0][at]), ALU.subtract).then_inc(g_lo, 1)
                for k in range(kt):
                    dve.wait_ge(hi, k + 1)
                    dve.tensor_tensor(wl[:, k % RING], raw[:, k % RING], f(wh[:, k % RING]), ALU.subtract
                                      ).then_inc(lo, 1)
                dve.wait_ge(gate_in, 16)
                if xin is not None:
                    dve.wait_ge(x_in, 16)
                for t in range(NX):
                    for half in range(2):
                        cols = slice(half * H, (half + 1) * H)
                        dve.wait_ge(done, 2 * t + half + 1)
                        y = raw[:, half, 0:H]
                        own.inc(dve.tensor_tensor(y, acc[2 * t + half][:, :], gate[:, cols], ALU.mult))
                        own.after(dve)
                        x_old = xin[:, t, cols] if xin is not None else res[:, t, cols]
                        own.inc(dve.tensor_tensor(res[:, t, cols], x_old, y, ALU.add))


def phase_route(nc, a, scr, ident, minus_half, layer, res, dest, wk, table):
    with ExitStack() as ctx:
        sb, sem, banks = alloc(nc, ctx, f"route{layer}")
        tok = sb("tok", [P, NX, D])
        fT = sb("fT", [P, 2, KT, P])
        md, nm, junk = sb("md", [P, 2, D]), sb("nm", [P, D]), sb("junk", [P, D])
        rw = sb("rw", [P, KT, NE])
        bias, order = sb("bias", [P, NE]), sb("order", [P, NE + NG + MAX_OVER + 1])
        below = sb("below", [P, 2, P])
        ss, rs = sb("ss", [P, NX]), sb("rs", [P, NX])
        sc, sel, oh0, oh1, tmp, both = (sb(n, [P, NX, NE]) for n in ("sc", "sel", "oh0", "oh1", "tmp", "both"))
        rank = sb("rank", [P, NX, NE])
        pair = sb("pair", [P, NX * NG, 6])
        gsum, gone, gkey = (sb(n, [P, NX, NG]) for n in ("gsum", "gone", "gkey"))
        mx, wf, df = sb("mx", [P, NX, 1]), sb("wf", [P, NX, 2]), sb("df", [P, NX, 2])
        cnt = sb("cnt", [P, 8, NE])
        cmp_ = sb("cmp", [P, MAX_OVER, NE])
        tf = sb("tf", [P, NBLK + 1])
        pT, pL = banks("pT", 4), banks("pL", 3)
        in_tok, in_c, sq, ms, rs_ok = sem("mod_in"), sem("consts_in"), sem("squares"), sem("ms"), sem("rs_ready")
        tok_ok, tr, fT_ok, logit, score = sem("tok_ready"), sem("transposed"), sem("fT_ready"), sem("logits"), sem("scores")
        chosen, ranked, placed, dv = sem("chosen"), sem("ranked"), sem("placed"), sem("dve_steps")
        sent = sem("rows_sent")
        with nc.Block() as block:

            @block.sync
            def _(sp):
                for v in range(2):
                    sp.dma_start(md[:, v], scr["mod"][layer, 0:1, (3 + v) * D:(4 + v) * D].to_broadcast([P, D])
                                 ).then_inc(in_tok, 16)
                sp.dma_start(nm[:], a["norm_ffn"][layer:layer + 1, :].to_broadcast([P, D])).then_inc(in_tok, 16)
                sp.dma_start(rw[:], a["router_w"].rearrange("(k p) e -> p k e", p=P)).then_inc(in_c, 16)
                sp.dma_start(bias[:], a["router_bias"].rearrange("(o e) -> o e", o=1).to_broadcast([P, NE])
                             ).then_inc(in_c, 16)
                sp.dma_start(order[:], a["order"].to_broadcast([P, NE + NG + MAX_OVER + 1])).then_inc(in_c, 16)
                sp.dma_start(below[:], a["below"].rearrange("s p c -> p s c")).then_inc(in_c, 16)

            @block.scalar
            def _(act):
                for t in range(NX):
                    if t:
                        act.wait_ge(sq, t)
                    act.activation(junk[:], res[:, t], ACT.Square, accum_out=ss[:, t:t + 1]).then_inc(sq, 1)
                for t in range(NX):
                    for half in range(2):
                        n = 2 * t + half
                        act.wait_ge(tr, n + 1)
                        if t >= 2:
                            act.wait_ge(logit, t - 1)
                        act.activation(fT[:, t % 2, 4 * half:4 * half + 4].rearrange("p k c -> p (k c)"),
                                       pT[n % 4][:, :], ACT.Copy).then_inc(fT_ok, 1)
                act.wait_ge(logit, NX)
                act.activation(sc[:].rearrange("p t e -> p (t e)"), pL[0][:, 0:NX * NE], ACT.Sigmoid).then_inc(score, 1)

            @block.gpsimd
            def _(pool):
                pool.wait_ge(ms, 1)
                pool.tensor_tensor(rs[:], ss[:], minus_half[:, 0:NX], ALU.pow).then_inc(rs_ok, 1)
                pool.wait_ge(placed, 1)
                for t in range(NX):
                    for s in range(2):
                        pool.indirect_dma_start(
                            out=scr["xs"], out_offset=bass.IndirectOffsetOnAxis(ap=dest[:, 0, s, t:t + 1].bitcast(U32), axis=0),
                            in_=tok[:, t], in_offset=None, bounds_check=(NBLK + 1) * P - 1, oob_is_err=False
                        ).then_inc(sent, 16)
                pool.wait_ge(sent, 16 * 2 * NX)

            @block.tensor
            def _(pe):
                pe.wait_ge(in_c, 64)

                def logits(t):
                    pe.wait_ge(fT_ok, 2 * t + 2)
                    for k in range(KT):
                        last = pe.matmul(pL[0][:, t * NE:(t + 1) * NE], fT[:, t % 2, k], rw[:, k],
                                         start=k == 0, stop=k == KT - 1)
                    last.then_inc(logit, 1)

                for t in range(NX):
                    pe.wait_ge(tok_ok, t + 1)
                    for half in range(2):
                        n = 2 * t + half
                        if n >= 4:
                            pe.wait_ge(fT_ok, n - 3)
                        for k in range(4):
                            last = pe.transpose(pT[n % 4][:, k * P:(k + 1) * P],
                                                tok[:, t, (4 * half + k) * P:(4 * half + k + 1) * P], ident[:])
                        last.then_inc(tr, 1)
                    if t:
                        logits(t - 1)
                logits(NX - 1)
                pe.wait_ge(chosen, 1)
                for t in range(NX):
                    for u in range(t + 1):
                        last = pe.matmul(pL[1][:, t * NE:(t + 1) * NE], below[:, 0 if u == t else 1], both[:, u],
                                         start=u == 0, stop=u == t)
                for u in range(NX):
                    last = pe.matmul(pL[2][:, 0:NE], below[:, 1], both[:, u], start=u == 0, stop=u == NX - 1)
                last.then_inc(ranked, 1)

            @block.vector
            def _(dve):
                own = Count(dv)

                def step(ins):
                    own.inc(ins)
                    own.after(dve)

                dve.wait_ge(sq, NX)
                dve.tensor_scalar(ss[:], ss[:], 1.0 / D, EPS, ALU.mult, ALU.add).then_inc(ms, 1)
                dve.wait_ge(in_tok, 48)
                step(dve.scalar_tensor_tensor(md[:, 1], md[:, 1], 1.0, nm[:], ALU.add, ALU.mult))
                dve.wait_ge(rs_ok, 1)
                for t in range(NX):
                    step(dve.scalar_tensor_tensor(tok[:, t], res[:, t], rs[:, t:t + 1], md[:, 1], ALU.mult, ALU.mult))
                    dve.tensor_tensor(tok[:, t], tok[:, t], md[:, 0], ALU.add).then_inc(tok_ok, 1)
                dve.wait_ge(in_c, 64)
                dve.wait_ge(score, 1)
                flat = [P, NX * NG, EPG]
                step(dve.tensor_tensor(sel[:], sc[:], bias[:].rearrange("p (o e) -> p o e", o=1).to_broadcast([P, NX, NE]),
                                       ALU.add))
                s4 = sel[:].rearrange("p t (g e) -> p (t g) e", e=EPG)
                pairs = [(i, j) for i in range(EPG) for j in range(i + 1, EPG)]
                for n, (i, j) in enumerate(pairs):
                    own.inc(dve.tensor_tensor(pair[:, :, n:n + 1], s4[:, :, i:i + 1], s4[:, :, j:j + 1], ALU.add))
                own.after(dve)
                step(dve.tensor_reduce(gsum[:].rearrange("p t g -> p (t g)"), pair[:], AX.X, ALU.max))

                def first_largest(out, v, key, n, first):
                    step(dve.tensor_reduce(mx[:].rearrange("p t o -> p (t o)"), v, AX.X, ALU.max))
                    step(dve.tensor_tensor(key, v, mx[:].to_broadcast([P, NX, n]), ALU.is_ge))
                    step(dve.tensor_tensor(key, key, first.rearrange("p (o e) -> p o e", o=1).to_broadcast([P, NX, n]),
                                           ALU.mult))
                    step(dve.tensor_reduce(mx[:].rearrange("p t o -> p (t o)"), key, AX.X, ALU.max))
                    step(dve.tensor_tensor(out, key, mx[:].to_broadcast([P, NX, n]), ALU.is_equal))

                first_largest(gone[:], gsum[:], gkey[:], NG, order[:, NE:NE + NG])
                step(dve.tensor_scalar(gkey[:], gone[:], BIG, -BIG, ALU.mult, ALU.add))
                step(dve.tensor_tensor(s4, s4, gkey[:].rearrange("p t (g o) -> p (t g) o", o=1).to_broadcast(flat), ALU.add))
                for s, oh in enumerate((oh0, oh1)):
                    first_largest(oh[:], sel[:], tmp[:], NE, order[:, 0:NE])
                    if s == 0:
                        step(dve.scalar_tensor_tensor(sel[:], oh[:], -2 * BIG, sel[:], ALU.mult, ALU.add))
                    step(dve.tensor_tensor(tmp[:], oh[:], sc[:], ALU.mult))
                    step(dve.tensor_reduce(wf[:, :, s], tmp[:], AX.X, ALU.add))
                dve.tensor_tensor(both[:], oh0[:], oh1[:], ALU.add).then_inc(chosen, 1)
                step(dve.tensor_tensor(mx[:], wf[:, :, 0:1], wf[:, :, 1:2], ALU.add))
                step(dve.reciprocal(mx[:], mx[:]))
                step(dve.tensor_tensor(wk[:], wf[:], mx[:].to_broadcast([P, NX, 2]), ALU.mult))
                dve.wait_ge(ranked, 1)
                step(dve.tensor_copy(rank[:].rearrange("p t e -> p (t e)"), pL[1][:, 0:NX * NE]))
                total, more, end, other = (cnt[:, i] for i in range(4))
                step(dve.tensor_copy(total, pL[2][:, 0:NE]))
                step(dve.tensor_scalar(more, total, float(P), None, ALU.is_gt))
                for m in range(2, SEQ // P):
                    step(dve.scalar_tensor_tensor(more, total, float(m * P), more, ALU.is_gt, ALU.add))
                step(dve.tensor_copy(end, more))
                src, dst = end, other
                for d in (1, 2, 4, 8):
                    own.inc(dve.tensor_copy(dst[:, 0:d], src[:, 0:d]))
                    step(dve.tensor_tensor(dst[:, d:], src[:, d:], src[:, 0:NE - d], ALU.add))
                    src, dst = dst, src
                end = src
                base, over = cnt[:, 4], cnt[:, 5]
                step(dve.tensor_scalar(base, order[:, 0:NE], -float(P), float(NE * P), ALU.mult, ALU.add))
                step(dve.tensor_tensor(over, end, more, ALU.subtract))
                step(dve.tensor_scalar(over, over, float(P), float(NE * P - P), ALU.mult, ALU.add))
                step(dve.tensor_tensor(over, over, base, ALU.subtract))
                wide = lambda v: v.rearrange("p (o e) -> p o e", o=1).to_broadcast([P, NX, NE])
                step(dve.tensor_scalar(tmp[:], rank[:], float(P), None, ALU.is_ge))
                step(dve.tensor_tensor(tmp[:], tmp[:], wide(over), ALU.mult))
                step(dve.tensor_tensor(tmp[:], tmp[:], wide(base), ALU.add))
                step(dve.tensor_tensor(rank[:], rank[:], tmp[:], ALU.add))
                for s, oh in enumerate((oh0, oh1)):
                    step(dve.tensor_tensor(tmp[:], oh[:], rank[:], ALU.mult))
                    step(dve.tensor_reduce(df[:, :, s], tmp[:], AX.X, ALU.add))
                step(dve.tensor_copy(dest[:, 0], df[:].rearrange("p t s -> p s t")))
                step(dve.tensor_scalar(df[:], df[:], float(P), None, ALU.add))
                step(dve.tensor_copy(dest[:, 1], df[:].rearrange("p t s -> p s t")))
                step(dve.tensor_scalar(tf[:, 0:NE], order[:, 0:NE], -1.0, float(NE), ALU.mult, ALU.add))
                step(dve.tensor_tensor(cmp_[:], end.rearrange("p (o e) -> p o e", o=1).to_broadcast([P, MAX_OVER, NE]),
                                       order[:, NE + NG:NE + NG + MAX_OVER].rearrange("p (b o) -> p b o", o=1
                                                                                      ).to_broadcast([P, MAX_OVER, NE]),
                                       ALU.is_le))
                step(dve.tensor_reduce(tf[:, NE:NBLK], cmp_[:], AX.X, ALU.add))
                step(dve.tensor_scalar(tf[:, NE:NBLK], tf[:, NE:NBLK], float(NE - 1), None, ALU.min))
                step(dve.tensor_scalar(tf[:, NBLK:NBLK + 1], end[:, NE - 1:NE], float(NE), None, ALU.add))
                step(dve.tensor_copy(table[:], tf[:]))
                dve.nop().then_inc(placed, 1)


def phase_experts(nc, a, scr, ident, layer, table):
    RAW, RING = 12, 8
    NCH = 3 * KT
    with ExitStack() as ctx:
        sb, sem, banks = alloc(nc, ctx, f"moe{layer}")
        raw = sb("raw", [P, RAW, D])
        wh, wl = sb("wh", [P, RING, D], F32R), sb("wl", [P, RING, D], F32R)
        xb, sg, hs, yb = sb("xb", [P, D]), sb("sg", [P, D]), sb("hs", [P, D]), sb("yb", [P, D])
        xh, xl = sb("xh", [P, KT, P], F32R), sb("xl", [P, KT, P], F32R)
        hh, hl = sb("hh", [P, KT, P], F32R), sb("hl", [P, KT, P], F32R)
        pg, pu, pd, pT = banks("pg", 2), banks("pu", 2), banks("pd", 2), banks("pT", 2)
        raw_in = [sem(f"raw_in{i}") for i in range(RAW)]
        x_in, x_t, x_hi, x_lo = sem("x_in"), sem("x_transposed"), sem("x_hi"), sem("x_lo")
        hi, lo, used = sem("w_hi"), sem("w_lo"), sem("chunk_used")
        sg_ok, h_ok, h_t, h_hi, h_lo = sem("silu_ready"), sem("h_ready"), sem("h_transposed"), sem("h_hi"), sem("h_lo")
        y_read, y_out, d_set = sem("y_read"), sem("y_out"), sem("y_first")
        weights = [a[n][layer].rearrange("e (k p) n -> e p k n", p=P) for n in ("moe_w_gate", "moe_w_up", "moe_w_down")]
        xs = scr["xs"].rearrange("(b p) d -> b p d", p=P)
        ys = scr["ys"].rearrange("(b p) d -> b p d", p=P)

        def turns(eng, body, bound):
            with eng.Fori(0, NBLK) as b:
                with eng.If(b < bound):
                    body(b)
                with eng.Else():
                    eng.nop()
            eng.nop()

        with nc.Block() as block:

            @block.sync
            def _(sp):
                bound = sp.value_load(table[0:1, NBLK:NBLK + 1], min_val=NE, max_val=NBLK)
                sp.dma_start(xb[:], xs[0]).then_inc(x_in, 16)

                def body(b):
                    e = sp.value_load(table[0:1, bass.ds(b, 1)], min_val=0, max_val=NE - 1)
                    for c in range(NCH):
                        sp.wait_ge(lo, b * NCH + c + 1)
                        sp.dma_start(raw[:, c % RAW],
                                     weights[c // KT][bass.ds(e, 1), :, c % KT, :].rearrange("o p n -> (o p) n")
                                     ).then_inc(raw_in[c % RAW], 16)
                        if c == 4:
                            sp.wait_ge(x_t, b * 2 + 2)
                            sp.dma_start(xb[:], xs[bass.ds(b + 1, 1)].rearrange("o p d -> (o p) d")).then_inc(x_in, 16)

                turns(sp, body, bound)

            @block.tensor
            def _(pe):
                pe.nop().then_inc(used, RING)
                bound = pe.value_load(table[0:1, NBLK:NBLK + 1], min_val=NE, max_val=NBLK)

                def transpose_x():
                    for half in range(2):
                        for k in range(4):
                            last = pe.transpose(pT[half][:, k * P:(k + 1) * P],
                                                xb[:, (4 * half + k) * P:(4 * half + k + 1) * P], ident[:])
                        last.then_inc(x_t, 1)

                pe.wait_ge(x_in, 16)
                for half in range(2):
                    pe.matmul(pd[half][:, :], ident[:], xb[:, half * H:(half + 1) * H], start=True, stop=True
                              ).then_inc(d_set, 1)
                transpose_x()

                def body(b):
                    pe.wait_ge(x_lo, b * 2 + 2)
                    for c in range(NCH):
                        k = c % KT
                        pe.wait_ge(lo, b * NCH + RAW + c + 1)
                        if c < 2 * KT:
                            out, lhs = (pg, pu)[c // KT], (xh[:, k], xl[:, k])
                        else:
                            out, lhs = pd, (hh[:, k], hl[:, k])
                            if k == 0:
                                pe.wait_ge(y_read, b * 2 + 2)
                            if k % 4 == 0:
                                pe.wait_ge(h_lo, b * 2 + k // 4 + 1)
                        for half in range(2):
                            cols = slice(half * H, (half + 1) * H)
                            last = three(pe, out[half][:, :], lhs, (wh[:, c % RING, cols], wl[:, c % RING, cols]),
                                         k == 0, k == KT - 1)
                        last.then_inc(used, 1)
                        if c == 2 * KT - 1:
                            for half in range(2):
                                pe.wait_ge(h_ok, b * 2 + half + 1)
                                for kk in range(4):
                                    last = pe.transpose(pT[half][:, kk * P:(kk + 1) * P],
                                                        hs[:, (4 * half + kk) * P:(4 * half + kk + 1) * P], ident[:])
                                last.then_inc(h_t, 1)
                        if c == 2 * KT + 4:
                            pe.wait_ge(x_in, b * 16 + 32)
                            transpose_x()

                turns(pe, body, bound)

            @block.scalar
            def _(act):
                bound = act.value_load(table[0:1, NBLK:NBLK + 1], min_val=NE, max_val=NBLK)

                def x_parts(n0):
                    for half in range(2):
                        act.wait_ge(x_t, n0 + half)
                        act.activation(xh[:, 4 * half:4 * half + 4].rearrange("p k c -> p (k c)"), pT[half][:, :],
                                       ACT.Copy).then_inc(x_hi, 1)

                x_parts(1)

                act.wait_ge(d_set, 2)

                def store(b):
                    act.wait_ge(used, b * NCH + RING)
                    act.wait_ge(y_out, b * 16 + 1)
                    for half in range(2):
                        act.activation(yb[:, half * H:(half + 1) * H], pd[half][:, :], ACT.Copy).then_inc(y_read, 1)
                    act.wait_ge(y_read, b * 2 + 2)
                    act.dma_start(ys[bass.ds(b, 1)].rearrange("o p d -> (o p) d"), yb[:]).then_inc(y_out, 16)

                act.nop().then_inc(y_out, 1)

                def body(b):
                    for c in range(NCH):
                        act.wait_ge(raw_in[c % RAW], b * (16 * NCH // RAW) + 16 * (c // RAW + 1))
                        act.wait_ge(used, b * NCH + c + 1)
                        act.activation(wh[:, c % RING], raw[:, c % RAW], ACT.Copy).then_inc(hi, 1)
                        if c == 3:
                            store(b)
                        if c == 12:
                            act.wait_ge(used, b * NCH + RING + KT)
                            for half in range(2):
                                act.activation(sg[:, half * H:(half + 1) * H], pg[half][:, :], ACT.Silu).then_inc(sg_ok, 1)
                        if c == 19:
                            for half in range(2):
                                act.wait_ge(h_t, b * 2 + half + 1)
                                act.activation(hh[:, 4 * half:4 * half + 4].rearrange("p k c -> p (k c)"), pT[half][:, :],
                                               ACT.Copy).then_inc(h_hi, 1)
                    x_parts(b * 2 + 3)

                turns(act, body, bound)
                store(bound)
                act.wait_ge(y_out, bound * 16 + 17)
                act.activation(yb[0:1, 0:1], sg[0:1, 0:1], ACT.Copy)

            @block.vector
            def _(dve):
                dve.nop().then_inc(lo, RAW)
                bound = dve.value_load(table[0:1, NBLK:NBLK + 1], min_val=NE, max_val=NBLK)

                def x_parts(n0):
                    for half in range(2):
                        dve.wait_ge(x_hi, n0 + half)
                        at = xh[:, 4 * half:4 * half + 4].rearrange("p k c -> p (k c)")
                        dve.tensor_tensor(xl[:, 4 * half:4 * half + 4].rearrange("p k c -> p (k c)"), pT[half][:, :],
                                          f(at), ALU.subtract).then_inc(x_lo, 1)

                x_parts(1)

                def body(b):
                    for c in range(NCH):
                        dve.wait_ge(hi, b * NCH + c + 1)
                        dve.tensor_tensor(wl[:, c % RING], raw[:, c % RAW], f(wh[:, c % RING]), ALU.subtract
                                          ).then_inc(lo, 1)
                        if c == 19:
                            dve.wait_ge(used, b * NCH + RING + 2 * KT)
                            for half in range(2):
                                cols = slice(half * H, (half + 1) * H)
                                dve.wait_ge(sg_ok, b * 2 + half + 1)
                                dve.tensor_tensor(hs[:, cols], pu[half][:, :], sg[:, cols], ALU.mult).then_inc(h_ok, 1)
                            for half in range(2):
                                dve.wait_ge(h_hi, b * 2 + half + 1)
                                at = hh[:, 4 * half:4 * half + 4].rearrange("p k c -> p (k c)")
                                dve.tensor_tensor(hl[:, 4 * half:4 * half + 4].rearrange("p k c -> p (k c)"),
                                                  pT[half][:, :], f(at), ALU.subtract).then_inc(h_lo, 1)
                    x_parts(b * 2 + 3)

                turns(dve, body, bound)


def phase_combine(nc, a, scr, layer, res, dest, wk, minus_half, then):
    with ExitStack() as ctx:
        sb, sem, banks = alloc(nc, ctx, f"combine{layer}")
        yg = sb("yg", [P, 2, NX, D])
        gate, nm, junk = sb("gate", [P, D]), sb("nm", [P, D]), sb("junk", [P, 2, D])
        md = sb("md", [P, 2, D])
        ss, rs = sb("ss", [P, NX]), sb("rs", [P, NX])
        got = [[sem(f"y{s}_{t}") for t in range(NX)] for s in range(2)]
        c_in, sq, ms, rs_ok, dv, res_ok = (sem(n) for n in ("consts_in", "squares", "ms", "rs_ready", "dve_steps", "res_ready"))
        h_f32, h_hi, outs, normed = sem("h_f32"), sem("h_hi"), sem("outs"), sem("normed")
        norm_row, mod_layer, hh, hl = then
        with nc.Block() as block:

            @block.gpsimd
            def _(pool):
                for t in range(NX):
                    for s in range(2):
                        pool.indirect_dma_start(
                            out=yg[:, s, t], out_offset=None, in_=scr["ys"],
                            in_offset=bass.IndirectOffsetOnAxis(ap=dest[:, 1, s, t:t + 1].bitcast(U32), axis=0),
                            bounds_check=(NBLK + 1) * P - 1, oob_is_err=False).then_inc(got[s][t], 16)
                for t in range(NX):
                    pool.wait_ge(ms, t + 1)
                    pool.tensor_tensor(rs[:, t:t + 1], ss[:, t:t + 1], minus_half[:, 0:1], ALU.pow).then_inc(rs_ok, 1)

            @block.sync
            def _(sp):
                sp.dma_start(gate[:], scr["mod"][layer, 0:1, 5 * D:6 * D].to_broadcast([P, D])).then_inc(c_in, 16)
                sp.dma_start(nm[:], norm_row.to_broadcast([P, D])).then_inc(c_in, 16)
                if mod_layer is not None:
                    for v in range(2):
                        sp.dma_start(md[:, v], scr["mod"][mod_layer, 0:1, v * D:(v + 1) * D].to_broadcast([P, D])
                                     ).then_inc(c_in, 16)
                else:
                    for t in range(NX):
                        sp.wait_ge(normed, t + 1)
                        sp.dma_start(a["out"][0, t * P:(t + 1) * P, :], yg[:, 0, t]).then_inc(outs, 16)
                    sp.wait_ge(outs, 16 * NX)

            @block.scalar
            def _(act):
                for t in range(NX):
                    act.wait_ge(res_ok, t + 1)
                    if t >= 2:
                        act.wait_ge(sq, t - 1)
                    act.activation(junk[:, t % 2], res[:, t], ACT.Square, accum_out=ss[:, t:t + 1]).then_inc(sq, 1)
                if mod_layer is not None:
                    for t in range(NX):
                        act.wait_ge(h_f32, t + 1)
                        act.activation(hh[:, t], yg[:, 0, t], ACT.Copy).then_inc(h_hi, 1)

            @block.vector
            def _(dve):
                own = Count(dv)

                def step(ins):
                    own.inc(ins)
                    own.after(dve)

                dve.wait_ge(c_in, 16 * (4 if mod_layer is not None else 2))
                if mod_layer is not None:
                    step(dve.scalar_tensor_tensor(md[:, 1], md[:, 1], 1.0, nm[:], ALU.add, ALU.mult))
                for t in range(NX):
                    for s in range(2):
                        dve.wait_ge(got[s][t], 16)
                    step(dve.tensor_scalar(yg[:, 0, t], yg[:, 0, t], wk[:, t, 0:1], None, ALU.mult))
                    step(dve.scalar_tensor_tensor(yg[:, 0, t], yg[:, 1, t], wk[:, t, 1:2], yg[:, 0, t],
                                                  ALU.mult, ALU.add))
                    step(dve.tensor_tensor(yg[:, 0, t], yg[:, 0, t], gate[:], ALU.mult))
                    dve.tensor_tensor(res[:, t], res[:, t], yg[:, 0, t], ALU.add).then_inc(res_ok, 1)
                for t in range(NX):
                    dve.wait_ge(sq, t + 1)
                    dve.tensor_scalar(ss[:, t:t + 1], ss[:, t:t + 1], 1.0 / D, EPS, ALU.mult, ALU.add).then_inc(ms, 1)
                    dve.wait_ge(rs_ok, t + 1)
                    scale = md[:, 1] if mod_layer is not None else nm[:]
                    ins = dve.scalar_tensor_tensor(yg[:, 0, t], res[:, t], rs[:, t:t + 1], scale, ALU.mult, ALU.mult)
                    if mod_layer is None:
                        ins.then_inc(normed, 1)
                    else:
                        step(ins)
                        dve.tensor_tensor(yg[:, 0, t], yg[:, 0, t], md[:, 0], ALU.add).then_inc(h_f32, 1)
                        dve.wait_ge(h_hi, t + 1)
                        dve.tensor_tensor(hl[:, t], yg[:, 0, t], f(hh[:, t]), ALU.subtract)


def phase_fourier(nc, a, hh, hl, fh, fl):
    with ExitStack() as ctx:
        sb, sem, banks = alloc(nc, ctx, "fourier")
        raw = sb("raw", [P, 2, NX, SEQ])
        ch, cl = sb("ch", [P, 2, NX, SEQ], F32R), sb("cl", [P, 2, NX, SEQ], F32R)
        gr = sb("gr", [P, 2, 2, FG])
        gh, gl = sb("gh", [P, 2, 2, FG], F32R), sb("gl", [P, 2, 2, FG], F32R)
        uh, ul = sb("uh", [P, 2, 2, SEQ], F32R), sb("ul", [P, 2, 2, SEQ], F32R)
        pU, pF = banks("pU", 4), banks("pF", 4)
        c_in = [sem("cos_in"), sem("sin_in"), sem("chan_in")]
        hi, lo, u_done, u_hi, u_lo = sem("table_hi"), sem("table_lo"), sem("u_done"), sem("u_hi"), sem("u_lo")
        f_done, f_hi, f_lo = sem("f_done"), sem("f_hi"), sem("f_lo")
        tables = [(raw[:, 0], ch[:, 0], cl[:, 0]), (raw[:, 1], ch[:, 1], cl[:, 1]), (gr[:], gh[:], gl[:])]
        NGR = D // FG
        with nc.Block() as block:

            @block.sync
            def _(sp):
                for s in range(2):
                    sp.dma_start(raw[:, s], a["dft_seq"][s].rearrange("(t p) n -> p t n", p=P)).then_inc(c_in[s], 16)
                sp.dma_start(gr[:], a["dft_chan"].rearrange("s (k p) n -> p s k n", p=P)).then_inc(c_in[2], 16)

            @block.tensor
            def _(pe):
                def sequence(g):
                    for d in range(2):
                        col = (g * 2 + d) * P
                        for s in range(2):
                            n = g * 4 + d * 2 + s
                            pe.wait_ge(lo, s + 1)
                            if g:
                                pe.wait_ge(u_lo, n - 3)
                            for t in range(NX):
                                last = three(pe, pU[d * 2 + s][:, :], (hh[:, t, col:col + P], hl[:, t, col:col + P]),
                                             (ch[:, s, t], cl[:, s, t]), t == 0, t == NX - 1)
                            last.then_inc(u_done, 1)

                def channels(g):
                    pe.wait_ge(lo, 3)
                    pe.wait_ge(u_lo, g * 4 + 4)
                    for e in range(2):
                        n = g * 2 + e
                        if n >= 4:
                            pe.wait_ge(f_lo, n - 3)
                        for d in range(2):
                            for s in range(2):
                                last = three(pe, pF[n % 4][:, :],
                                             tuple(m[:, s, d, e * P:(e + 1) * P] for m in (gh, gl)),
                                             (uh[:, d, s], ul[:, d, s]), d + s == 0, d + s == 2)
                        last.then_inc(f_done, 1)

                for g in range(NGR):
                    sequence(g)
                    channels(g)

            @block.scalar
            def _(act):
                for i, (r, h_, l_) in enumerate(tables):
                    act.wait_ge(c_in[i], 16)
                    act.activation(h_, r, ACT.Copy).then_inc(hi, 1)
                for g in range(NGR):
                    for n in range(4):
                        act.wait_ge(u_done, g * 4 + n + 1)
                        if g:
                            act.wait_ge(f_done, g * 2)
                        act.activation(uh[:, n // 2, n % 2], pU[n][:, :], ACT.Copy).then_inc(u_hi, 1)
                    for n in range(g * 2, g * 2 + 2):
                        act.wait_ge(f_done, n + 1)
                        act.activation(fh[:, n], pF[n % 4][:, :], ACT.Copy).then_inc(f_hi, 1)

            @block.vector
            def _(dve):
                for i, (r, h_, l_) in enumerate(tables):
                    dve.wait_ge(hi, i + 1)
                    dve.tensor_tensor(l_, r, f(h_), ALU.subtract).then_inc(lo, 1)
                for g in range(NGR):
                    for n in range(4):
                        dve.wait_ge(u_hi, g * 4 + n + 1)
                        dve.tensor_tensor(ul[:, n // 2, n % 2], pU[n][:, :], f(uh[:, n // 2, n % 2]), ALU.subtract
                                          ).then_inc(u_lo, 1)
                    for n in range(g * 2, g * 2 + 2):
                        dve.wait_ge(f_hi, n + 1)
                        dve.tensor_tensor(fl[:, n], pF[n % 4][:, :], f(fh[:, n]), ALU.subtract).then_inc(f_lo, 1)


def build(nc, a):
    def dram(name, shape):
        return nc.dram_tensor(name, shape, F32, kind="Internal").ap()

    scr = {"mod": dram("mod_scr", (2, 2, NMOD * D)), "strips": dram("strips_scr", (HEADS, P, STRIPS)),
           "gated": dram("gated_scr", (SEQ, HEADS * DV)),
           "xs": dram("xs_scr", ((NBLK + 1) * P, D)), "ys": dram("ys_scr", ((NBLK + 1) * P, D))}
    with ExitStack() as ctx:
        def keep(name, shape, dt=F32):
            return ctx.enter_context(nc.sbuf_tensor(name, shape, dt))

        ident, minus_half = keep("ident", [P, P]), keep("minus_half", [P, 8])
        cT = keep("cT", [P, 2 * KT])
        with nc.sbuf_tensor("hTh", [P, KT, NTOK * P], F32R) as hTh, nc.sbuf_tensor("hTl", [P, KT, NTOK * P], F32R) as hTl:
            phase_first(nc, a, scr, ident, minus_half, cT, hTh, hTl)
            phase_heads(nc, a, scr, ident, minus_half, cT, hTh, hTl)
        res = keep("res", [P, NX, D])
        dest, wk = keep("dest", [P, 2, 2, NX], I32), keep("wk", [P, NX, 2])
        table = keep("table", [P, NBLK + 1], I32)
        KO = HEADS * DV // P
        with nc.sbuf_tensor("gTh", [P, KO, SEQ], F32R) as gTh, nc.sbuf_tensor("gTl", [P, KO, SEQ], F32R) as gTl:
            project_residual(nc, a, scr, "out0", 0, KO, a["ret_w_out"][0].rearrange("(k p) n -> p k n", p=P),
                             (gTh, gTl), a["x"][0], res, ident, scr["gated"])
        phase_route(nc, a, scr, ident, minus_half, 0, res, dest, wk, table)
        phase_experts(nc, a, scr, ident, 0, table)
        with nc.sbuf_tensor("fh", [P, KT, SEQ], F32R) as fh, nc.sbuf_tensor("fl", [P, KT, SEQ], F32R) as fl:
            with nc.sbuf_tensor("h2h", [P, NX, D], F32R) as h2h, nc.sbuf_tensor("h2l", [P, NX, D], F32R) as h2l:
                phase_combine(nc, a, scr, 0, res, dest, wk, minus_half, (a["norm_mix"][1:2, :], 1, h2h, h2l))
                phase_fourier(nc, a, h2h, h2l, fh, fl)
            project_residual(nc, a, scr, "out1", 1, KT, a["fn_w_out"][0].rearrange("(k p) n -> p k n", p=P),
                             (fh, fl), None, res, ident)
        phase_route(nc, a, scr, ident, minus_half, 1, res, dest, wk, table)
        phase_experts(nc, a, scr, ident, 1, table)
        phase_combine(nc, a, scr, 1, res, dest, wk, minus_half,
                      (a["norm_final"].rearrange("(o d) -> o d", o=1), None, None, None))


_INS = ["x", "c", "ctx", "c_ctx", "w_mod", "b_mod", "norm_mix", "norm_ffn", "norm_final", "ret_w_in", "ret_decay",
        "ret_gn", "ret_w_out", "fn_w_out", "router_w", "router_bias", "moe_w_gate", "moe_w_up", "moe_w_down"]


def shape_constants():
    import numpy as np
    p = np.arange(P, dtype=np.float64)[:, None]
    delta = np.arange(XR)[None, :] - XO - p
    w = np.arange(CR)[None, :]
    ahead, behind = w - P + CTX - p, SEQ - (w - P) + p
    distances = np.concatenate([np.maximum(delta, 0), np.maximum(-delta, 0), ahead, behind], 1)
    nf = DK // 4
    inv = (np.float32(10000.0) ** (-np.arange(nf, dtype=np.float32) / np.float32(nf))).astype(np.float32)
    t = np.arange(SEQ)
    ang = np.stack([(t // 64).astype(np.float32)[:, None] * inv, (t % 64).astype(np.float32)[:, None] * inv], 1)
    rope = np.stack([np.cos(ang), np.sin(ang)], 1)
    rope = rope.reshape(NX, P, 2 * 2 * nf).transpose(1, 0, 2)
    a = 2 * np.pi * (np.outer(np.arange(SEQ), np.arange(SEQ)) % SEQ) / SEQ
    g = 2 * np.pi * (np.outer(np.arange(FG), np.arange(FG)) % FG) / FG
    return {
        "identity": np.eye(P), "distances": distances, "rope": rope,
        "dft_seq": np.stack([np.cos(a), np.sin(a)]) / np.sqrt(SEQ),
        "dft_chan": np.stack([np.cos(g), -np.sin(g)]) / np.sqrt(FG),
        "below": np.stack([np.tril(np.ones((P, P)), -1).T, np.ones((P, P))]),
        "order": np.concatenate([NE - np.arange(NE), NG - np.arange(NG), np.arange(MAX_OVER + 1)])[None],
    }


def kernel(**inputs):
    import numpy as _np
    import concourse.bacc as _bacc
    from concourse import mybir as _mybir
    from concourse.bass_utils import run_bass_kernel_spmd as _run

    nc = _bacc.Bacc("TRN2", target_bir_lowering=False, num_devices=1)
    arrays, args = {}, {}
    given = {name: _np.ascontiguousarray(inputs[name]) for name in _INS}
    given.update({k: _np.ascontiguousarray(v, dtype=_np.float32) for k, v in shape_constants().items()})
    for name, arr in given.items():
        arrays[f"in_{name}_dram"] = arr
        args[name] = nc.dram_tensor(f"in_{name}_dram", arr.shape, _mybir.dt.from_np(arr.dtype),
                                    kind="ExternalInput").ap()
    args["out"] = nc.dram_tensor("out_0_dram", (1, SEQ, D), _mybir.dt.float32, kind="ExternalOutput").ap()
    build(nc, args)
    r = _run(nc, [arrays], core_ids=[0])
    return r.results[0]["out_0_dram"]
```

```python
import concourse.bass as bass
from concourse import mybir
from contextlib import ExitStack

F32, F32R = mybir.dt.float32, mybir.dt.float32r
I32, U32 = mybir.dt.int32, mybir.dt.uint32
ALU = mybir.AluOpType
ACT = mybir.ActivationFunctionType
AX = mybir.AxisListType

P = 128
D = 1024
KT = D // P
SEQ, CTX = 512, 256
NX, NC = SEQ // P, CTX // P
NTOK = NX + NC
NMOD = 6
EPS = 1e-6
HEADS, DK, DV = 4, 256, 512
NE, NG, EPG = 16, 4, 4
MAX_OVER = (2 * SEQ) // (P + 1)
NBLK = NE + MAX_OVER
XR = SEQ + 3 * P
XO = SEQ - P
CR = SEQ + P
STRIPS = XR + CR
H = 512
FG = 256
BIG = 1e30


class Count:

    def __init__(self, sem, base=0):
        self.sem, self.n, self.base = sem, 0, base

    def inc(self, ins):
        ins.then_inc(self.sem, 1)
        self.n += 1
        return self.n

    def after(self, eng):
        eng.wait_ge(self.sem, self.base + self.n)


def alloc(nc, ctx, tag):
    def sb(name, shape, dt=F32):
        return ctx.enter_context(nc.sbuf_tensor(f"{tag}_{name}", shape, dt))

    sems = []

    def clear():
        nc.clear_and_free_semaphores(sems)
        nc.all_engine_barrier()

    ctx.callback(clear)

    def sem(name):
        sems.append(nc.alloc_semaphore(f"{tag}_{name}"))
        return sems[-1]

    def banks(name, n):
        return [ctx.enter_context(nc.psum_tensor(f"{tag}_{name}{i}", [P, H], F32)) for i in range(n)]

    return sb, sem, banks


def f(ap):
    return ap.bitcast(F32)


def phase_first(nc, a, scr, ident, minus_half, cT, hTh, hTl, raw):
    SL = 2 * D // H
    NCH = 2 * SL
    EW = 2 * XR + 2 * CR
    with ExitStack() as ctx:
        sb, sem, banks = alloc(nc, ctx, "first")
        crow, csilu = sb("crow", [2 * KT, P]), sb("csilu", [2 * KT, P])
        wm = sb("wm", [P, 4, 4, H])
        brow = sb("brow", [2, 2 * D])
        dist, dl = sb("dist", [P, EW]), sb("dl", [P, 2 * HEADS])
        t = sb("t", [P, 8, 2 * HEADS])
        ex, strip = sb("ex", [P, EW]), sb("strip", [P, HEADS, STRIPS])
        xt = sb("xt", [P, NTOK, D])
        md, nm, junk = sb("md", [P, 4, D]), sb("nm", [P, D]), sb("junk", [P, D])
        ss, rs = sb("ss", [P, NTOK]), sb("rs", [P, NTOK])
        pm, pc, pT = banks("pm", 2), banks("pc", 1)[0], banks("pT", 4)
        s_c, s_id, s_b, s_dist, s_dl = (sem(n) for n in ("c_in", "id_in", "b_in", "dist_in", "dl_in"))
        w_in = [sem(f"w_in{i}") for i in range(NCH)]
        s_silu, s_cT, s_cTs, half_ok = sem("c_silu"), sem("c_transposed"), sem("cT_ready"), sem("minus_half")
        chunk_used, row_ready, md_row = sem("chunk_used"), sem("row_ready"), sem("mod_row_on_all_partitions")
        dv, lg, e_ready, strip_ready = sem("dve_steps"), sem("log_decay"), sem("exps_ready"), sem("strip_ready")
        s_exp, strip_out = sem("exp_abs"), sem("strip_out")
        x_in = [sem(f"x_in{i}") for i in range(NTOK)]
        md_in, nm_in, sq, ms, rs_ready = sem("mod_rows_spread"), sem("norm_row_in"), sem("squares"), sem("mean_square"), sem("rs_ready")
        w1_in = sem("head_weights_in")
        h_ready, tr, hi, lo = sem("h_ready"), sem("transposed"), sem("hi_ready"), sem("lo_ready")
        w_view = a["w_mod"][0].rearrange("(b k p) n -> b p k n", p=P, k=4)
        with nc.Block() as block:

            @block.sync
            def _(sp):
                sp.dma_start(crow[0:KT, :], a["c"].rearrange("o (k p) -> (o k) p", p=P)).then_inc(s_c, 16)
                sp.dma_start(crow[KT:2 * KT, :], a["c_ctx"].rearrange("(k p) -> k p", p=P)).then_inc(s_c, 16)
                sp.dma_start(ident[:], a["identity"]).then_inc(s_id, 16)
                for c in range(NCH):
                    if c >= 4:
                        sp.wait_ge(chunk_used, c - 3)
                    sp.dma_start(wm[:, c % 4], w_view[c % 2, :, :, (c // 2) * H:(c // 2 + 1) * H]).then_inc(w_in[c], 16)
                w1 = a["ret_w_in"].rearrange("o (k p) n -> p (o k) n", p=P)
                for cc in range(KT // 2):
                    for part in range(2):
                        sp.dma_start(raw[:, cc, :, part * DK:(part + 1) * DK],
                                     w1[:, 2 * cc:2 * cc + 2, part * D:part * D + DK]).then_inc(w1_in, 16)
                sp.wait_ge(w1_in, 16 * KT)

            @block.tensor
            def _(pe):
                pe.wait_ge(s_id, 16)
                pe.wait_ge(s_silu, 1)
                pe.transpose(pc[:, 0:2 * KT], csilu[:], ident[0:2 * KT, 0:2 * KT]).then_inc(s_cT, 1)
                pe.wait_ge(s_cTs, 1)
                for c in range(NCH):
                    sl = c // 2
                    if c % 2 == 0 and sl >= 2:
                        pe.wait_ge(row_ready, sl - 1)
                    pe.wait_ge(w_in[c], 16)
                    for k in range(4):
                        kk = (c % 2) * 4 + k
                        mm = pe.matmul(pm[sl % 2][0:2, :], cT[:, kk:kk + KT + 1:KT], wm[:, c % 4, k, :],
                                       start=kk == 0, stop=kk == KT - 1)
                    mm.then_inc(chunk_used, 1)
                for sl in range(SL):
                    pe.wait_ge(row_ready, sl + 1)
                    for s in range(2):
                        n = 2 * sl + s
                        if n >= 4:
                            pe.wait_ge(md_in, n - 3)
                        pe.matmul(pT[n % 4][:, :], ident[0:2, s:s + 1].to_broadcast([2, P]), brow[:, sl * H:(sl + 1) * H],
                                  start=True, stop=True).then_inc(md_row, 1)
                pe.wait_ge(md_in, 2 * SL)
                for tb in range(NTOK):
                    pe.wait_ge(h_ready, tb + 1)
                    for half in range(2):
                        n = 2 * tb + half
                        if n >= 4:
                            pe.wait_ge(lo, n - 3)
                        for k in range(4):
                            ins = pe.transpose(pT[n % 4][:, k * P:(k + 1) * P],
                                               xt[:, tb, (4 * half + k) * P:(4 * half + k + 1) * P], ident[:])
                        ins.then_inc(tr, 1)

            @block.scalar
            def _(act):
                act.dma_start(dist[:], a["distances"]).then_inc(s_dist, 16)
                act.dma_start(brow[0:1, :], a["b_mod"][0:1, 0:2 * D]).then_inc(s_b, 16)
                act.dma_start(brow[1:2, :], a["b_mod"][0:1, 0:2 * D]).then_inc(s_b, 16)
                for tb in range(NTOK):
                    src = (a["x"][0, tb * P:(tb + 1) * P, :] if tb < NX
                           else a["ctx"][0, (tb - NX) * P:(tb - NX + 1) * P, :])
                    act.dma_start(xt[:, tb, :], src).then_inc(x_in[tb], 16)
                act.dma_start(nm[:], a["norm_mix"][0:1, :].to_broadcast([P, D])).then_inc(nm_in, 16)
                act.wait_ge(s_c, 32)
                act.activation(csilu[:], crow[:], ACT.Silu).then_inc(s_silu, 1)
                act.wait_ge(s_cT, 1)
                act.activation(cT[:], pc[:, 0:2 * KT], ACT.Copy).then_inc(s_cTs, 1)
                act.wait_ge(dv, 2)
                act.activation(t[:, 1, :], t[:, 0, :], ACT.Exp, scale=-1.0).then_inc(s_exp, 1)
                act.wait_ge(lg, 1)
                act.wait_ge(s_dist, 16)

                def exps(h):
                    if h:
                        act.wait_ge(strip_ready, h)
                    fwd, bwd = t[:, 7, h:h + 1], t[:, 7, HEADS + h:HEADS + h + 1]
                    act.activation(ex[:, 0:XR], dist[:, 0:XR], ACT.Exp, scale=fwd)
                    act.activation(ex[:, XR:2 * XR], dist[:, XR:2 * XR], ACT.Exp, scale=bwd)
                    act.activation(ex[:, 2 * XR:2 * XR + CR], dist[:, 2 * XR:2 * XR + CR], ACT.Exp, scale=fwd)
                    act.activation(ex[:, 2 * XR + CR:], dist[:, 2 * XR + CR:], ACT.Exp, scale=bwd).then_inc(e_ready, 1)

                for h in range(HEADS):
                    exps(h)
                for tb in range(NTOK):
                    act.wait_ge(x_in[tb], 16)
                    if tb:
                        act.wait_ge(sq, tb)
                    act.activation(junk[:], xt[:, tb, :], ACT.Square, accum_out=ss[:, tb:tb + 1]).then_inc(sq, 1)
                for n in range(2 * SL):
                    sl, s = n // 2, n % 2
                    act.wait_ge(md_row, n + 1)
                    act.activation(md[:, 2 * s + sl * H // D, sl * H % D:sl * H % D + H], pT[n % 4][:, :], ACT.Copy
                                   ).then_inc(md_in, 1)
                for tb in range(NTOK):
                    for half in range(2):
                        n = 2 * tb + half
                        act.wait_ge(tr, n + 1)
                        act.activation(hTh[:, 4 * half:4 * half + 4, tb * P:(tb + 1) * P],
                                       pT[n % 4][:, :].rearrange("p (k c) -> p k c", k=4), ACT.Copy).then_inc(hi, 1)

            @block.gpsimd
            def _(pool):
                pool.dma_start(dl[:], a["ret_decay"].rearrange("o a h -> o (a h)").to_broadcast([P, 2 * HEADS])
                               ).then_inc(s_dl, 16)
                pool.memset(minus_half[:], -0.5).then_inc(half_ok, 1)
                pool.wait_ge(half_ok, 1)
                for h in range(HEADS):
                    pool.wait_ge(strip_ready, h + 1)
                    pool.dma_start(scr["strips"][h], strip[:, h]).then_inc(strip_out, 16)
                pool.wait_ge(ms, 1)
                pool.tensor_tensor(rs[:], ss[:], minus_half[:, 0:NTOK], ALU.pow).then_inc(rs_ready, 1)
                pool.wait_ge(strip_out, 16 * HEADS)

            @block.vector
            def _(dve):
                own = Count(dv)

                def step(ins):
                    own.inc(ins)
                    own.after(dve)

                dve.wait_ge(s_dl, 16)
                step(dve.tensor_scalar(t[:, 2, :], dl[:], -1.0, None, ALU.mult))
                step(dve.tensor_tensor(t[:, 0, :], dl[:], t[:, 2, :], ALU.max))
                dve.wait_ge(s_exp, 1)
                step(dve.tensor_scalar(t[:, 2, :], t[:, 1, :], 2.0, None, ALU.add))
                step(dve.reciprocal(t[:, 3, :], t[:, 2, :]))
                step(dve.tensor_tensor(t[:, 3, :], t[:, 1, :], t[:, 3, :], ALU.mult))
                step(dve.tensor_tensor(t[:, 4, :], t[:, 3, :], t[:, 3, :], ALU.mult))
                step(dve.memset(t[:, 5, :], 2.0 / 17))
                for n in (15, 13, 11, 9, 7, 5, 3, 1):
                    step(dve.tensor_tensor(t[:, 6, :], t[:, 5, :], t[:, 4, :], ALU.mult))
                    step(dve.tensor_scalar(t[:, 5, :], t[:, 6, :], 2.0 / n, None, ALU.add))
                step(dve.tensor_tensor(t[:, 6, :], t[:, 5, :], t[:, 3, :], ALU.mult))
                step(dve.tensor_scalar(t[:, 2, :], dl[:], 0.0, None, ALU.min))
                dve.tensor_tensor(t[:, 7, :], t[:, 2, :], t[:, 6, :], ALU.subtract).then_inc(lg, 1)

                def row(sl):
                    dve.wait_ge(chunk_used, (sl + 1) * 2)
                    dve.tensor_tensor(brow[:, sl * H:(sl + 1) * H], pm[sl % 2][0:2, :], brow[:, sl * H:(sl + 1) * H],
                                      ALU.add).then_inc(row_ready, 1)

                def strips(h):
                    dve.wait_ge(e_ready, h + 1)
                    step(dve.scalar_tensor_tensor(ex[:, 0:XR], dist[:, XR:2 * XR], 0.0, ex[:, 0:XR],
                                                  ALU.is_le, ALU.mult))
                    step(dve.scalar_tensor_tensor(ex[:, XR:2 * XR], dist[:, 0:XR], 0.0, ex[:, XR:2 * XR],
                                                  ALU.is_le, ALU.mult))
                    step(dve.tensor_tensor(strip[:, h, 0:XR], ex[:, 0:XR], ex[:, XR:2 * XR], ALU.add))
                    dve.tensor_tensor(strip[:, h, XR:], ex[:, 2 * XR:2 * XR + CR], ex[:, 2 * XR + CR:],
                                      ALU.add).then_inc(strip_ready, 1)

                strips(0)
                strips(1)
                dve.wait_ge(s_b, 32)
                for sl in range(SL):
                    row(sl)
                    if sl + 2 < HEADS:
                        strips(sl + 2)
                dve.wait_ge(sq, NTOK)
                dve.tensor_scalar(ss[:], ss[:], 1.0 / D, EPS, ALU.mult, ALU.add).then_inc(ms, 1)
                dve.wait_ge(md_in, 2 * SL)
                dve.wait_ge(nm_in, 16)
                for s in range(2):
                    own.inc(dve.scalar_tensor_tensor(md[:, 2 * s + 1, :], md[:, 2 * s + 1, :], 1.0, nm[:],
                                                     ALU.add, ALU.mult))
                own.after(dve)
                dve.wait_ge(rs_ready, 1)

                def modulate(tb):
                    s = tb // NX
                    own.inc(dve.scalar_tensor_tensor(xt[:, tb, :], xt[:, tb, :], rs[:, tb:tb + 1], md[:, 2 * s + 1, :],
                                                     ALU.mult, ALU.mult))
                    own.after(dve)
                    dve.tensor_tensor(xt[:, tb, :], xt[:, tb, :], md[:, 2 * s, :], ALU.add).then_inc(h_ready, 1)

                modulate(0)
                for tb in range(NTOK):
                    if tb + 1 < NTOK:
                        modulate(tb + 1)
                    for half in range(2):
                        n = 2 * tb + half
                        dve.wait_ge(hi, n + 1)
                        dst = slice(4 * half, 4 * half + 4)
                        dve.tensor_tensor(hTl[:, dst, tb * P:(tb + 1) * P],
                                          pT[n % 4][:, :].rearrange("p (k c) -> p k c", k=4),
                                          f(hTh[:, dst, tb * P:(tb + 1) * P]), ALU.subtract).then_inc(lo, 1)


def three(pe, out, lhs, rhs, start, stop):
    pe.matmul(out, lhs[0], rhs[0], start=start, stop=False)
    pe.matmul(out, lhs[0], rhs[1], start=False, stop=False)
    return pe.matmul(out, lhs[1], rhs[0], start=False, stop=stop)


def phase_heads(nc, a, scr, ident, minus_half, cT, hTh, hTl, raw):
    CPS = 4
    NCH = 3 * CPS
    NSL = 2 * NTOK + NX
    MH = 5
    BEFORE = {4: 0, 5: 1, 8: 2, 9: 3, 10: 4}
    ITEMS = []
    for c in range(CPS, NCH + CPS):
        if c in BEFORE:
            ITEMS += [("m", BEFORE[c], q) for q in range(4)]
        ITEMS.append(("w", c, 0))
    NIT = len(ITEMS)
    RING = 4
    assert NIT % RING == 0 and CPS == RING
    at_item = {it: r for r, it in enumerate(ITEMS)}
    arrivals, seen = {}, [2] * RING
    for r, it in enumerate(ITEMS):
        seen[r % RING] += 2 if it[0] == "w" and it[1] >= NCH else 1
        arrivals[it] = seen[r % RING]
    per_turn = [n - 2 for n in seen]
    with ExitStack() as ctx:
        sb, sem, banks = alloc(nc, ctx, "heads")
        wh, wl = sb("wh", [P, RING, 2, H], F32R), sb("wl", [P, RING, 2, H], F32R)
        rope = sb("rope", [P, NX, 2, 2, DK // 4])
        rt = sb("rt", [P, 2, 4, 2, 2, DK // 4])
        qk = sb("qk", [P, NX, 2, 2, 2, DK // 4])
        kc = sb("kc", [P, NC, DK])
        qh, ql = sb("qh", [P, 2, SEQ], F32R), sb("ql", [P, 2, SEQ], F32R)
        kh, kl = sb("kh", [P, 2, NTOK * P], F32R), sb("kl", [P, 2, NTOK * P], F32R)
        vh, vl = sb("vh", [P, NTOK, DV], F32R), sb("vl", [P, NTOK, DV], F32R)
        gs, gn = sb("gs", [P, NX, DV]), sb("gn", [P, DV])
        strip = sb("strip", [P, STRIPS])
        af = sb("af", [P, 2, SEQ])
        ah, al = sb("ah", [P, 2, SEQ], F32R), sb("al", [P, 2, SEQ], F32R)
        og = sb("og", [P, NX, DV])
        bst, mv, pad = sb("bst", [P, NX, 6]), sb("mv", [P, NX, 4]), sb("pad", [1, 1])
        macc, mbias, mout = sb("macc", [P, 2, H]), sb("mbias", [P, H]), sb("mout", [1, H])
        ones, zero = sb("ones", [P, 1]), sb("zero", [P, D // 8])
        pj, pS = banks("pj", NTOK), banks("pS", 2)
        raw_in = [sem(f"raw_in{i}") for i in range(RING)]
        rope_in, strip_in, gn_in, set_ok = sem("rope_in"), sem("strip_in"), sem("gn_in"), sem("constants_set")
        hi, consumed, chunk_used, proj = sem("w_hi"), sem("raw_consumed"), sem("chunk_used"), sem("projected")
        rope_read, kc_read, rotated = sem("rope_read"), sem("ctx_key_read"), sem("rotated")
        v_hi, v_lo, g_read, g_ready = sem("v_hi"), sem("v_lo"), sem("gate_read"), sem("gate_ready")
        qkt, qkt_hi, qkt_lo = sem("qk_transposed"), sem("qkT_hi"), sem("qkT_lo")
        s_done, a_f, a_hi, a_lo = sem("scores_done"), sem("att_f32"), sem("att_hi"), sem("att_lo")
        av, o_done, o_read, ms, rstd = sem("av_done"), sem("o_done"), sem("o_read"), sem("o_var"), sem("o_rstd")
        normed, gated, dv, zero_out = sem("o_normed"), sem("gated"), sem("dve_steps"), sem("zero_out")
        bias_in, m_first, m_sum, m_row, m_out = (sem(n) for n in ("mod_bias_in", "mod_first", "mod_summed", "mod_row", "mod_out"))
        row_free, pool_pad = sem("mod_row_free"), sb("pool_pad", [1, 1])
        m_acc, m_step = sem("mod_accumulated"), sem("mod_steps")
        g_out = [sem(f"gated_out{i}") for i in range(NX)]
        w1 = a["ret_w_in"].rearrange("o (k p) n -> p (o k) n", p=P)
        wm = [a["w_mod"][lay].rearrange("(k p) n -> p k n", p=P) for lay in range(2)]
        xs_rows, ys_rows = (scr[n].rearrange("(b p) (q d) -> b p q d", p=P, q=8) for n in ("xs", "ys"))

        XZ, YZ = (NBLK + 1) // HEADS, -(-MAX_OVER // HEADS)
        assert HEADS * XZ == NBLK + 1 and HEADS * YZ >= MAX_OVER
        b_mod = a["b_mod"].rearrange("(o l) n -> o (l n)", o=1)

        def mod_at(h, v):
            return (0, h * (2 * H) + (2 * D + v * H)) if v < 2 else (1, h * (3 * H) + (v - 2) * H)

        with nc.Block() as block:

            @block.sync
            def _(sp):
                def load_w(h, c, slot):
                    s, cc = c % NCH // CPS, c % CPS
                    if s == 0:
                        for part in range(2):
                            sp.dma_start(raw[:, slot, :, part * DK:(part + 1) * DK],
                                         w1[:, 2 * cc:2 * cc + 2, bass.ds(h * DK + DK + part * D, DK)]
                                         ).then_inc(raw_in[slot], 16)
                    else:
                        sp.dma_start(raw[:, slot], w1[:, 2 * cc:2 * cc + 2, bass.ds(h * DV + 2 * s * D, DV)]
                                     ).then_inc(raw_in[slot], 16)

                for s in raw_in:
                    sp.nop().then_inc(s, 32)
                sp.dma_start(rope[:], a["rope"].rearrange("p t (a b c) -> p t a b c", a=2, b=2)).then_inc(rope_in, 16)
                sp.wait_ge(set_ok, 1)
                sp.dma_start(mbias[0:1, :], a["b_mod"][0:1, 2 * D:2 * D + H]).then_inc(bias_in, 16)
                with sp.Fori(0, HEADS) as h:
                    for r, it in enumerate(ITEMS):
                        sp.wait_ge(consumed, h * NIT + r + 1)
                        if it[0] == "w":
                            load_w(h, it[1], r % RING)
                        else:
                            lay, col = mod_at(h, it[1])
                            sp.dma_start(raw[:, r % RING], wm[lay][:, 2 * it[2]:2 * it[2] + 2, bass.ds(col, H)]
                                         ).then_inc(raw_in[r % RING], 16)
                            if it[2] == 2:
                                lay, col = mod_at(h, it[1] + 1) if it[1] + 1 < MH else mod_at(h + 1, 0)
                                sp.wait_ge(m_first, h * MH + it[1] + 1)
                                sp.dma_start(mbias[0:1, :], b_mod[:, bass.ds(lay * NMOD * D + col, H)]
                                             ).then_inc(bias_in, 16)
                        if it == ("w", 9, 0):
                            sp.wait_ge(g_ready, h * NX + 1)
                            sp.wait_ge(a_lo, h * NTOK + 1)
                            sp.dma_start(strip[:], scr["strips"][bass.ds(h, 1)].rearrange("o p w -> (o p) w")
                                         ).then_inc(strip_in, 16)
                            sp.dma_start(gn[:], a["ret_gn"][0:1, bass.ds(h * DV, DV)].to_broadcast([P, DV])
                                         ).then_inc(gn_in, 16)
                sp.wait_ge(bias_in, 16 * (HEADS * MH + 1))

            @block.tensor
            def _(pe):
                with pe.Fori(0, HEADS) as h:

                    def transpose_qk(t):
                        if t < NX:
                            pe.wait_ge(rotated, h * NX + t + 1)
                        else:
                            pe.wait_ge(kc_read, h * NC + t - NX + 1)
                        if t >= 2:
                            pe.wait_ge(qkt_lo, h * NTOK + t - 1)
                        for i in range(0 if t < NX else 2, 4):
                            src = (qk[:, t, i // 2, i % 2].rearrange("p b c -> p (b c)") if t < NX
                                   else kc[:, t - NX, (i - 2) * P:(i - 1) * P])
                            last = pe.transpose(pS[t % 2][:, i * P:(i + 1) * P], src, ident[:])
                        last.then_inc(qkt, 1)

                    def sum_mod(v):
                        if v >= 2:
                            pe.wait_ge(m_row, h * MH + v - 1)
                        pe.wait_ge(m_acc, h * MH + v + 1)
                        pe.matmul(pS[v % 2][0:1, :], ones[:], macc[:, v % 2], start=True, stop=True).then_inc(m_sum, 1)

                    for c in range(NCH):
                        s, cc = c // CPS, c % CPS
                        if c < CPS:
                            pe.wait_ge(consumed, h * NIT + c + 1)
                        else:
                            pe.wait_ge(consumed, h * NIT + RING + at_item["w", c, 0] + 1)
                        for t in range(NX if s == 2 else NTOK):
                            if cc == 0:
                                if s == 0 and t < NX:
                                    pe.wait_ge(o_read, h * NX + t + 1)
                                elif s == 1 and t < NX:
                                    pe.wait_ge(rope_read, h * NX + t + 1)
                                elif s == 1:
                                    pe.wait_ge(kc_read, h * NC + t - NX + 1)
                                elif s == 2:
                                    pe.wait_ge(v_lo, h * NTOK + t + 1)
                            c0 = DK if s == 0 and t >= NX else 0
                            for k in range(2):
                                kk = 2 * cc + k
                                last = three(pe, pj[t][:, c0:H],
                                             (hTh[:, kk, t * P:(t + 1) * P], hTl[:, kk, t * P:(t + 1) * P]),
                                             (wh[:, cc, k, c0:H], wl[:, cc, k, c0:H]),
                                             kk == 0, kk == KT - 1)
                            if cc == CPS - 1:
                                last.then_inc(proj, 1)
                        if cc < CPS - 1:
                            last.then_inc(chunk_used, 1)
                        if c in (2, 4, 5, 6, 7):
                            sum_mod({2: 0, 4: 1, 5: 2, 6: 3, 7: 4}[c])
                        if c == 8:
                            pe.wait_ge(m_row, h * MH + MH)
                        if 8 <= c < 11:
                            transpose_qk(2 * (c - 8))
                            transpose_qk(2 * (c - 8) + 1)
                    pe.wait_ge(qkt_lo, h * NTOK + NTOK)
                    pe.wait_ge(v_lo, h * NTOK + NTOK)

                    def scores(j):
                        for kk in range(2):
                            last = three(pe, pS[j % 2][:, :],
                                         tuple(m[:, kk, j * P:(j + 1) * P] for m in (kh, kl)),
                                         tuple(m[:, kk] for m in (qh, ql)), kk == 0, kk == 1)
                        last.then_inc(s_done, 1)

                    def weighted(j):
                        pe.wait_ge(a_lo, h * NTOK + j + 2)
                        for i in range(NX):
                            if j == 0:
                                pe.wait_ge(g_read, h * NX + i + 1)
                            last = three(pe, pj[i][:, :], tuple(m[:, j % 2, i * P:(i + 1) * P] for m in (ah, al)),
                                         (vh[:, j], vl[:, j]), j == 0, j == NTOK - 1)
                            if j == NTOK - 1:
                                last.then_inc(o_done, 1)
                        if j < NTOK - 1:
                            last.then_inc(av, 1)

                    scores(0)
                    for j in range(1, NTOK):
                        scores(j)
                        weighted(j - 1)
                    weighted(NTOK - 1)

            def split_hi(act, h, c):
                s, cc = c // CPS, c % CPS
                if c < CPS:
                    act.wait_ge(raw_in[cc], 32)
                else:
                    it = ("w", c, 0)
                    slot = at_item[it] % RING
                    act.wait_ge(raw_in[slot], h * (16 * per_turn[slot]) + 16 * arrivals[it])
                    if cc < CPS - 1:
                        act.wait_ge(chunk_used, h * (NCH - 3) + (s - 1) * (CPS - 1) + cc + 1)
                    else:
                        act.wait_ge(proj, h * NSL + (NTOK, 2 * NTOK, NSL)[s - 1])
                slot = cc if c < CPS else at_item["w", c, 0] % RING
                act.activation(wh[:, cc], raw[:, slot], ACT.Copy).then_inc(hi, 1)

            @block.scalar
            def _(act):
                for s in g_out:
                    act.nop().then_inc(s, 1)
                for c in range(CPS):
                    split_hi(act, 0, c)
                with act.Fori(0, HEADS) as h:

                    def qkT_hi(t):
                        act.wait_ge(qkt, h * NTOK + t + 1)
                        cols = slice(t * P, (t + 1) * P)
                        if t < NX:
                            act.activation(qh[:, :, cols], pS[t % 2][:, 0:2 * P].rearrange("p (i c) -> p i c", c=P),
                                           ACT.Copy)
                        act.activation(kh[:, :, cols], pS[t % 2][:, 2 * P:].rearrange("p (i c) -> p i c", c=P),
                                       ACT.Copy).then_inc(qkt_hi, 1)

                    def att_hi(j):
                        act.wait_ge(a_f, h * NTOK + j + 1)
                        if j >= 2:
                            act.wait_ge(av, h * (NTOK - 1) + j - 1)
                        act.activation(ah[:, j % 2], af[:, j % 2], ACT.Copy).then_inc(a_hi, 1)

                    for c in (4, 5, 6):
                        split_hi(act, h, c)
                    for t in range(NX, NTOK):
                        act.wait_ge(proj, h * NSL + t + 1)
                        act.activation(kc[:, t - NX], pj[t][:, DK:H], ACT.Copy).then_inc(kc_read, 1)
                    for c in (7, 8, 9, 10):
                        split_hi(act, h, c)
                    for t in range(NTOK):
                        act.wait_ge(proj, h * NSL + NTOK + t + 1)
                        act.activation(vh[:, t], pj[t][:, :], ACT.Copy).then_inc(v_hi, 1)
                    for n, c in enumerate((11, 12, 13)):
                        split_hi(act, h, c)
                        qkT_hi(2 * n)
                        qkT_hi(2 * n + 1)
                    split_hi(act, h, 14)
                    for t in range(NX):
                        act.wait_ge(proj, h * NSL + 2 * NTOK + t + 1)
                        act.activation(gs[:, t], pj[t][:, :], ACT.Silu).then_inc(g_read, 1)
                    att_hi(0)
                    split_hi(act, h, 15)
                    for j in range(1, NTOK):
                        att_hi(j)
                    for i in range(NX):
                        act.wait_ge(g_out[i], h * 16 + 1)
                        act.wait_ge(o_done, h * NX + i + 1)
                        act.activation(og[:, i], pj[i][:, :], ACT.Copy).then_inc(o_read, 1)
                    for i in range(NX):
                        act.wait_ge(gated, h * NX + i + 1)
                        act.dma_start(scr["gated"][i * P:(i + 1) * P, bass.ds(h * DV, DV)], og[:, i]
                                      ).then_inc(g_out[i], 16)
                for s in g_out:
                    act.wait_ge(s, 16 * HEADS + 1)

            @block.gpsimd
            def _(pool):
                pool.memset(ones[:], 1.0)
                pool.memset(zero[:], 0.0)
                pool.memset(mbias[:], 0.0).then_inc(set_ok, 1)
                pool.nop().then_inc(g_ready, 1)
                pool.nop().then_inc(row_free, 1)
                pool.wait_ge(set_ok, 1)
                src = zero[:].rearrange("p (q d) -> p q d", q=1).to_broadcast([P, 8, D // 8])
                pool.dma_start(xs_rows[HEADS * XZ], src).then_inc(zero_out, 16)
                with pool.Fori(0, HEADS) as h:

                    def store_mod(v):
                        pool.wait_ge(m_row, h * MH + v + 1)
                        lay, col = mod_at(h, v)
                        pool.dma_start(scr["mod"][lay, 0:1, bass.ds(col, H)], mout[:]).then_inc(m_out, 16)
                        pool.wait_ge(m_out, h * (16 * MH) + 16 * v + 16)
                        pool.tensor_tensor(pool_pad[:], ones[0:1, :], ones[0:1, :], ALU.mult).then_inc(row_free, 1)

                    store_mod(0)
                    for t in range(NX):
                        pool.wait_ge(rope_read, h * NX + t + 1)
                        m = rt[:, t % 2]
                        pool.tensor_tensor(qk[:, t, :, :, 0], m[:, 0], m[:, 1], ALU.subtract)
                        pool.tensor_tensor(qk[:, t, :, :, 1], m[:, 2], m[:, 3], ALU.add).then_inc(rotated, 1)
                    for v in range(1, MH):
                        store_mod(v)
                    pool.wait_ge(gn_in, h * 16 + 16)
                    for t in range(NX):
                        pool.wait_ge(g_read, h * NX + t + 1)
                        pool.tensor_tensor(gs[:, t], gs[:, t], gn[:], ALU.mult).then_inc(g_ready, 1)
                    for b in range(XZ):
                        pool.dma_start(xs_rows[bass.ds(h * XZ + b, 1)].rearrange("o p q d -> (o p) q d"), src
                                       ).then_inc(zero_out, 16)
                    for b in range(YZ):
                        pool.dma_start(ys_rows[bass.ds(h * YZ + NBLK + 1 - HEADS * YZ + b, 1)]
                                       .rearrange("o p q d -> (o p) q d"), src).then_inc(zero_out, 16)
                    for i in range(NX):
                        pool.wait_ge(ms, h * NX + i + 1)
                        pool.tensor_tensor(mv[:, i, 3:4], mv[:, i, 2:3], minus_half[:, 0:1], ALU.pow
                                           ).then_inc(rstd, 1)
                    for i in range(NX):
                        pool.wait_ge(normed, h * NX + i + 1)
                        pool.tensor_tensor(og[:, i], og[:, i], gs[:, i], ALU.mult).then_inc(gated, 1)
                pool.wait_ge(zero_out, 16 * (1 + HEADS * (XZ + YZ)))
                pool.wait_ge(m_out, 16 * HEADS * MH)

            @block.vector
            def _(dve):
                def split_lo(h, c):
                    dve.wait_ge(hi, h * NCH + c + 1)
                    slot = c if c < CPS else at_item["w", c, 0] % RING
                    dve.tensor_tensor(wl[:, c % CPS], raw[:, slot], f(wh[:, c % CPS]), ALU.subtract
                                      ).then_inc(consumed, 1)

                dve.nop().then_inc(o_read, NX)
                dve.nop().then_inc(a_lo, 1)
                for c in range(CPS):
                    split_lo(0, c)
                dve.wait_ge(rope_in, 16)
                with dve.Fori(0, HEADS) as h:

                    def weigh_mod(v):
                        dve.wait_ge(bias_in, h * (16 * MH) + 16 * v + 16)
                        steps = 0
                        for k in range(KT):
                            it = ("m", v, k // 2)
                            slot = at_item[it] % RING
                            if k % 2 == 0:
                                dve.wait_ge(raw_in[slot], h * (16 * per_turn[slot]) + 16 * arrivals[it])
                            if k == 0:
                                if v >= 2:
                                    dve.wait_ge(m_sum, h * MH + v - 1)
                            elif k == 1:
                                dve.wait_ge(m_first, h * MH + v + 1)
                            elif k % 2:
                                dve.wait_ge(m_step, h * (3 * MH) + v * 3 + k // 2)
                            else:
                                dve.wait_ge(consumed, h * NIT + RING + at_item[it])
                            ins = dve.scalar_tensor_tensor(macc[:, v % 2], raw[:, slot, k % 2], cT[:, k:k + 1],
                                                           mbias[:] if k == 0 else macc[:, v % 2], ALU.mult, ALU.add)
                            if k == 0:
                                ins.then_inc(m_first, 1)
                            elif k % 2 == 0:
                                ins.then_inc(m_step, 1)
                            elif k < KT - 1:
                                ins.then_inc(consumed, 1)
                            else:
                                ins.then_inc(m_acc, 1)
                        dve.wait_ge(m_acc, h * MH + v + 1)
                        dve.memset(pad[:], 0.0).then_inc(consumed, 1)

                    def row_mod(v):
                        dve.wait_ge(m_sum, h * MH + v + 1)
                        dve.wait_ge(row_free, h * MH + v + 1)
                        dve.tensor_copy(mout[:], pS[v % 2][0:1, :]).then_inc(m_row, 1)

                    def rotate(t):
                        dve.wait_ge(proj, h * NSL + t + 1)
                        if t >= 2:
                            dve.wait_ge(rotated, h * NX + t - 1)
                        m = rt[:, t % 2]
                        src = pj[t][:, :].rearrange("p (q s b c) -> p q s b c", q=2, s=2, b=2)
                        cos = rope[:, t, 0:1].to_broadcast([P, 2, 2, DK // 4])
                        sin = rope[:, t, 1:2].to_broadcast([P, 2, 2, DK // 4])
                        dve.tensor_tensor(m[:, 0], src[:, :, :, 0], cos, ALU.mult)
                        dve.tensor_tensor(m[:, 1], src[:, :, :, 1], sin, ALU.mult)
                        dve.tensor_tensor(m[:, 2], src[:, :, :, 0], sin, ALU.mult)
                        dve.tensor_tensor(m[:, 3], src[:, :, :, 1], cos, ALU.mult).then_inc(rope_read, 1)

                    def qkT_lo(t):
                        dve.wait_ge(qkt_hi, h * NTOK + t + 1)
                        cols = slice(t * P, (t + 1) * P)
                        if t < NX:
                            dve.tensor_tensor(ql[:, :, cols], pS[t % 2][:, 0:2 * P].rearrange("p (i c) -> p i c", c=P),
                                              f(qh[:, :, cols]), ALU.subtract)
                        dve.tensor_tensor(kl[:, :, cols], pS[t % 2][:, 2 * P:].rearrange("p (i c) -> p i c", c=P),
                                          f(kh[:, :, cols]), ALU.subtract).then_inc(qkt_lo, 1)

                    def att(j):
                        at = XO - j * P if j < NX else XR + P - (j - NX) * P
                        dve.wait_ge(s_done, h * NTOK + j + 1)
                        dve.scalar_tensor_tensor(af[:, j % 2], pS[j % 2][:, :], DK ** -0.5, strip[:, at:at + SEQ],
                                                 ALU.mult, ALU.mult).then_inc(a_f, 1)
                        dve.wait_ge(a_hi, h * NTOK + j + 1)
                        dve.tensor_tensor(al[:, j % 2], af[:, j % 2], f(ah[:, j % 2]), ALU.subtract
                                          ).then_inc(a_lo, 1)

                    weigh_mod(0)
                    split_lo(h, 4)
                    weigh_mod(1)
                    split_lo(h, 5)
                    row_mod(0)
                    split_lo(h, 6)
                    for t in range(NX):
                        rotate(t)
                    split_lo(h, 7)
                    weigh_mod(2)
                    row_mod(1)
                    split_lo(h, 8)
                    weigh_mod(3)
                    row_mod(2)
                    split_lo(h, 9)
                    weigh_mod(4)
                    split_lo(h, 10)
                    row_mod(3)
                    for t in range(NTOK):
                        dve.wait_ge(v_hi, h * NTOK + t + 1)
                        dve.tensor_tensor(vl[:, t], pj[t][:, :], f(vh[:, t]), ALU.subtract).then_inc(v_lo, 1)
                    row_mod(4)
                    for n, c in enumerate((11, 12, 13)):
                        split_lo(h, c)
                        qkT_lo(2 * n)
                        qkT_lo(2 * n + 1)
                    split_lo(h, 14)
                    dve.wait_ge(strip_in, h * 16 + 16)
                    att(0)
                    split_lo(h, 15)
                    for j in range(1, NTOK):
                        att(j)
                    for i in range(NX):
                        dve.wait_ge(o_read, h * NX + NX + i + 1)
                        dve.bn_stats(bst[:, i], og[:, i]).then_inc(dv, 1)
                    dve.wait_ge(dv, h * (2 * NX) + NX)
                    dve.memset(pad[:], 0.0)
                    for i in range(NX):
                        dve.bn_aggr(mv[:, i, 0:2], bst[:, i]).then_inc(dv, 1)
                    for i in range(NX):
                        dve.wait_ge(dv, h * (2 * NX) + NX + i + 1)
                        dve.tensor_scalar(mv[:, i, 2:3], mv[:, i, 1:2], EPS, None, ALU.add).then_inc(ms, 1)
                    for i in range(NX):
                        dve.wait_ge(rstd, h * NX + i + 1)
                        dve.tensor_scalar(og[:, i], og[:, i], mv[:, i, 0:1], mv[:, i, 3:4],
                                          ALU.subtract, ALU.mult).then_inc(normed, 1)


def project_residual(nc, a, scr, tag, layer, kt, w_view, gT, x_src, res, tok, sc, ident, minus_half, rows=None):
    RING = 4
    with ExitStack() as ctx:
        sb, sem, banks = alloc(nc, ctx, tag)
        raw = sb("raw", [P, RING, D])
        wh, wl = sb("wh", [P, RING, D], F32R), sb("wl", [P, RING, D], F32R)
        gate = sb("gate", [P, D])
        xin = sb("xin", [P, NX, D]) if x_src is not None else None
        md, nm, junk = sb("md", [P, 2, D]), sb("nm", [P, D]), sb("junk", [P, D])
        ss, rs = sb("ss", [P, NX]), sb("rs", [P, NX])
        fT, rw = sb("fT", [P, 2, KT, P]), sb("rw", [P, KT, NE])
        acc = banks("acc", 2 * NX)
        raw_in = [sem(f"raw_in{i}") for i in range(RING)]
        rows_in = [sem(f"rows_in{t}") for t in range(NX)]
        gate_in, x_in = sem("gate_in"), sem("x_in")
        tr, g_hi, g_lo = sem("transposed"), sem("g_hi"), sem("g_lo")
        md_in, res_ok, sq, ms, rs_ok = (sem(n) for n in ("mod_in", "residual", "squares", "mean_square", "rs_ready"))
        rw_in, tok_ok, tok_t, fT_ok, logit = (sem(n) for n in ("router_in", "tok_ready", "tok_transposed", "fT_ready", "logits"))
        hi, lo, used, done, dv = sem("w_hi"), sem("w_lo"), sem("chunk_used"), sem("acc_done"), sem("dve_steps")
        groups = NX * kt // 4 if rows is not None else 0
        with nc.Block() as block:

            @block.sync
            def _(sp):
                if rows is not None:
                    for t in range(NX):
                        sp.dma_start(rows[:, t], scr["gated"][t * P:(t + 1) * P, :]).then_inc(rows_in[t], 16)
                for k in range(kt):
                    if k >= RING:
                        sp.wait_ge(lo, k - RING + 1)
                    sp.dma_start(raw[:, k % RING], w_view[:, k, :]).then_inc(raw_in[k % RING], 16)
                    if k == 3:
                        sp.dma_start(gate[:], scr["mod"][layer, 0:1, 2 * D:3 * D].to_broadcast([P, D])
                                     ).then_inc(gate_in, 16)
                        if xin is not None:
                            sp.dma_start(xin[:], x_src.rearrange("(t p) d -> p t d", p=P)).then_inc(x_in, 16)
                for v in range(2):
                    sp.dma_start(md[:, v], scr["mod"][layer, 0:1, (3 + v) * D:(4 + v) * D].to_broadcast([P, D])
                                 ).then_inc(md_in, 16)
                sp.dma_start(nm[:], a["norm_ffn"][layer:layer + 1, :].to_broadcast([P, D])).then_inc(md_in, 16)
                sp.dma_start(rw[:], a["router_w"].rearrange("(k p) e -> p k e", p=P)).then_inc(rw_in, 16)

            @block.gpsimd
            def _(pool):
                for t in range(NX):
                    pool.wait_ge(ms, t + 1)
                    pool.tensor_tensor(rs[:, t:t + 1], ss[:, t:t + 1], minus_half[:, 0:1], ALU.pow).then_inc(rs_ok, 1)

            @block.tensor
            def _(pe):
                for n in range(groups):
                    t, q = n // (kt // 4), n % (kt // 4)
                    if q == 0:
                        pe.wait_ge(rows_in[t], 16)
                    if n >= 2 * NX:
                        pe.wait_ge(g_lo, n - 2 * NX + 1)
                    for k in range(4):
                        last = pe.transpose(acc[n % (2 * NX)][:, k * P:(k + 1) * P],
                                            rows[:, t, (4 * q + k) * P:(4 * q + k + 1) * P], ident[:])
                    last.then_inc(tr, 1)
                if groups:
                    pe.wait_ge(g_lo, groups)

                def multiply(k, t):
                    for half in range(2):
                        cols = slice(half * H, (half + 1) * H)
                        last = three(pe, acc[2 * t + half][:, :], tuple(m[:, k, t * P:(t + 1) * P] for m in gT),
                                     (wh[:, k % RING, cols], wl[:, k % RING, cols]), k == 0, k == kt - 1)
                    return last

                for k in range(kt - RING):
                    pe.wait_ge(lo, k + 1)
                    for t in range(NX):
                        last = multiply(k, t)
                    last.then_inc(used, 1)
                def transpose_tok(t):
                    pe.wait_ge(tok_ok, t + 1)
                    for half in range(2):
                        for k in range(4):
                            last = pe.transpose(acc[2 * t + half][:, k * P:(k + 1) * P],
                                                tok[:, t, (4 * half + k) * P:(4 * half + k + 1) * P], ident[:])
                        last.then_inc(tok_t, 1)

                def logits(t):
                    pe.wait_ge(fT_ok, 2 * t + 2)
                    for k in range(KT):
                        last = pe.matmul(acc[2 * t][:, 0:NE], fT[:, t % 2, k], rw[:, k], start=k == 0, stop=k == KT - 1)
                    last.then_inc(logit, 1)

                for t in range(NX):
                    for k in range(kt - RING, kt):
                        if t == 0:
                            pe.wait_ge(lo, k + 1)
                        last = multiply(k, t)
                    last.then_inc(done, 1)
                    if t == NX - 2:
                        transpose_tok(0)
                pe.wait_ge(rw_in, 16)
                for t in range(1, NX):
                    transpose_tok(t)
                    logits(t - 1)
                logits(NX - 1)

            @block.scalar
            def _(act):
                for n in range(groups):
                    t, q = n // (kt // 4), n % (kt // 4)
                    act.wait_ge(tr, n + 1)
                    act.activation(gT[0][:, 4 * q:4 * q + 4, t * P:(t + 1) * P],
                                   acc[n % (2 * NX)][:, :].rearrange("p (k c) -> p k c", k=4), ACT.Copy
                                   ).then_inc(g_hi, 1)
                for k in range(kt):
                    act.wait_ge(raw_in[k % RING], 16 * (k // RING + 1))
                    if k >= RING:
                        act.wait_ge(used, k - RING + 1)
                    act.activation(wh[:, k % RING], raw[:, k % RING], ACT.Copy).then_inc(hi, 1)

                def squares(t):
                    act.wait_ge(res_ok, t + 1)
                    if t:
                        act.wait_ge(sq, t)
                    act.activation(junk[:], res[:, t], ACT.Square, accum_out=ss[:, t:t + 1]).then_inc(sq, 1)

                def tok_T(t):
                    for half in range(2):
                        act.wait_ge(tok_t, 2 * t + half + 1)
                        if t >= 2:
                            act.wait_ge(logit, t - 1)
                        act.activation(fT[:, t % 2, 4 * half:4 * half + 4].rearrange("p k c -> p (k c)"),
                                       acc[2 * t + half][:, :], ACT.Copy).then_inc(fT_ok, 1)

                for t in range(NX - 1):
                    squares(t)
                tok_T(0)
                squares(NX - 1)
                for t in range(1, NX):
                    tok_T(t)
                for t in range(NX):
                    act.wait_ge(logit, t + 1)
                    act.activation(sc[:, t], acc[2 * t][:, 0:NE], ACT.Sigmoid)

            @block.vector
            def _(dve):
                own = Count(dv)
                for n in range(groups):
                    t, q = n // (kt // 4), n % (kt // 4)
                    dve.wait_ge(g_hi, n + 1)
                    at = (slice(None), slice(4 * q, 4 * q + 4), slice(t * P, (t + 1) * P))
                    dve.tensor_tensor(gT[1][at], acc[n % (2 * NX)][:, :].rearrange("p (k c) -> p k c", k=4),
                                      f(gT[0][at]), ALU.subtract).then_inc(g_lo, 1)
                for k in range(kt):
                    dve.wait_ge(hi, k + 1)
                    dve.tensor_tensor(wl[:, k % RING], raw[:, k % RING], f(wh[:, k % RING]), ALU.subtract
                                      ).then_inc(lo, 1)
                dve.wait_ge(gate_in, 16)
                if xin is not None:
                    dve.wait_ge(x_in, 16)
                dve.wait_ge(md_in, 48)
                own.inc(dve.scalar_tensor_tensor(md[:, 1], md[:, 1], 1.0, nm[:], ALU.add, ALU.mult))
                own.after(dve)

                def residual(t):
                    dve.wait_ge(done, t + 1)
                    for half in range(2):
                        own.inc(dve.tensor_tensor(raw[:, t, half * H:(half + 1) * H], acc[2 * t + half][:, :],
                                                  gate[:, half * H:(half + 1) * H], ALU.mult))
                    own.after(dve)
                    x_old = xin[:, t] if xin is not None else res[:, t]
                    dve.tensor_tensor(res[:, t], x_old, raw[:, t], ALU.add).then_inc(res_ok, 1)

                def norm(t):
                    dve.wait_ge(sq, t + 1)
                    dve.tensor_scalar(ss[:, t:t + 1], ss[:, t:t + 1], 1.0 / D, EPS, ALU.mult, ALU.add).then_inc(ms, 1)
                    dve.wait_ge(rs_ok, t + 1)
                    own.inc(dve.scalar_tensor_tensor(tok[:, t], res[:, t], rs[:, t:t + 1], md[:, 1], ALU.mult, ALU.mult))
                    own.after(dve)
                    dve.tensor_tensor(tok[:, t], tok[:, t], md[:, 0], ALU.add).then_inc(tok_ok, 1)

                residual(0)
                for t in range(1, NX):
                    residual(t)
                    norm(t - 1)
                norm(NX - 1)


def phase_route(nc, a, scr, layer, tok, sc, dest, wk, table, raw):
    with ExitStack() as ctx:
        sb, sem, banks = alloc(nc, ctx, f"route{layer}")
        bias, order = sb("bias", [P, NE]), sb("order", [P, NE + NG + MAX_OVER + 1])
        below = sb("below", [P, 2, P])
        sel, oh0, oh1, tmp, both = (sb(n, [P, NX, NE]) for n in ("sel", "oh0", "oh1", "tmp", "both"))
        rank = sb("rank", [P, NX, NE])
        pair = sb("pair", [P, NX * NG, 6])
        gsum, gone, gkey = (sb(n, [P, NX, NG]) for n in ("gsum", "gone", "gkey"))
        mx, wf, df = sb("mx", [P, NX, 1]), sb("wf", [P, NX, 2]), sb("df", [P, NX, 2])
        cnt = sb("cnt", [P, 8, NE])
        cmp_ = sb("cmp", [P, MAX_OVER, NE])
        tf = sb("tf", [P, NBLK + 2])
        pL = banks("pL", 2)
        in_c = sem("consts_in")
        chosen, ranked, placed, dv = sem("chosen"), sem("ranked"), sem("placed"), sem("dve_steps")
        sent, w_in = sem("rows_sent"), sem("weights_in")
        with nc.Block() as block:

            @block.sync
            def _(sp):
                sp.dma_start(bias[:], a["router_bias"].rearrange("(o e) -> o e", o=1).to_broadcast([P, NE])
                             ).then_inc(in_c, 16)
                sp.dma_start(order[:], a["order"].to_broadcast([P, NE + NG + MAX_OVER + 1])).then_inc(in_c, 16)
                sp.dma_start(below[:], a["below"].rearrange("s p c -> p s c")).then_inc(in_c, 16)
                weights = expert_weights(a, layer)
                for c in range(RAW):
                    sp.dma_start(raw[:, c], weights[c // KT][0, :, c % KT, :]).then_inc(w_in, 16)
                sp.wait_ge(w_in, 16 * RAW)

            @block.gpsimd
            def _(pool):
                pool.wait_ge(placed, 1)
                for t in range(NX):
                    for s in range(2):
                        pool.indirect_dma_start(
                            out=scr["xs"], out_offset=bass.IndirectOffsetOnAxis(ap=dest[:, 0, s, t:t + 1].bitcast(U32), axis=0),
                            in_=tok[:, t], in_offset=None, bounds_check=(NBLK + 1) * P - 1, oob_is_err=False
                        ).then_inc(sent, 16)
                pool.wait_ge(sent, 16 * 2 * NX)

            @block.tensor
            def _(pe):
                pe.wait_ge(in_c, 48)
                pe.wait_ge(chosen, 1)
                for t in range(NX):
                    for u in range(t + 1):
                        last = pe.matmul(pL[0][:, t * NE:(t + 1) * NE], below[:, 0 if u == t else 1], both[:, u],
                                         start=u == 0, stop=u == t)
                for u in range(NX):
                    last = pe.matmul(pL[1][:, 0:NE], below[:, 1], both[:, u], start=u == 0, stop=u == NX - 1)
                last.then_inc(ranked, 1)

            @block.vector
            def _(dve):
                own = Count(dv)

                def step(ins):
                    own.inc(ins)
                    own.after(dve)

                dve.wait_ge(in_c, 48)
                flat = [P, NX * NG, EPG]
                step(dve.tensor_tensor(sel[:], sc[:], bias[:].rearrange("p (o e) -> p o e", o=1).to_broadcast([P, NX, NE]),
                                       ALU.add))
                s4 = sel[:].rearrange("p t (g e) -> p (t g) e", e=EPG)
                pairs = [(i, j) for i in range(EPG) for j in range(i + 1, EPG)]
                for n, (i, j) in enumerate(pairs):
                    own.inc(dve.tensor_tensor(pair[:, :, n:n + 1], s4[:, :, i:i + 1], s4[:, :, j:j + 1], ALU.add))
                own.after(dve)
                step(dve.tensor_reduce(gsum[:].rearrange("p t g -> p (t g)"), pair[:], AX.X, ALU.max))

                def first_largest(out, v, key, n, first):
                    step(dve.tensor_reduce(mx[:].rearrange("p t o -> p (t o)"), v, AX.X, ALU.max))
                    step(dve.tensor_tensor(key, v, mx[:].to_broadcast([P, NX, n]), ALU.is_ge))
                    step(dve.tensor_tensor(key, key, first.rearrange("p (o e) -> p o e", o=1).to_broadcast([P, NX, n]),
                                           ALU.mult))
                    step(dve.tensor_reduce(mx[:].rearrange("p t o -> p (t o)"), key, AX.X, ALU.max))
                    step(dve.tensor_tensor(out, key, mx[:].to_broadcast([P, NX, n]), ALU.is_equal))

                first_largest(gone[:], gsum[:], gkey[:], NG, order[:, NE:NE + NG])
                step(dve.tensor_scalar(gkey[:], gone[:], BIG, -BIG, ALU.mult, ALU.add))
                step(dve.tensor_tensor(s4, s4, gkey[:].rearrange("p t (g o) -> p (t g) o", o=1).to_broadcast(flat), ALU.add))
                for s, oh in enumerate((oh0, oh1)):
                    first_largest(oh[:], sel[:], tmp[:], NE, order[:, 0:NE])
                    if s == 0:
                        step(dve.scalar_tensor_tensor(sel[:], oh[:], -2 * BIG, sel[:], ALU.mult, ALU.add))
                    step(dve.tensor_tensor(tmp[:], oh[:], sc[:], ALU.mult))
                    step(dve.tensor_reduce(wf[:, :, s], tmp[:], AX.X, ALU.add))
                dve.tensor_tensor(both[:], oh0[:], oh1[:], ALU.add).then_inc(chosen, 1)
                step(dve.tensor_tensor(mx[:], wf[:, :, 0:1], wf[:, :, 1:2], ALU.add))
                step(dve.reciprocal(mx[:], mx[:]))
                step(dve.tensor_tensor(wk[:], wf[:], mx[:].to_broadcast([P, NX, 2]), ALU.mult))
                dve.wait_ge(ranked, 1)
                step(dve.tensor_copy(rank[:].rearrange("p t e -> p (t e)"), pL[0][:, 0:NX * NE]))
                total, more, end, other = (cnt[:, i] for i in range(4))
                step(dve.tensor_copy(total, pL[1][:, 0:NE]))
                step(dve.tensor_scalar(more, total, float(P), None, ALU.is_gt))
                for m in range(2, SEQ // P):
                    step(dve.scalar_tensor_tensor(more, total, float(m * P), more, ALU.is_gt, ALU.add))
                step(dve.tensor_copy(end, more))
                src, dst = end, other
                for d in (1, 2, 4, 8):
                    own.inc(dve.tensor_copy(dst[:, 0:d], src[:, 0:d]))
                    step(dve.tensor_tensor(dst[:, d:], src[:, d:], src[:, 0:NE - d], ALU.add))
                    src, dst = dst, src
                end = src
                base, over = cnt[:, 4], cnt[:, 5]
                step(dve.tensor_scalar(base, order[:, 0:NE], -float(P), float(NE * P), ALU.mult, ALU.add))
                step(dve.tensor_tensor(over, end, more, ALU.subtract))
                step(dve.tensor_scalar(over, over, float(P), float(NE * P - P), ALU.mult, ALU.add))
                step(dve.tensor_tensor(over, over, base, ALU.subtract))
                wide = lambda v: v.rearrange("p (o e) -> p o e", o=1).to_broadcast([P, NX, NE])
                step(dve.tensor_scalar(tmp[:], rank[:], float(P), None, ALU.is_ge))
                step(dve.tensor_tensor(tmp[:], tmp[:], wide(over), ALU.mult))
                step(dve.tensor_tensor(tmp[:], tmp[:], wide(base), ALU.add))
                step(dve.tensor_tensor(rank[:], rank[:], tmp[:], ALU.add))
                for s, oh in enumerate((oh0, oh1)):
                    step(dve.tensor_tensor(tmp[:], oh[:], rank[:], ALU.mult))
                    step(dve.tensor_reduce(df[:, :, s], tmp[:], AX.X, ALU.add))
                dve.tensor_copy(dest[:, 0], df[:].rearrange("p t s -> p s t")).then_inc(placed, 1)
                dve.wait_ge(placed, 1)
                step(dve.tensor_scalar(df[:], df[:], float(P), None, ALU.add))
                step(dve.tensor_copy(dest[:, 1], df[:].rearrange("p t s -> p s t")))
                step(dve.tensor_scalar(tf[:, 0:NE], order[:, 0:NE], -1.0, float(NE), ALU.mult, ALU.add))
                step(dve.tensor_tensor(cmp_[:], end.rearrange("p (o e) -> p o e", o=1).to_broadcast([P, MAX_OVER, NE]),
                                       order[:, NE + NG:NE + NG + MAX_OVER].rearrange("p (b o) -> p b o", o=1
                                                                                      ).to_broadcast([P, MAX_OVER, NE]),
                                       ALU.is_le))
                step(dve.tensor_reduce(tf[:, NE:NBLK], cmp_[:], AX.X, ALU.add))
                step(dve.tensor_scalar(tf[:, NE:NBLK], tf[:, NE:NBLK], float(NE - 1), None, ALU.min))
                step(dve.memset(tf[:, NBLK:NBLK + 1], 0.0))
                step(dve.tensor_scalar(tf[:, NBLK + 1:], end[:, NE - 1:NE], float(NE), None, ALU.add))
                step(dve.tensor_copy(table[:], tf[:]))


RAW, RING = 12, 8
AHEAD = 3


def expert_weights(a, layer):
    return [a[n][layer].rearrange("e (k p) n -> e p k n", p=P) for n in ("moe_w_gate", "moe_w_up", "moe_w_down")]


def phase_experts(nc, a, scr, ident, layer, table, raw):
    NCH = 3 * KT
    GATE, UP, DOWN = range(3)
    ORDER = ([(GATE, k, 0) for k in range(AHEAD, KT)] + [(UP, k, 0) for k in range(KT)]
             + [(GATE, k, 1) for k in range(AHEAD)] + [(DOWN, k, 0) for k in range(KT)])
    at = {o: i for i, o in enumerate(ORDER)}
    GATE_END, UP_MID, UP_END = at[GATE, KT - 1, 0], at[UP, KT // 2 - 1, 0], at[UP, KT - 1, 0]
    with ExitStack() as ctx:
        sb, sem, banks = alloc(nc, ctx, f"moe{layer}")
        wh, wl = sb("wh", [P, RING, D], F32R), sb("wl", [P, RING, D], F32R)
        xb, sg, hs, yb = sb("xb", [P, D]), sb("sg", [P, D]), sb("hs", [P, D]), sb("yb", [P, D])
        xh, xl = sb("xh", [P, KT, P], F32R), sb("xl", [P, KT, P], F32R)
        hh, hl = sb("hh", [P, KT, P], F32R), sb("hl", [P, KT, P], F32R)
        pg, pu, pd, pT = banks("pg", 2), banks("pu", 2), banks("pd", 2), banks("pT", 2)
        raw_in = [sem(f"raw_in{i}") for i in range(RAW)]
        x_in, x_t, x_hi, x_lo = sem("x_in"), sem("x_transposed"), sem("x_hi"), sem("x_lo")
        hi, lo, used = sem("w_hi"), sem("w_lo"), sem("chunk_used")
        sg_ok, h_ok, h_t, h_hi, h_lo = sem("silu_ready"), sem("h_ready"), sem("h_transposed"), sem("h_hi"), sem("h_lo")
        y_read, y_out, d_set = sem("y_read"), sem("y_out"), sem("y_first")
        weights = expert_weights(a, layer)
        xs = scr["xs"].rearrange("(b p) d -> b p d", p=P)
        ys = scr["ys"].rearrange("(b p) d -> b p d", p=P)

        def turns(eng, body, bound, first=0):
            with eng.Fori(first, NBLK) as b:
                with eng.If(b < bound):
                    body(b)
                with eng.Else():
                    eng.nop()
            eng.nop()

        def place(i):
            return AHEAD + i

        with nc.Block() as block:

            @block.sync
            def _(sp):
                bound = sp.value_load(table[0:1, NBLK + 1:NBLK + 2], min_val=NE, max_val=NBLK)

                def load(b, i, experts):
                    which, k, nxt = ORDER[i]
                    if k > 0:
                        first_next = i + 1 < NCH and ORDER[i + 1][1] == 0
                        sp.wait_ge(lo, b * NCH + place(i) + (2 if first_next else 1))
                    slot = place(i) % RAW
                    sp.dma_start(raw[:, slot], weights[which][bass.ds(experts[nxt], 1), :, k, :]
                                 .rearrange("o p n -> (o p) n")).then_inc(raw_in[slot], 16)

                for i in range(RAW - AHEAD, NCH):
                    load(0, i, (0, 1))

                def body(b):
                    experts = [sp.value_load(table[0:1, bass.ds(b + n, 1)], min_val=0, max_val=NE - 1)
                               for n in range(2)]
                    for i in range(NCH):
                        load(b, i, experts)

                turns(sp, body, bound, 1)

            @block.tensor
            def _(pe):
                pe.nop().then_inc(used, RING)
                bound = pe.value_load(table[0:1, NBLK + 1:NBLK + 2], min_val=NE, max_val=NBLK)

                def transpose_x(half):
                    for k in range(4):
                        last = pe.transpose(pT[half][:, k * P:(k + 1) * P],
                                            xb[:, (4 * half + k) * P:(4 * half + k + 1) * P], ident[:])
                    last.then_inc(x_t, 1)

                def multiply(b, c, out, lhs, k):
                    pe.wait_ge(lo, b * NCH + RAW + c + 1)
                    for half in range(2):
                        cols = slice(half * H, (half + 1) * H)
                        last = three(pe, out[half][:, :], lhs, (wh[:, c % RING, cols], wl[:, c % RING, cols]),
                                     k == 0, k == KT - 1)
                    last.then_inc(used, 1)

                pe.wait_ge(x_in, 16)
                for half in range(2):
                    pe.matmul(pd[half][:, :], ident[:], xb[:, half * H:(half + 1) * H], start=True, stop=True
                              ).then_inc(d_set, 1)
                transpose_x(0)
                transpose_x(1)
                pe.wait_ge(x_lo, 1)
                for k in range(AHEAD):
                    multiply(0, k, pg, (xh[:, k], xl[:, k]), k)

                def body(b):
                    for i, (which, k, nxt) in enumerate(ORDER):
                        if (which, k) == (GATE, 4):
                            pe.wait_ge(x_lo, b * 2 + 2)
                        if (which, k, nxt) == (GATE, 0, 1):
                            pe.wait_ge(x_lo, b * 2 + 3)
                            pe.wait_ge(sg_ok, b * 2 + 2)
                        if (which, k) == (DOWN, 0):
                            pe.wait_ge(y_read, b * 2 + 2)
                        if which == DOWN and k % 4 == 0:
                            pe.wait_ge(h_lo, b * 2 + k // 4 + 1)
                        lhs = (hh[:, k], hl[:, k]) if which == DOWN else (xh[:, k], xl[:, k])
                        multiply(b, place(i), (pg, pu, pd)[which], lhs, k)
                        if i == GATE_END:
                            pe.wait_ge(x_in, b * 16 + 32)
                            transpose_x(0)
                        if (which, k, nxt) == (GATE, AHEAD - 2, 1):
                            for half in range(2):
                                pe.wait_ge(h_ok, b * 2 + half + 1)
                                for kk in range(4):
                                    last = pe.transpose(pT[half][:, kk * P:(kk + 1) * P],
                                                        hs[:, (4 * half + kk) * P:(4 * half + kk + 1) * P], ident[:])
                                last.then_inc(h_t, 1)
                        if (which, k) == (DOWN, 4):
                            transpose_x(1)

                turns(pe, body, bound)
                for half in range(2):
                    pe.matmul(pg[half][:, :], xh[:, 0], wh[:, 0, half * H:(half + 1) * H], start=False, stop=True)

            @block.scalar
            def _(act):
                bound = act.value_load(table[0:1, NBLK + 1:NBLK + 2], min_val=NE, max_val=NBLK)
                for s in raw_in:
                    act.nop().then_inc(s, 16)
                act.nop().then_inc(y_out, 1)
                act.dma_start(xb[:], xs[0]).then_inc(x_in, 16)

                def split_hi(b, c):
                    act.wait_ge(raw_in[c % RAW], b * (16 * NCH // RAW) + 16 * (c // RAW + 1))
                    act.wait_ge(used, b * NCH + c + 1)
                    act.activation(wh[:, c % RING], raw[:, c % RAW], ACT.Copy).then_inc(hi, 1)

                def x_hi_part(n, half):
                    act.wait_ge(x_t, n)
                    act.activation(xh[:, 4 * half:4 * half + 4].rearrange("p k c -> p (k c)"), pT[half][:, :],
                                   ACT.Copy).then_inc(x_hi, 1)

                for half in range(2):
                    x_hi_part(half + 1, half)
                act.dma_start(xb[:], xs[1]).then_inc(x_in, 16)
                for c in range(AHEAD):
                    split_hi(0, c)
                act.wait_ge(d_set, 2)

                def store(b):
                    act.wait_ge(used, b * NCH + RING + AHEAD)
                    act.wait_ge(y_out, b * 16 + 1)
                    for half in range(2):
                        act.activation(yb[:, half * H:(half + 1) * H], pd[half][:, :], ACT.Copy).then_inc(y_read, 1)
                    act.wait_ge(y_read, b * 2 + 2)
                    act.dma_start(ys[bass.ds(b, 1)].rearrange("o p d -> (o p) d"), yb[:]).then_inc(y_out, 16)

                def body(b):
                    for i in range(NCH):
                        split_hi(b, place(i))
                        if i == 3:
                            store(b)
                        if i == GATE_END + 4:
                            act.wait_ge(used, b * NCH + RING + place(GATE_END) + 1)
                            for half in range(2):
                                act.activation(sg[:, half * H:(half + 1) * H], pg[half][:, :], ACT.Silu).then_inc(sg_ok, 1)
                        if i == UP_MID + 3:
                            act.wait_ge(used, b * NCH + RING + place(UP_MID) + 1)
                            x_hi_part(b * 2 + 3, 0)
                        if i == at[DOWN, 0, 0]:
                            for half in range(2):
                                act.wait_ge(h_t, b * 2 + half + 1)
                                act.activation(hh[:, 4 * half:4 * half + 4].rearrange("p k c -> p (k c)"), pT[half][:, :],
                                               ACT.Copy).then_inc(h_hi, 1)
                    x_hi_part(b * 2 + 4, 1)
                    act.dma_start(xb[:], xs[bass.ds(b + 2, 1)].rearrange("o p d -> (o p) d")).then_inc(x_in, 16)

                turns(act, body, bound)
                store(bound)
                act.wait_ge(y_out, bound * 16 + 17)
                act.activation(yb[0:1, 0:1], sg[0:1, 0:1], ACT.Copy)
                act.wait_ge(x_in, bound * 16 + 32)
                act.activation(yb[0:1, 1:2], sg[0:1, 0:1], ACT.Copy)

            @block.vector
            def _(dve):
                dve.nop().then_inc(lo, RAW)
                bound = dve.value_load(table[0:1, NBLK + 1:NBLK + 2], min_val=NE, max_val=NBLK)

                def split_lo(b, c):
                    dve.wait_ge(hi, b * NCH + c + 1)
                    dve.tensor_tensor(wl[:, c % RING], raw[:, c % RAW], f(wh[:, c % RING]), ALU.subtract
                                      ).then_inc(lo, 1)

                def x_lo_part(n, half):
                    dve.wait_ge(x_hi, n)
                    part = xh[:, 4 * half:4 * half + 4].rearrange("p k c -> p (k c)")
                    dve.tensor_tensor(xl[:, 4 * half:4 * half + 4].rearrange("p k c -> p (k c)"), pT[half][:, :],
                                      f(part), ALU.subtract).then_inc(x_lo, 1)

                for half in range(2):
                    x_lo_part(half + 1, half)
                for c in range(AHEAD):
                    split_lo(0, c)

                def body(b):
                    for i in range(NCH):
                        split_lo(b, place(i))
                        if i == UP_MID + 3:
                            x_lo_part(b * 2 + 3, 0)
                        if i == UP_END + AHEAD:
                            dve.wait_ge(used, b * NCH + RING + place(UP_END) + 1)
                            for half in range(2):
                                cols = slice(half * H, (half + 1) * H)
                                dve.wait_ge(sg_ok, b * 2 + half + 1)
                                dve.tensor_tensor(hs[:, cols], pu[half][:, :], sg[:, cols], ALU.mult).then_inc(h_ok, 1)
                        if i == at[DOWN, 0, 0]:
                            for half in range(2):
                                dve.wait_ge(h_hi, b * 2 + half + 1)
                                part = hh[:, 4 * half:4 * half + 4].rearrange("p k c -> p (k c)")
                                dve.tensor_tensor(hl[:, 4 * half:4 * half + 4].rearrange("p k c -> p (k c)"),
                                                  pT[half][:, :], f(part), ALU.subtract).then_inc(h_lo, 1)
                    x_lo_part(b * 2 + 4, 1)

                turns(dve, body, bound)


def phase_combine(nc, a, scr, layer, res, dest, wk, minus_half, then):
    with ExitStack() as ctx:
        sb, sem, banks = alloc(nc, ctx, f"combine{layer}")
        yg = sb("yg", [P, 2, NX, D])
        gate, nm, junk = sb("gate", [P, D]), sb("nm", [P, D]), sb("junk", [P, 2, D])
        md = sb("md", [P, 2, D])
        ss, rs = sb("ss", [P, NX]), sb("rs", [P, NX])
        got = [[sem(f"y{s}_{t}") for t in range(NX)] for s in range(2)]
        c_in, sq, ms, rs_ok, dv, res_ok = (sem(n) for n in ("consts_in", "squares", "ms", "rs_ready", "dve_steps", "res_ready"))
        y0_ok = sem("y0_weighted")
        h_f32, h_hi, outs, normed = sem("h_f32"), sem("h_hi"), sem("outs"), sem("normed")
        norm_row, mod_layer, hh, hl = then
        with nc.Block() as block:

            @block.gpsimd
            def _(pool):
                for t in range(NX):
                    for s in range(2):
                        pool.indirect_dma_start(
                            out=yg[:, s, t], out_offset=None, in_=scr["ys"],
                            in_offset=bass.IndirectOffsetOnAxis(ap=dest[:, 1, s, t:t + 1].bitcast(U32), axis=0),
                            bounds_check=(NBLK + 1) * P - 1, oob_is_err=False).then_inc(got[s][t], 16)
                for t in range(NX):
                    pool.wait_ge(ms, t + 1)
                    pool.tensor_tensor(rs[:, t:t + 1], ss[:, t:t + 1], minus_half[:, 0:1], ALU.pow).then_inc(rs_ok, 1)

            @block.sync
            def _(sp):
                sp.dma_start(gate[:], scr["mod"][layer, 0:1, 5 * D:6 * D].to_broadcast([P, D])).then_inc(c_in, 16)
                sp.dma_start(nm[:], norm_row.to_broadcast([P, D])).then_inc(c_in, 16)
                if mod_layer is not None:
                    for v in range(2):
                        sp.dma_start(md[:, v], scr["mod"][mod_layer, 0:1, v * D:(v + 1) * D].to_broadcast([P, D])
                                     ).then_inc(c_in, 16)
                else:
                    for t in range(NX):
                        sp.wait_ge(normed, t + 1)
                        sp.dma_start(a["out"][0, t * P:(t + 1) * P, :], yg[:, 0, t]).then_inc(outs, 16)
                    sp.wait_ge(outs, 16 * NX)

            @block.scalar
            def _(act):
                for t in range(NX):
                    act.wait_ge(got[0][t], 16)
                    act.activation(yg[:, 0, t], yg[:, 0, t], ACT.Copy, scale=wk[:, t, 0:1]).then_inc(y0_ok, 1)
                for t in range(NX):
                    act.wait_ge(res_ok, t + 1)
                    if t >= 2:
                        act.wait_ge(sq, t - 1)
                    act.activation(junk[:, t % 2], res[:, t], ACT.Square, accum_out=ss[:, t:t + 1]).then_inc(sq, 1)
                if mod_layer is not None:
                    for t in range(NX):
                        act.wait_ge(h_f32, t + 1)
                        act.activation(hh[:, t], yg[:, 0, t], ACT.Copy).then_inc(h_hi, 1)

            @block.vector
            def _(dve):
                own = Count(dv)

                def step(ins):
                    own.inc(ins)
                    own.after(dve)

                dve.wait_ge(c_in, 16 * (4 if mod_layer is not None else 2))
                if mod_layer is not None:
                    step(dve.scalar_tensor_tensor(md[:, 1], md[:, 1], 1.0, nm[:], ALU.add, ALU.mult))
                for t in range(NX):
                    dve.wait_ge(got[1][t], 16)
                    dve.wait_ge(y0_ok, t + 1)
                    step(dve.scalar_tensor_tensor(yg[:, 0, t], yg[:, 1, t], wk[:, t, 1:2], yg[:, 0, t],
                                                  ALU.mult, ALU.add))
                    step(dve.tensor_tensor(yg[:, 0, t], yg[:, 0, t], gate[:], ALU.mult))
                    dve.tensor_tensor(res[:, t], res[:, t], yg[:, 0, t], ALU.add).then_inc(res_ok, 1)
                for t in range(NX):
                    dve.wait_ge(sq, t + 1)
                    dve.tensor_scalar(ss[:, t:t + 1], ss[:, t:t + 1], 1.0 / D, EPS, ALU.mult, ALU.add).then_inc(ms, 1)

                def low(t):
                    dve.wait_ge(h_hi, t + 1)
                    dve.tensor_tensor(hl[:, t], yg[:, 0, t], f(hh[:, t]), ALU.subtract)

                scale = md[:, 1] if mod_layer is not None else nm[:]
                for t in range(NX):
                    dve.wait_ge(rs_ok, t + 1)
                    dve.scalar_tensor_tensor(yg[:, 0, t], res[:, t], rs[:, t:t + 1], scale, ALU.mult, ALU.mult
                                             ).then_inc(normed, 1)
                    if mod_layer is not None:
                        dve.wait_ge(normed, t + 1)
                        dve.tensor_tensor(yg[:, 0, t], yg[:, 0, t], md[:, 0], ALU.add).then_inc(h_f32, 1)
                        if t:
                            low(t - 1)
                if mod_layer is not None:
                    low(NX - 1)


def phase_fourier(nc, a, hh, hl, fh, fl):
    with ExitStack() as ctx:
        sb, sem, banks = alloc(nc, ctx, "fourier")
        raw = sb("raw", [P, 2, NX, SEQ])
        ch, cl = sb("ch", [P, 2, NX, SEQ], F32R), sb("cl", [P, 2, NX, SEQ], F32R)
        gr = sb("gr", [P, 2, 2, FG])
        gh, gl = sb("gh", [P, 2, 2, FG], F32R), sb("gl", [P, 2, 2, FG], F32R)
        uh, ul = sb("uh", [P, 2, 2, SEQ], F32R), sb("ul", [P, 2, 2, SEQ], F32R)
        pU, pF = banks("pU", 4), banks("pF", 4)
        c_in = [sem("cos_in"), sem("sin_in"), sem("chan_in")]
        hi, lo, u_done, u_hi, u_lo = sem("table_hi"), sem("table_lo"), sem("u_done"), sem("u_hi"), sem("u_lo")
        f_done, f_hi, f_lo = sem("f_done"), sem("f_hi"), sem("f_lo")
        tables = [(raw[:, 0], ch[:, 0], cl[:, 0]), (raw[:, 1], ch[:, 1], cl[:, 1]), (gr[:], gh[:], gl[:])]
        NGR = D // FG
        with nc.Block() as block:

            @block.sync
            def _(sp):
                for s in range(2):
                    sp.dma_start(raw[:, s], a["dft_seq"][s].rearrange("(t p) n -> p t n", p=P)).then_inc(c_in[s], 16)
                sp.dma_start(gr[:], a["dft_chan"].rearrange("s (k p) n -> p s k n", p=P)).then_inc(c_in[2], 16)

            @block.tensor
            def _(pe):
                def sequence(g):
                    for d in range(2):
                        col = (g * 2 + d) * P
                        for s in range(2):
                            n = g * 4 + d * 2 + s
                            pe.wait_ge(lo, s + 1)
                            if g:
                                pe.wait_ge(u_lo, n - 3)
                            for t in range(NX):
                                last = three(pe, pU[d * 2 + s][:, :], (hh[:, t, col:col + P], hl[:, t, col:col + P]),
                                             (ch[:, s, t], cl[:, s, t]), t == 0, t == NX - 1)
                            last.then_inc(u_done, 1)

                def channels(g):
                    pe.wait_ge(lo, 3)
                    pe.wait_ge(u_lo, g * 4 + 4)
                    for e in range(2):
                        n = g * 2 + e
                        if n >= 4:
                            pe.wait_ge(f_lo, n - 3)
                        for d in range(2):
                            for s in range(2):
                                last = three(pe, pF[n % 4][:, :],
                                             tuple(m[:, s, d, e * P:(e + 1) * P] for m in (gh, gl)),
                                             (uh[:, d, s], ul[:, d, s]), d + s == 0, d + s == 2)
                        last.then_inc(f_done, 1)

                for g in range(NGR):
                    sequence(g)
                    channels(g)

            @block.scalar
            def _(act):
                for i, (r, h_, l_) in enumerate(tables):
                    act.wait_ge(c_in[i], 16)
                    act.activation(h_, r, ACT.Copy).then_inc(hi, 1)
                for g in range(NGR):
                    for n in range(4):
                        act.wait_ge(u_done, g * 4 + n + 1)
                        if g:
                            act.wait_ge(f_done, g * 2)
                        act.activation(uh[:, n // 2, n % 2], pU[n][:, :], ACT.Copy).then_inc(u_hi, 1)
                    for n in range(g * 2, g * 2 + 2):
                        act.wait_ge(f_done, n + 1)
                        act.activation(fh[:, n], pF[n % 4][:, :], ACT.Copy).then_inc(f_hi, 1)

            @block.vector
            def _(dve):
                for i, (r, h_, l_) in enumerate(tables):
                    dve.wait_ge(hi, i + 1)
                    dve.tensor_tensor(l_, r, f(h_), ALU.subtract).then_inc(lo, 1)
                for g in range(NGR):
                    for n in range(4):
                        dve.wait_ge(u_hi, g * 4 + n + 1)
                        dve.tensor_tensor(ul[:, n // 2, n % 2], pU[n][:, :], f(uh[:, n // 2, n % 2]), ALU.subtract
                                          ).then_inc(u_lo, 1)
                    for n in range(g * 2, g * 2 + 2):
                        dve.wait_ge(f_hi, n + 1)
                        dve.tensor_tensor(fl[:, n], pF[n % 4][:, :], f(fh[:, n]), ALU.subtract).then_inc(f_lo, 1)


def build(nc, a):
    def dram(name, shape):
        return nc.dram_tensor(name, shape, F32, kind="Internal").ap()

    scr = {"mod": dram("mod_scr", (2, 1, NMOD * D)), "strips": dram("strips_scr", (HEADS, P, STRIPS)),
           "gated": dram("gated_scr", (SEQ, HEADS * DV)),
           "xs": dram("xs_scr", ((NBLK + 2) * P, D)), "ys": dram("ys_scr", ((NBLK + 1) * P, D))}
    with ExitStack() as ctx:
        def keep(name, shape, dt=F32):
            return ctx.enter_context(nc.sbuf_tensor(name, shape, dt))

        ident, minus_half = keep("ident", [P, P]), keep("minus_half", [P, 8])
        cT = keep("cT", [P, 2 * KT])
        with nc.sbuf_tensor("hTh", [P, KT, NTOK * P], F32R) as hTh, nc.sbuf_tensor("hTl", [P, KT, NTOK * P], F32R) as hTl:
            with nc.sbuf_tensor("head_raw", [P, 4, 2, H], F32) as raw:
                phase_first(nc, a, scr, ident, minus_half, cT, hTh, hTl, raw)
                phase_heads(nc, a, scr, ident, minus_half, cT, hTh, hTl, raw)
        res = keep("res", [P, NX, D])
        dest, wk = keep("dest", [P, 2, 2, NX], I32), keep("wk", [P, NX, 2])
        sc = keep("scores", [P, NX, NE])
        table = keep("table", [P, NBLK + 2], I32)
        KO = HEADS * DV // P
        with nc.sbuf_tensor("rows", [P, NX, HEADS * DV], F32) as rows:
            tok = rows[:, :, 0:D]
            with nc.sbuf_tensor("gTh", [P, KO, SEQ], F32R) as gTh, nc.sbuf_tensor("gTl", [P, KO, SEQ], F32R) as gTl:
                project_residual(nc, a, scr, "out0", 0, KO, a["ret_w_out"][0].rearrange("(k p) n -> p k n", p=P),
                                 (gTh, gTl), a["x"][0], res, tok, sc, ident, minus_half, rows)
            with nc.sbuf_tensor("raw0", [P, RAW, D], F32) as raw:
                phase_route(nc, a, scr, 0, tok, sc, dest, wk, table, raw)
                phase_experts(nc, a, scr, ident, 0, table, raw)
        with nc.sbuf_tensor("tok", [P, NX, D], F32) as tok:
            with nc.sbuf_tensor("fh", [P, KT, SEQ], F32R) as fh, nc.sbuf_tensor("fl", [P, KT, SEQ], F32R) as fl:
                with nc.sbuf_tensor("h2h", [P, NX, D], F32R) as h2h, nc.sbuf_tensor("h2l", [P, NX, D], F32R) as h2l:
                    phase_combine(nc, a, scr, 0, res, dest, wk, minus_half, (a["norm_mix"][1:2, :], 1, h2h, h2l))
                    phase_fourier(nc, a, h2h, h2l, fh, fl)
                project_residual(nc, a, scr, "out1", 1, KT, a["fn_w_out"][0].rearrange("(k p) n -> p k n", p=P),
                                 (fh, fl), None, res, tok, sc, ident, minus_half)
            with nc.sbuf_tensor("raw1", [P, RAW, D], F32) as raw:
                phase_route(nc, a, scr, 1, tok, sc, dest, wk, table, raw)
                phase_experts(nc, a, scr, ident, 1, table, raw)
        phase_combine(nc, a, scr, 1, res, dest, wk, minus_half,
                      (a["norm_final"].rearrange("(o d) -> o d", o=1), None, None, None))


_INS = ["x", "c", "ctx", "c_ctx", "w_mod", "b_mod", "norm_mix", "norm_ffn", "norm_final", "ret_w_in", "ret_decay",
        "ret_gn", "ret_w_out", "fn_w_out", "router_w", "router_bias", "moe_w_gate", "moe_w_up", "moe_w_down"]


def shape_constants():
    import numpy as np
    p = np.arange(P, dtype=np.float64)[:, None]
    delta = np.arange(XR)[None, :] - XO - p
    w = np.arange(CR)[None, :]
    ahead, behind = w - P + CTX - p, SEQ - (w - P) + p
    distances = np.concatenate([np.maximum(delta, 0), np.maximum(-delta, 0), ahead, behind], 1)
    nf = DK // 4
    inv = (np.float32(10000.0) ** (-np.arange(nf, dtype=np.float32) / np.float32(nf))).astype(np.float32)
    t = np.arange(SEQ)
    ang = np.stack([(t // 64).astype(np.float32)[:, None] * inv, (t % 64).astype(np.float32)[:, None] * inv], 1)
    rope = np.stack([np.cos(ang), np.sin(ang)], 1)
    rope = rope.reshape(NX, P, 2 * 2 * nf).transpose(1, 0, 2)
    a = 2 * np.pi * (np.outer(np.arange(SEQ), np.arange(SEQ)) % SEQ) / SEQ
    g = 2 * np.pi * (np.outer(np.arange(FG), np.arange(FG)) % FG) / FG
    return {
        "identity": np.eye(P), "distances": distances, "rope": rope,
        "dft_seq": np.stack([np.cos(a), np.sin(a)]) / np.sqrt(SEQ),
        "dft_chan": np.stack([np.cos(g), -np.sin(g)]) / np.sqrt(FG),
        "below": np.stack([np.tril(np.ones((P, P)), -1).T, np.ones((P, P))]),
        "order": np.concatenate([NE - np.arange(NE), NG - np.arange(NG), np.arange(MAX_OVER + 1)])[None],
    }


def kernel(**inputs):
    import numpy as _np
    import concourse.bacc as _bacc
    from concourse import mybir as _mybir
    from concourse.bass_utils import run_bass_kernel_spmd as _run

    nc = _bacc.Bacc("TRN2", target_bir_lowering=False, num_devices=1)
    arrays, args = {}, {}
    given = {name: _np.ascontiguousarray(inputs[name]) for name in _INS}
    given.update({k: _np.ascontiguousarray(v, dtype=_np.float32) for k, v in shape_constants().items()})
    for name, arr in given.items():
        arrays[f"in_{name}_dram"] = arr
        args[name] = nc.dram_tensor(f"in_{name}_dram", arr.shape, _mybir.dt.from_np(arr.dtype),
                                    kind="ExternalInput").ap()
    args["out"] = nc.dram_tensor("out_0_dram", (1, SEQ, D), _mybir.dt.float32, kind="ExternalOutput").ap()
    build(nc, args)
    r = _run(nc, [arrays], core_ids=[0])
    return r.results[0]["out_0_dram"]
```
